# Optimizing a Trainium2 kernel written in Bass

```python
import math
import jax
import jax.numpy as jnp
from jax import lax
import numpy as np

D_MODEL = 1024
BATCH = 1
SEQ = 256
DEPTH = 2

GRID_W = 64
CTX_LEN = 256
EPS = 1e-6
N_MOD = 6

H_A = 4
DK = 64
DV = 2 * DK
QK_W = H_A * 2 * DK
W_A = H_A * DV
ROT_AX = DK // 2
ROPE_BASE = 10000.0
Q_BLOCK = 128

W_B = 512
G_B = 4
CHUNK_B = 128

H_C = 4
DH_C = 128
W_C = H_C * DH_C
CONV_K = 3
MLSTM_CHUNK = 128

N_BRANCH = 3
W_BR = 512

A_K0 = 0
A_V0 = A_K0 + QK_W
C_X0 = A_V0 + W_A
MEM_COLS = C_X0 + W_C
A_Q0 = MEM_COLS
B_UV0 = A_Q0 + QK_W
C_Z0 = B_UV0 + 2 * W_B
GATE0 = C_Z0 + W_C
IN_COLS = GATE0 + N_BRANCH * D_MODEL

N_GROUPS = 4
EXP_PER_GROUP = 8
N_EXPERTS = N_GROUPS * EXP_PER_GROUP
TOP_K = 2
D_EXPERT = 512
MOE_BLOCK = 128

kernel_name = 'hybrid_prefix_diffattn_gmlp_mlstm_hmoe'

def rmsnorm(x, g):
    xf = x.astype(jnp.float32)
    y = xf * lax.rsqrt(jnp.mean(xf * xf, axis=-1, keepdims=True) + EPS)
    return y.astype(x.dtype) * g

def modulate(h, shift, scale):
    return h * (1 + scale) + shift

def axial_angles(n_tokens):
    rows = n_tokens // GRID_W
    row = jnp.broadcast_to(jnp.arange(rows)[:, None], (rows, GRID_W)).reshape(-1).astype(jnp.float32)
    col = jnp.broadcast_to(jnp.arange(GRID_W)[None, :], (rows, GRID_W)).reshape(-1).astype(jnp.float32)
    inv = ROPE_BASE ** (-jnp.arange(0, ROT_AX, 2, dtype=jnp.float32) / ROT_AX)
    return row[:, None] * inv, col[:, None] * inv

def rope_rotate(x, ang):
    cos = jnp.cos(ang)[:, None, None, :].astype(x.dtype)
    sin = jnp.sin(ang)[:, None, None, :].astype(x.dtype)
    x1, x2 = jnp.split(x, 2, axis=-1)
    return jnp.concatenate([x1 * cos - x2 * sin, x1 * sin + x2 * cos], axis=-1)

def apply_axial_rope(x, ang_r, ang_c):
    return jnp.concatenate([rope_rotate(x[..., :ROT_AX], ang_r), rope_rotate(x[..., ROT_AX:], ang_c)], axis=-1)

def diff_lambda_value(lp, layer_idx):
    lam_init = 0.8 - 0.6 * math.exp(-0.3 * layer_idx)
    lpf = lp.astype(jnp.float32)
    lam = jnp.exp(jnp.sum(lpf[0] * lpf[1])) - jnp.exp(jnp.sum(lpf[2] * lpf[3])) + lam_init
    return lam, lam_init

def diff_attention(q, k, v, lam):
    s = jnp.einsum('bqhmd,bkhmd->bhmqk', q.astype(jnp.float32), k.astype(jnp.float32)) * (DK ** -0.5)
    p = jax.nn.softmax(s, axis=-1)
    a = p[:, :, 0] - lam * p[:, :, 1]
    return jnp.einsum('bhqk,bkhd->bqhd', a, v.astype(jnp.float32)).astype(v.dtype)

def blocked_diff_attention(q, k, v, lam):
    b, t = q.shape[:2]
    nb = t // Q_BLOCK
    qb = jnp.moveaxis(q.reshape(b, nb, Q_BLOCK, *q.shape[2:]), 1, 0)
    o = lax.map(lambda blk: diff_attention(blk, k, v, lam), qb)
    return jnp.moveaxis(o, 0, 1).reshape(b, t, *o.shape[3:])

def diff_heads_out(o, g, lam_init):
    b, t = o.shape[:2]
    return (rmsnorm(o, g) * (1.0 - lam_init)).reshape(b, t, W_A)

def chunk_spatial_gate(uv, g_v, w_s, b_s):
    b, t, _ = uv.shape
    u, v = jnp.split(uv, 2, axis=-1)
    v = rmsnorm(v, g_v).reshape(b, t // CHUNK_B, CHUNK_B, G_B, W_B // G_B)
    mixed = jnp.einsum('gts,bcsgd->bctgd', w_s, v) + jnp.swapaxes(b_s, 0, 1)[:, :, None]
    return u * mixed.reshape(b, t, W_B)

def depthwise_conv(x, w, b):
    out = lax.conv_general_dilated(x, w[:, None, :], window_strides=(1,),
                                   padding=[(CONV_K // 2, CONV_K // 2)],
                                   dimension_numbers=('NWC', 'WIO', 'NWC'),
                                   feature_group_count=x.shape[-1])
    return out + b

def mlstm_features(xm, w_conv, b_conv, w_qkv, w_if, b_if):
    b, t, _ = xm.shape
    xconv = jax.nn.silu(depthwise_conv(xm, w_conv, b_conv))
    heads = lambda a: a.reshape(b, t, H_C, DH_C)
    q = jnp.einsum('bthd,hde->bthe', heads(xconv), w_qkv[0])
    k = jnp.einsum('bthd,hde->bthe', heads(xconv), w_qkv[1])
    v = jnp.einsum('bthd,hde->bthe', heads(xm), w_qkv[2])
    qkv = jnp.concatenate([q.reshape(b, t, W_C), k.reshape(b, t, W_C), v.reshape(b, t, W_C)], axis=-1)
    gates = (qkv @ w_if + b_if).reshape(b, t, 4, H_C)
    return xconv, q, k * (DH_C ** -0.5), v, gates

def mlstm_zero_state(b):
    return (jnp.zeros((b, H_C, DH_C, DH_C), jnp.float32),
            jnp.zeros((b, H_C, DH_C), jnp.float32),
            jnp.zeros((b, H_C), jnp.float32))

def mlstm_scan(q, k, v, i_pre, f_pre, state, with_h):
    b, t, h, dh = q.shape
    nc = t // MLSTM_CHUNK
    f32 = jnp.float32

    def chunks(a):
        a = a.astype(f32).reshape(b, nc, MLSTM_CHUNK, *a.shape[2:])
        return jnp.moveaxis(a, 3, 1)

    qc, kc, vc = chunks(q), chunks(k), chunks(v)
    ig = chunks(i_pre)
    bcum = jnp.cumsum(jax.nn.log_sigmoid(chunks(f_pre)), axis=-1)
    g = bcum[..., -1]
    a_end = g[..., None] - bcum + ig
    m_loc = jnp.max(a_end, axis=-1)
    w_end = jnp.exp(a_end - m_loc[..., None])
    c_loc = jnp.einsum('bhcs,bhcsd,bhcse->bhcde', w_end, vc, kc)
    n_loc = jnp.einsum('bhcs,bhcse->bhce', w_end, kc)

    def step(carry, xs):
        c_st, n_st, m_st = carry
        c_l, n_l, m_l, g_c = xs
        m_new = jnp.maximum(g_c + m_st, m_l)
        a_old = jnp.exp(g_c + m_st - m_new)
        a_new = jnp.exp(m_l - m_new)
        c_new = a_old[..., None, None] * c_st + a_new[..., None, None] * c_l
        n_new = a_old[..., None] * n_st + a_new[..., None] * n_l
        return (c_new, n_new, m_new), carry

    xs = tuple(jnp.moveaxis(a, 2, 0) for a in (c_loc, n_loc, m_loc, g))
    init = tuple(s.astype(f32) for s in state)
    final, starts = lax.scan(step, init, xs)
    if not with_h:
        return final
    c0, n0, m0 = (jnp.moveaxis(s, 0, 2) for s in starts)
    ln = MLSTM_CHUNK
    causal = jnp.tril(jnp.ones((ln, ln), dtype=bool))
    log_d = jnp.where(causal, bcum[..., :, None] - bcum[..., None, :] + ig[..., None, :], -jnp.inf)
    log_inter = bcum + m0[..., None]
    m_t = jnp.maximum(log_inter, jnp.max(log_d, axis=-1))
    s = jnp.einsum('bhctd,bhcsd->bhcts', qc, kc) * jnp.exp(log_d - m_t[..., None])
    w_inter = jnp.exp(log_inter - m_t)
    num = (jnp.einsum('bhcts,bhcsd->bhctd', s, vc)
           + w_inter[..., None] * jnp.einsum('bhcde,bhcte->bhctd', c0, qc))
    den = jnp.sum(s, axis=-1) + w_inter * jnp.einsum('bhce,bhcte->bhct', n0, qc)
    hh = num / jnp.maximum(jnp.abs(den), jnp.exp(-m_t))[..., None]
    hh = jnp.moveaxis(hh, 1, 3).reshape(b, t, h, dh)
    return hh.astype(q.dtype), final

def mlstm_bidir(q, k, v, gates, init_f, init_b, with_h):
    rev = lambda a: jnp.flip(a, axis=1)
    out_f = mlstm_scan(q, k, v, gates[:, :, 0], gates[:, :, 1], init_f, with_h)
    out_b = mlstm_scan(rev(q), rev(k), rev(v), rev(gates[:, :, 2]), rev(gates[:, :, 3]), init_b, with_h)
    if not with_h:
        return None, out_f, out_b
    h_f, st_f = out_f
    h_b, st_b = out_b
    return h_f + rev(h_b), st_f, st_b

def mlstm_out(h_sum, xconv, z, g, skip):
    b, t = h_sum.shape[:2]
    hn = rmsnorm(h_sum, g.reshape(H_C, DH_C)).reshape(b, t, W_C)
    return (hn + skip * xconv) * jax.nn.sigmoid(z)

def merge_branches(ys, gate_pre, w_br, w_o):
    g = jax.nn.sigmoid(gate_pre.reshape(*gate_pre.shape[:-1], N_BRANCH, D_MODEL))
    merged = (g[..., 0, :] * (ys[0] @ w_br[0]) + g[..., 1, :] * (ys[1] @ w_br[1])
              + g[..., 2, :] * (ys[2] @ w_br[2]))
    return merged @ w_o

def hier_route(h, w_rg, b_rg, w_re, b_re):
    f32 = jnp.float32
    hf = h.astype(f32)
    p_group = jax.nn.softmax(hf @ w_rg.astype(f32) + b_rg.astype(f32), axis=-1)
    g_star = jnp.argmax(p_group, axis=-1)
    logit_e = (hf @ w_re.astype(f32) + b_re.astype(f32)).reshape(-1, N_GROUPS, EXP_PER_GROUP)
    logit_sel = jnp.take_along_axis(logit_e, g_star[:, None, None], axis=1)[:, 0]
    top_v, top_i = lax.top_k(logit_sel, TOP_K)
    p_g = jnp.take_along_axis(p_group, g_star[:, None], axis=1)
    wt = jax.nn.softmax(top_v, axis=-1) * p_g
    eid = (g_star[:, None] * EXP_PER_GROUP + top_i).astype(jnp.int32)
    return eid, wt.astype(h.dtype)

def moe_experts(h, eid, wt, w_gate, w_up, w_down):
    n, d = h.shape
    a = n * TOP_K
    n_blocks = -(-(a + N_EXPERTS * (MOE_BLOCK - 1)) // MOE_BLOCK)
    slots = n_blocks * MOE_BLOCK
    flat_e = eid.reshape(a)
    flat_tok = jnp.repeat(jnp.arange(n, dtype=jnp.int32), TOP_K)
    flat_w = wt.reshape(a)
    order = jnp.argsort(flat_e)
    se, stok, sw = flat_e[order], flat_tok[order], flat_w[order]
    counts = jnp.bincount(flat_e, length=N_EXPERTS)
    start = jnp.cumsum(counts) - counts
    padded = (counts + MOE_BLOCK - 1) // MOE_BLOCK * MOE_BLOCK
    pend = jnp.cumsum(padded)
    dest = (pend - padded)[se] + jnp.arange(a) - start[se]
    buf_tok = jnp.full((slots,), n, jnp.int32).at[dest].set(stok)
    buf_w = jnp.zeros((slots,), wt.dtype).at[dest].set(sw)
    block_e = jnp.minimum(jnp.searchsorted(pend, jnp.arange(n_blocks) * MOE_BLOCK, side='right'),
                          N_EXPERTS - 1)
    xb = jnp.concatenate([h, jnp.zeros((1, d), h.dtype)], axis=0)[buf_tok].reshape(n_blocks, MOE_BLOCK, d)

    def run_block(args):
        xblk, e = args
        return (jax.nn.silu(xblk @ w_gate[e]) * (xblk @ w_up[e])) @ w_down[e]

    yb = lax.map(run_block, (xb, block_e)).reshape(slots, d)
    return jax.ops.segment_sum(yb * buf_w[:, None], buf_tok, num_segments=n + 1)[:n]

def setup_inputs(seed: int = 0) -> dict:
    key = jax.random.key(seed)
    ks = list(jax.random.split(key, 40))
    nrm = lambda shape, s: jax.random.normal(ks.pop(), shape, jnp.float32) * s
    D = D_MODEL
    L = DEPTH
    forget_bias = jnp.linspace(3.0, 6.0, H_C)
    b_if = (jnp.zeros((L, 4, H_C), jnp.float32).at[:, 1].set(forget_bias).at[:, 3].set(forget_bias)
            + nrm((L, 4, H_C), 0.1)).reshape(L, 4 * H_C)
    return {
        'x': nrm((BATCH, SEQ, D), 1.0),
        'c': nrm((BATCH, D), 1.0),
        'ctx': nrm((BATCH, CTX_LEN, D), 1.0),
        'c_ctx': nrm((D,), 1.0),
        'w_mod': nrm((L, D, N_MOD * D), 0.5 * D ** -0.5),
        'b_mod': nrm((L, N_MOD * D), 0.02),
        'g_norm1': 1.0 + nrm((L, D), 0.02),
        'g_norm2': 1.0 + nrm((L, D), 0.02),
        'w_in': nrm((L, D, IN_COLS), D ** -0.5),
        'diff_lambda': nrm((L, 4, DK), 0.1),
        'g_diff_subln': 1.0 + nrm((L, DV), 0.02),
        'w_gmlp_s': nrm((L, G_B, CHUNK_B, CHUNK_B), CHUNK_B ** -0.5),
        'b_gmlp_s': 1.0 + nrm((L, G_B, CHUNK_B), 0.02),
        'g_gmlp_v': 1.0 + nrm((L, W_B), 0.02),
        'w_conv_m': nrm((L, CONV_K, W_C), CONV_K ** -0.5),
        'b_conv_m': nrm((L, W_C), 0.02),
        'w_qkv_m': nrm((L, 3, H_C, DH_C, DH_C), DH_C ** -0.5),
        'w_if_m': nrm((L, 3 * W_C, 4 * H_C), (3 * W_C) ** -0.5),
        'b_if_m': b_if,
        'g_mlstm_norm': 1.0 + nrm((L, W_C), 0.02),
        'skip_m': 1.0 + nrm((L, W_C), 0.02),
        'w_branch': nrm((L, N_BRANCH, W_BR, D), W_BR ** -0.5),
        'w_out': nrm((L, D, D), D ** -0.5),
        'w_route_g': nrm((L, D, N_GROUPS), D ** -0.5),
        'b_route_g': nrm((L, N_GROUPS), 0.01),
        'w_route_e': nrm((L, D, N_EXPERTS), D ** -0.5),
        'b_route_e': nrm((L, N_EXPERTS), 0.01),
        'w_e_gate': nrm((L, N_EXPERTS, D, D_EXPERT), D ** -0.5),
        'w_e_up': nrm((L, N_EXPERTS, D, D_EXPERT), D ** -0.5),
        'w_e_down': nrm((L, N_EXPERTS, D_EXPERT, D), D_EXPERT ** -0.5),
        'g_final': 1.0 + nrm((D,), 0.02),
    }

def reference(x, c, ctx, c_ctx, w_mod, b_mod, g_norm1, g_norm2, w_in, diff_lambda, g_diff_subln,
              w_gmlp_s, b_gmlp_s, g_gmlp_v, w_conv_m, b_conv_m, w_qkv_m, w_if_m, b_if_m,
              g_mlstm_norm, skip_m, w_branch, w_out, w_route_g, b_route_g, w_route_e, b_route_e,
              w_e_gate, w_e_up, w_e_down, g_final):
    B, T, D = x.shape
    tc = ctx.shape[1]
    ang_r, ang_c = axial_angles(T)
    xc = ctx
    for l in range(DEPTH):
        last = l == DEPTH - 1
        mod = (jax.nn.silu(c) @ w_mod[l] + b_mod[l]).reshape(B, N_MOD, 1, D)
        mod_c = (jax.nn.silu(c_ctx) @ w_mod[l] + b_mod[l]).reshape(N_MOD, D)

        h = modulate(rmsnorm(x, g_norm1[l]), mod[:, 0], mod[:, 1])
        hc = modulate(rmsnorm(xc, g_norm1[l]), mod_c[0], mod_c[1])
        p = h @ w_in[l]
        pc = hc @ (w_in[l, :, :MEM_COLS] if last else w_in[l])
        lam, lam_init = diff_lambda_value(diff_lambda[l], l)

        q_lat = apply_axial_rope(p[..., A_Q0:A_Q0 + QK_W].reshape(B, T, H_A, 2, DK), ang_r, ang_c)
        k_lat = apply_axial_rope(p[..., A_K0:A_K0 + QK_W].reshape(B, T, H_A, 2, DK), ang_r, ang_c)
        v_lat = p[..., A_V0:A_V0 + W_A].reshape(B, T, H_A, DV)
        k_ctx = pc[..., A_K0:A_K0 + QK_W].reshape(B, tc, H_A, 2, DK)
        v_ctx = pc[..., A_V0:A_V0 + W_A].reshape(B, tc, H_A, DV)
        o_a = blocked_diff_attention(q_lat, jnp.concatenate([k_ctx, k_lat], axis=1),
                                     jnp.concatenate([v_ctx, v_lat], axis=1), lam)
        y_a = diff_heads_out(o_a, g_diff_subln[l], lam_init)

        y_b = chunk_spatial_gate(jax.nn.gelu(p[..., B_UV0:B_UV0 + 2 * W_B]), g_gmlp_v[l], w_gmlp_s[l], b_gmlp_s[l])

        mparams = (w_conv_m[l], b_conv_m[l], w_qkv_m[l], w_if_m[l], b_if_m[l])
        xconv_c, q_c, k_c, v_c, gates_c = mlstm_features(pc[..., C_X0:C_X0 + W_C], *mparams)
        zero = mlstm_zero_state(B)
        h_mc, st_f, st_b = mlstm_bidir(q_c, k_c, v_c, gates_c, zero, zero, not last)
        xconv, q_m, k_m, v_m, gates_m = mlstm_features(p[..., C_X0:C_X0 + W_C], *mparams)
        h_m, _, _ = mlstm_bidir(q_m, k_m, v_m, gates_m, st_f, st_b, True)
        y_c = mlstm_out(h_m, xconv, p[..., C_Z0:C_Z0 + W_C], g_mlstm_norm[l], skip_m[l])

        y = merge_branches((y_a, y_b, y_c), p[..., GATE0:], w_branch[l], w_out[l])
        x = x + mod[:, 2] * y

        if not last:
            q_ctx = pc[..., A_Q0:A_Q0 + QK_W].reshape(B, tc, H_A, 2, DK)
            yc_a = diff_heads_out(diff_attention(q_ctx, k_ctx, v_ctx, lam), g_diff_subln[l], lam_init)
            yc_b = chunk_spatial_gate(jax.nn.gelu(pc[..., B_UV0:B_UV0 + 2 * W_B]), g_gmlp_v[l],
                                      w_gmlp_s[l], b_gmlp_s[l])
            yc_c = mlstm_out(h_mc, xconv_c, pc[..., C_Z0:C_Z0 + W_C], g_mlstm_norm[l], skip_m[l])
            yc = merge_branches((yc_a, yc_b, yc_c), pc[..., GATE0:], w_branch[l], w_out[l])
            xc = xc + mod_c[2] * yc

        h2 = modulate(rmsnorm(x, g_norm2[l]), mod[:, 3], mod[:, 4]).reshape(B * T, D)
        if last:
            tokens = h2
        else:
            hc2 = modulate(rmsnorm(xc, g_norm2[l]), mod_c[3], mod_c[4]).reshape(B * tc, D)
            tokens = jnp.concatenate([hc2, h2], axis=0)
        eid, wt = hier_route(tokens, w_route_g[l], b_route_g[l], w_route_e[l], b_route_e[l])
        f = moe_experts(tokens, eid, wt, w_e_gate[l], w_e_up[l], w_e_down[l])
        if not last:
            xc = xc + mod_c[5] * f[:B * tc].reshape(B, tc, D)
        x = x + mod[:, 5] * f[f.shape[0] - B * T:].reshape(B, T, D)

    return rmsnorm(x, g_final)


_drawn_inputs = setup_inputs


def setup_inputs(seed=0):
    import zlib

    import numpy as np

    out = dict(_drawn_inputs(seed))
    spreads = {}
    factors = {'g_norm1': 3.752,
     'g_norm2': 3.552,
     'diff_lambda': 3.978,
     'g_diff_subln': 25.4,
     'b_gmlp_s': 8.0,
     'g_gmlp_v': 8.0,
     'b_conv_m': 4.919,
     'g_mlstm_norm': 25.184,
     'skip_m': 8.0,
     'b_route_g': 8.0,
     'b_route_e': 5.952,
     'g_final': 23.524}
    for name, (base, spread) in spreads.items():
        noise = np.random.default_rng([zlib.crc32(name.encode()), seed]).standard_normal(out[name].shape)
        drawn = base * np.exp(spread * noise) if base else spread * noise
        out[name] = jnp.asarray(drawn.astype(out[name].dtype))
    for name, factor in factors.items():
        out[name] = (out[name] * factor).astype(out[name].dtype)
    return out
```

```python
import math
from collections import namedtuple
import numpy as np
import concourse.bass as bass
from concourse import mybir
from contextlib import ExitStack

F32 = mybir.dt.float32
I32 = mybir.dt.int32
ALU = mybir.AluOpType
ACT = mybir.ActivationFunctionType
AX = mybir.AxisListType.X

L, D, CTX, LAT = 2, 1024, 256, 256
T = CTX + LAT
GRID_W, ROPE_BASE, EPS = 64, 10000.0, 1e-6
H, DK, DV = 4, 64, 128
W = 512
CONV_K = 3
NMOD = 6
GROUPS, PER, E = 4, 8, 32
FE = 512
P = 128
KC = D // P
WC = W // P
NTILE = T // P
COLS = 256
RW = KC * COLS
MODG = NMOD * D // COLS
BRG = D // P
OUTG = D // COLS
SCALE = DK ** -0.5
MSCALE = DV ** -0.5
BIG = 1e30

Entry = namedtuple("Entry", "sem base")

BLK = 64
XBLK = [(T * 2) // (BLK + 1), (LAT * 2) // (BLK + 1)]
NBLK = [E + n for n in XBLK]
STEPS = T // BLK - 1


def offsets(parts):
    at, out = 0, {}
    for name, n in parts:
        out[name] = (at, at + n)
        at += n
    return out, at


SMALL, SMALL_W = offsets([
    ("b_mod", NMOD * KC), ("g1", KC), ("g2", KC), ("g_diff", 1), ("g_v", WC), ("w_conv", CONV_K * WC), ("b_conv", WC),
    ("g_ml", WC), ("skip", WC), ("g_fin", KC), ("c", KC * 2), ("w_if", 3 * WC * 16), ("w_route", KC * (GROUPS + E)),
    ("b_if", 16), ("b_route", GROUPS + E), ("w_sT", WC * P), ("w_qkv", 3 * WC * P)])
EARLY, EARLY_W = offsets([("b_s", WC * P), ("lam", 4 * DK)])
CONST, CONST_W = offsets([
    ("ident", P), ("ones", P), ("tri_f", P), ("tri_b", P), ("tri_x", P), ("mask_f", P), ("mask_b", P), ("rot", P),
    ("cos", LAT), ("sin", LAT), ("sel", 2), ("iota", BLK), ("thr", STEPS), ("tok", NTILE)])


def constants():
    t = np.zeros((P, CONST_W), np.float32)

    def put(name, a):
        t[:, CONST[name][0]:CONST[name][1]] = a
    i, j = np.arange(P)[:, None], np.arange(P)[None, :]
    put("ident", i == j)
    put("ones", 1.0)
    put("tri_f", i <= j)
    put("tri_b", i >= j)
    put("tri_x", i < j)
    put("mask_f", np.where(i <= j, 0.0, BIG))
    put("mask_b", np.where(i >= j, 0.0, BIG))
    half = (np.arange(P) // 16) % 2
    rot = np.zeros((P, P), np.float32)
    for p in range(P):
        if half[p] == 0:
            rot[p + 16, p] = -1.0
        else:
            rot[p - 16, p] = 1.0
    put("rot", rot)
    inv = (ROPE_BASE ** (-np.arange(0, 32, 2, dtype=np.float32) / 32)).astype(np.float32)
    tok = np.arange(LAT)
    pos = np.stack([tok // GRID_W, tok % GRID_W]).astype(np.float32)
    ang = pos[(np.arange(P) // 32) % 2] * inv[np.arange(P) % 16][:, None]
    put("cos", np.cos(ang.astype(np.float32)))
    put("sin", np.sin(ang.astype(np.float32)))
    put("sel", np.stack([(np.arange(P) % 32) == 0, (np.arange(P) % 32) == 1], 1))
    put("iota", np.arange(BLK)[None, :])
    put("thr", BLK * (1 + np.arange(STEPS))[None, :])
    put("tok", np.arange(P)[:, None] + P * np.arange(NTILE)[None, :])
    return t


WIN = [(k, c + COLS * g, g) for k, c, n in
       [("k", 0, 2), ("x", 1024, 2), ("v", 512, 2), ("q", 1536, 2), ("u", 2048, 2), ("bv", 2560, 2), ("z", 3072, 2),
        ("gate", 3584, 12)] for g in range(n)]
NGATE = 12
NDENSE = len(WIN) - NGATE
MOD_FIRST = 8
MOD_IN = [MODG, MODG - MOD_FIRST]


def build(nc, xt_in, consts_in, small_in, early_in, wmod, win, wbr, wout, w_gate, w_up, w_down, out, h2_dram, y_dram):
    stack = ExitStack()
    with stack:
        def sb(name, cols, dt=F32, rows=P):
            return stack.enter_context(nc.sbuf_tensor(name, [rows, cols], dt))

        def sem(name):
            return stack.enter_context(nc.semaphore(name))

        def cut(buf, at, *dims):
            n = math.prod(dims)
            v = buf[:, at:at + n]
            if len(dims) == 1:
                return v
            names = "abc"[:len(dims)]
            return v.rearrange(f"p ({' '.join(names)}) -> p {' '.join(names)}", **dict(zip(names, dims)))

        xT = cut(sb("xT", KC * T), 0, KC, T)
        hT = cut(sb("hT", KC * T), 0, KC, T)
        slotA = sb("slotA", 3 * 4096)
        slotB = sb("slotB", 3 * 4096)
        ring = sb("ring", 2 * RW)
        mix = sb("mix", 5 * WC * T)
        small = sb("small", SMALL_W)
        consts = sb("consts", CONST_W)
        misc = sb("misc", 1100)

        def const(name, rows=P):
            return consts[0:rows, CONST[name][0]:CONST[name][1]]

        def par(name, *dims):
            if name in EARLY:
                return cut(slotA, 9216 + EARLY[name][0], *dims)
            a, _ = SMALL[name]
            return cut(small, a, *dims) if dims else small[:, a:a + 1]

        ident = const("ident")
        ones = const("ones")
        xm = cut(mix, 0, WC, T)
        xc = cut(mix, 1 * WC * T, WC, T)
        uT = cut(mix, 2 * WC * T, WC, T)
        vG = cut(mix, 3 * WC * T, NTILE, W)
        yaT = cut(mix, 3 * WC * T, WC, T)
        zT = cut(mix, 4 * WC * T, WC, T)
        gates = cut(slotB, 0, 3 * KC, T)
        qT = cut(slotA, 0, WC, T)
        kT = cut(slotA, 2048, WC, T)
        vA = cut(slotA, 4096, NTILE, W)
        probs = cut(slotA, 6144, 2, T)
        attT = cut(slotA, 7168, NTILE, P)
        attw = cut(slotA, 7680, T)
        oraw = cut(slotA, 9984, H, P)
        oN = cut(slotA, 10496, H, P)
        osq = cut(slotA, 8320, P)
        rope_c = cut(slotA, 8448, LAT)
        rope_s = cut(slotA, 8704, LAT)
        mq = cut(slotA, 6144, WC, 256)
        mk = cut(slotA, 7168, WC, 256)
        mv = cut(slotA, 8192, WC, 256)
        mkt = cut(slotA, 9216, 2, WC, P)
        mvt = cut(slotA, 10240, 2, WC, P)
        hsum = cut(slotA, 11264, 2, WC, P)
        nd = cut(slotA, 0, WC, P)
        dmat = cut(slotA, 512, WC, P)
        sg = cut(slotA, 1024, WC, P)
        vw = cut(slotA, 1536, WC, P)
        num = cut(slotA, 2048, WC, P)
        inter = cut(slotA, 2560, WC, P)
        state = cut(slotA, 3072, 2, WC, P)
        hsq = cut(slotA, 4096, WC, P)
        hn = cut(slotA, 4608, 2, WC, P)
        xs = cut(slotA, 0, WC, 256)
        yt = cut(slotA, 1024, WC, 256)
        nbuf1 = slotB
        nbuf2 = mix
        xg = [mix[0:BLK, i * D:(i + 1) * D] for i in range(2)]
        xgT = [cut(mix, 2048 + 512 * i, KC, BLK) for i in range(2)]
        gs = [mix[:, 3072 + 512 * i:3584 + 512 * i] for i in range(2)]
        act_ = [mix[:, 4096 + 512 * i:4608 + 512 * i] for i in range(2)]
        aT = [cut(mix, 5120 + 256 * i, 4, BLK) for i in range(2)]
        yS = [mix[:, 5632 + 512 * i:6144 + 512 * i] for i in range(2)]
        h2row = [mix[:, 6656 + D * i:6656 + D * (i + 1)] for i in range(2)]
        rt = mix[:, 8704:10240]
        yg = [cut(mix, 2 * D * i, 2, D) for i in range(2)]
        fw = [mix[:, 4096 + D * i:4096 + D * (i + 1)] for i in range(2)]

        at = [0]

        def small_tile(*dims):
            v = cut(misc, at[0], *dims)
            at[0] += math.prod(dims)
            assert at[0] <= 1100
            return v
        csil = small_tile(KC, 32)
        mraw = small_tile(COLS)
        modT = small_tile(L, NMOD * KC, 2)
        normA = small_tile(KC, 2)
        gate2 = small_tile(KC, 2)
        lamv = small_tile(4)
        gvec = small_tile(4 * WC)
        ssq = small_tile(NTILE)
        rst = small_tile(NTILE)
        nmax = small_tile(2)
        nbias = small_tile(2)
        psum_ = small_tile(2)
        prec = small_tile(2)
        oss = small_tile(H)
        orms = small_tile(H)
        mgate = small_tile(2, 16)
        mlf = small_tile(2, 2, H)
        mtmp = small_tile(2, 2, H)
        mb = small_tile(2, 2, H)
        mg = small_tile(2, 2, H)
        mr = small_tile(2, 2, H)
        mMt = small_tile(2, 2, H)
        mst = small_tile(2, H)
        mend = small_tile(H)
        mmax = small_tile(H)
        mex = small_tile(4, H)
        mee = small_tile(4, H)
        nst = small_tile(2, H)
        mden = small_tile(H)
        mden2 = small_tile(H)
        hss = small_tile(2, H)
        PAD = P // 2
        cmax = [slotA[0:8, a:a + 2 * (P + PAD)].rearrange("p (d t) -> p d t", d=2) for a in (4096, 5632)]

        def cm_at(b, d, shift=0):
            a = (PAD - shift) if d == 0 else shift
            return cmax[b][:, d, a:a + P]
        ints = sb("ints", NBLK[0] + 2 * NTILE, I32)
        idxI = ints[0:BLK, 0:NBLK[0]]
        slotI = ints[:, NBLK[0]:]
        idxS = [sb(f"idxS{i}", 1, I32, BLK) for i in range(2)]
        ownI = sb("ownI", XBLK[0] + 1, I32, 1)
        misc_wt = small_tile(2 * NTILE)

        psum = stack.enter_context(nc.psum_tensor("psum", [P, 8 * 512], F32))
        bank = [psum[:, 512 * i:512 * i + 512] for i in range(8)]
        pmod = bank[3]


        BRB = ((4, 5, 6), (0, 1, 7))
        mrg = [mix[:, 512 * b:512 * b + 512] for b in range(3)]
        fin = mix[:, 4096:4096 + KC * LAT]
        y_flat = y_dram
        y_dram = y_dram.rearrange("(b r) n -> b r n", r=BLK)
        ro, used_cols = {}, [0]

        def ro_tile(name, *dims):
            sizes = [[d(l) if callable(d) else d for d in dims] for l in range(L)]
            ro[name] = [cut(rt, used_cols[0], *sizes[l]) for l in range(L)]
            used_cols[0] += max(math.prod(s) for s in sizes)
            assert used_cols[0] <= 1536

        def nt(l):
            return (NTILE, LAT // P)[l]
        for name, *dims in (
                ("lg", nt, GROUPS), ("ge", nt, GROUPS), ("goh", nt, GROUPS), ("gm", nt), ("gi", nt), ("pg", nt), ("t1", nt),
                ("le", nt, E), ("oh1", nt, E), ("oh2", nt, E), ("m", nt, E), ("cand", nt, E), ("m1", nt), ("m2", nt),
                ("idx", 2, nt), ("e2", nt), ("rank", 2, nt), ("ob", 2, nt), ("fl", 2, nt), ("jj", 2, nt), ("bb", 2, nt),
                ("fc", lambda l: 2 * nt(l), STEPS), ("oe", 2, E), ("cmp", STEPS), ("cnt", 1), ("obl", 1)):
            ro_tile(name, *dims)
        for name in ("cmp", "cnt", "obl"):
            ro[name] = [v[0:E] for v in ro[name]]
        ro["own"] = [rt[0:1, 1100:1100 + XBLK[l]] for l in range(L)]
        ro["wt"] = [cut(misc_wt, 0, 2, nt(l)) for l in range(L)]
        ro["cand"] = [cut(rt, 1200, NTILE * E)] * L
        ro["J"] = [cut(mix, 4096, 2 * nt(l), BLK) for l in range(L)]
        ro["BT"] = [cut(mix, 4608, 2 * nt(l), NBLK[l]) for l in range(L)]
        ro["owc"] = [mix[0:1, 5120:5120 + XBLK[l] * E].rearrange("p (a e) -> p a e", e=E) for l in range(L)]

        SPARE = 5
        NU = NTILE * H
        NF = 10
        MUN = [(0, 0), (1, 1), (0, 1), (1, 0)]

        def counted(name, n):
            s = sem(name)
            return [Entry(s, n * l) for l in range(L)]

        def apart(name):
            return [Entry(sem(f"{name}_{l}"), 0) for l in range(L)]

        def by_buffer(name, n):
            both = [counted(f"{name}{i}", n) for i in range(2)]
            return [[both[i][l] for i in range(2)] for l in range(L)]

        def since(entry, value):
            return entry.sem, value + entry.base

        s_const = sem("const_loaded")
        s_x = sem("x_loaded")
        s_zero = sem("padding_zeroed")
        s_c = sem("silu_c")
        mod_mm = sem("mod_parts")
        mod_ev = sem("mod_parts_copied")
        mod_t = sem("mod_transposed")
        mod_out = sem("mod_stored")
        act_step = sem("act_step")
        dve_step = sem("dve_step")
        pool_step = sem("pool_step")
        dense_full = sem("dense_chunk_ready")
        dense_out = sem("dense_chunk_copied")
        f_sq = sem("fin_squares")
        f_mm = sem("fin_summed")
        f_out = sem("fin_out")
        s_out = sem("out_stored")
        s_passed = sem("waits_passed")
        s_spare = sem("spare_rows_filled")
        ring_full = [sem(f"ring_full{i}") for i in range(2)]
        e_full = [sem(f"expert_full{i}") for i in range(2)]
        rms_in, rms_out = sem("mean_squares"), sem("inverse_roots")
        s_small, s_early = apart("small_loaded"), apart("early_loaded")
        n1_sq = counted("n1_squares", KC)
        n1_mm = counted("n1_summed", KC)
        n1_nt = counted("n1_scaled", KC)
        h_ready = counted("h_ready", KC)
        rope_mm = counted("rope_mm", 2 * WC)
        kq_done = counted("kq_roped", 2 * WC)
        conv_done = counted("conv_summed", 1)
        xc_done = counted("xconv_ready", 1)
        bv_sq = counted("bv_squares", NTILE)
        bv_done = counted("bv_normed", NTILE)
        mixg_mm = counted("gmlp_mixed", WC)
        yb_done = counted("yb_ready", WC)
        lam_in = counted("lam_sums", 1)
        lam_ex = counted("lam_exps", 1)
        at_s = counted("att_scores", NU)
        at_nb = counted("att_bias", NU)
        at_exp = counted("att_exp", 2 * NU)
        at_a = counted("att_weights", NU)
        at_T = counted("att_T", NU)
        at_aT = counted("att_T_copied", NU)
        at_o = counted("att_out", NU)
        at_sq = counted("att_squares", NU)
        at_on = counted("att_kept", NU)
        at_oT = counted("att_oT", NTILE)
        at_nd = counted("att_normed", NTILE)
        at_y = counted("att_y", NTILE)
        ml_ff = counted("ml_features", 2 * NF)
        ml_fe = counted("ml_features_copied", 2 * NF)
        ml_gm = counted("ml_gates", 2)
        ml_ga = counted("ml_abs", 2)
        ml_gl = counted("ml_ln", 2)
        ml_lf = counted("ml_logf", 2)
        ml_cs = counted("ml_cumsum", 2)
        ml_r = counted("ml_r", 2)
        ml_rT = counted("ml_rT", 2)
        ml_cm = counted("ml_cummax", 2)
        ml_mt = counted("ml_cummax_T", 2)
        ml_bc = counted("ml_bcast", 2 * len(MUN))
        ml_ei = counted("ml_exponents", 2 * len(MUN))
        ml_nd = counted("ml_neg_d", 2 * len(MUN))
        ml_ex = counted("ml_exps", 2 * len(MUN))
        ml_d = counted("ml_dmat", 2 * len(MUN))
        ml_qk = counted("ml_qk", 2 * len(MUN))
        ml_sg = counted("ml_sg", 2 * len(MUN))
        ml_num = counted("ml_num", 2 * len(MUN))
        ml_int = counted("ml_inter", 2 * len(MUN))
        ml_hr = counted("ml_h", 2 * len(MUN))
        ml_upd = counted("ml_update", 2 * len(MUN))
        ml_st = counted("ml_state", 2 * len(MUN))
        ml_vw = counted("ml_vw", 2 * len(MUN))
        ml_hn = counted("ml_hn", 2)
        ml_hT = counted("ml_hT", 2)
        ml_y = counted("ml_y", 2)
        br_mm = counted("branches_mm", BRG)
        br_step = counted("merge_step", 2 * BRG)
        br_done = counted("merged", BRG + 2)
        wo_mm = counted("out_mm", KC)
        res1 = counted("residual1", KC)
        n2_sq = counted("n2_squares", KC)
        n2_mm = counted("n2_summed", KC)
        n2_nt = counted("n2_scaled", KC)
        h2_ready = counted("h2_ready", KC)
        ro_mm = counted("ro_logits", 1)
        ro_in = counted("ro_biased", 1)
        ro_ei = counted("ro_exp_in", 2)
        ro_ex = counted("ro_exp", 2)
        ro_m = counted("ro_onehots", 1)
        ro_cnt = counted("ro_counts", 1)
        ro_obl = counted("ro_extra", 1)
        ro_ob = counted("ro_bases", 1)
        ro_jb = counted("ro_onehot_jb", 1)
        ro_ix = counted("ro_index_mm", 1)
        ro_done = counted("ro_done", 1)
        h2_T = counted("h2_transposed", NTILE)
        h2_row = counted("h2_row", NTILE)
        mo_ix = counted("mo_index", E)
        mo_xT = counted("mo_xT", E)
        mo_xc = counted("mo_xT_copied", E)
        mo_gu = counted("mo_gate_up", E)
        mo_s = counted("mo_silu", E)
        mo_a = counted("mo_act", E)
        mo_aT = counted("mo_actT", E)
        mo_ac = counted("mo_actT_copied", E)
        mo_d = counted("mo_down", E)
        mo_y = counted("mo_y", E)
        xt_w = apart("xt_weights")
        xt_ix = apart("xt_index")
        xt_xg = apart("xt_x")
        xt_xT = apart("xt_xT")
        xt_xc = apart("xt_xT_copied")
        xt_gu = apart("xt_gate_up")
        xt_s = apart("xt_silu")
        xt_a = apart("xt_act")
        xt_aT = apart("xt_actT")
        xt_ac = apart("xt_actT_copied")
        xt_d = apart("xt_down")
        xt_y = apart("xt_y")
        xt_st = apart("xt_stored")
        cb_w = counted("cb_weighted", NTILE)
        cb_T = counted("cb_transposed", NTILE)
        cb_r = counted("residual2", NTILE)
        h2_st = by_buffer("h2_stored", 16 * (NTILE // 2))
        mo_xg = by_buffer("mo_x", 16 * (E // 2))
        mo_st = by_buffer("mo_stored", 16 + 32 * (E // 2))
        cb_g = by_buffer("cb_gathered", 32 * (NTILE // 2))

        T0 = [0, CTX]
        NT = [T, LAT]
        TILES = [list(range(T0[l] // P, NTILE)) for l in range(L)]
        UNITS = [[(h, t) for t in TILES[l] for h in range(H)] for l in range(L)]

        def with_h(l, seg):
            return not (l == 1 and seg == 0)

        base_in = [MOD_FIRST, 0]
        base_br = [MOD_FIRST + len(WIN) + MOD_IN[0], 0]
        base_in[1] = base_br[0] + BRG + OUTG
        base_br[1] = base_in[1] + len(WIN) + MOD_IN[1]
        mods_in = [list(range(MOD_FIRST, MOD_FIRST + MOD_IN[0])), list(range(MOD_FIRST + MOD_IN[0], 2 * MODG))]

        def in_pos(l, g):
            return base_in[l] + g + min(g, MOD_IN[l])

        def rslot(s):
            return ring[:, s * RW:(s + 1) * RW]

        def chunk_no(l, g, c=1):
            return 2 * (l * len(WIN) + g) + c + 1

        def first_group(what):
            return next(g for g, (k, _, _) in enumerate(WIN) if k == what)

        def used(l_pos):
            for l in range(L):
                for g in range(len(WIN)):
                    if in_pos(l, g) == l_pos:
                        return dense_full, chunk_no(l, g)
                    if g < MOD_IN[l] and in_pos(l, g) + 1 == l_pos:
                        return mod_mm, mods_in[l][g] + 1
                if base_br[l] <= l_pos < base_br[l] + BRG:
                    return since(br_mm[l], l_pos - base_br[l] + 1)
                if base_br[l] + BRG <= l_pos < base_br[l] + BRG + OUTG:
                    return since(wo_mm[l], 2 * (l_pos - base_br[l] - BRG + 1))
            return mod_mm, l_pos + 1

        def fillers(l, u):
            n = 16 // len(UNITS[l])
            return range(u * n, (u + 1) * n)

        def store(eng, blk, buf, s_):
            dst = y_dram[bass.ds(blk, 1), :, :].rearrange("a p (h n) -> (a p) h n", h=2)
            for h in range(2):
                eng.dma_start(dst[:, h, :], buf[64 * h:64 * h + 64, :]).then_inc(s_.sem, 16)

        def wait_alone(eng, s, value):
            eng.wait_ge(s, value)
            eng.sem_inc(s_passed, 1)

        block = stack.enter_context(nc.Block())

        @block.sync
        def _(sp):
            def load(n, src):
                if n >= 2:
                    sp.wait_ge(*used(n - 2))
                sp.dma_start(rslot(n % 2)[:, 0:src.shape[1]], src).then_inc(ring_full[n % 2], 16)

            def row(src, i):
                return src[bass.ds(i, 1), :, :].rearrange("a p n -> (a p) n")

            def expert(l, s, e, full):
                for w, i, n in ((w_gate, 0, FE), (w_up, 1, FE), (w_down, 2, D)):
                    src = w[bass.ds(l * E + e, 1), :, :].rearrange("a (k p) f -> p (a k) f", p=P)
                    sp.dma_start(cut((slotA, slotB)[s], 4096 * i, 4096 // n, n), src).then_inc(full, 16)

            early = slotA[:, 9216:9216 + EARLY_W]
            sp.dma_start(small[:, :], small_in[0]).then_inc(s_small[0].sem, 16)
            sp.dma_start(early, early_in[0]).then_inc(s_early[0].sem, 16)
            load(0, wmod[0])
            load(1, wmod[1])
            sp.dma_start(consts[:, :], consts_in).then_inc(s_const, 16)
            sp.dma_start(xT.rearrange("p c t -> p (c t)"), xt_in).then_inc(s_x, 16)
            with sp.Fori(1, MOD_FIRST // 2) as j:
                for s in range(2):
                    wait_alone(sp, mod_mm, 2 * j + (s - 1))
                    sp.dma_start(rslot(s), row(wmod, 2 * j + s)).then_inc(ring_full[s], 16)
            for l in range(L):
                for g in range(len(WIN)):
                    load(in_pos(l, g), win[l * len(WIN) + g])
                    if g < MOD_IN[l]:
                        load(in_pos(l, g) + 1, wmod[mods_in[l][g]])
                for s in range(2):
                    load(base_br[l] + s, wbr[l * BRG + s])
                sp.wait_ge(*since(ml_y[l], 2 - l))
                expert(l, 0, 0, e_full[0])
                with sp.Fori(1, BRG // 2) as j:
                    for s in range(2):
                        wait_alone(sp, *since(br_mm[l], 2 * j + (s - 1)))
                        w = row(wbr, 2 * j + (l * BRG + s))
                        sp.dma_start(rslot(s)[:, 0:w.shape[1]], w).then_inc(ring_full[s], 16)
                for s in range(2):
                    load(base_br[l] + BRG + s, wout[l * OUTG + s])
                sp.wait_ge(*since(br_done[l], BRG + 2))
                expert(l, 1, 1, e_full[1])
                for s in range(2, OUTG):
                    load(base_br[l] + BRG + s, wout[l * OUTG + s])
                for s in range(2):
                    sp.sem_inc(mo_st[l][s].sem, 16)
                with sp.Fori(1, E // 2) as j:
                    for s in range(2):
                        wait_alone(sp, *since(mo_d[l], 2 * j + (s - 1)))
                        expert(l, s, 2 * j + s, e_full[s])
                        wait_alone(sp, *since(mo_y[l], 2 * j + (s - 1)))
                        store(sp, 2 * j + (s - 2), yS[s], mo_st[l][s])
                for s in range(2):
                    sp.wait_ge(*since(mo_y[l], E - 1 + s))
                    store(sp, E - 2 + s, yS[s], mo_st[l][s])
                if l == 0:
                    sp.wait_ge(*since(ro_in[l], 1))
                    sp.dma_start(small[:, :], small_in[1]).then_inc(s_small[1].sem, 16)
                sp.wait_ge(*since(ro_done[l], 1))
                sp.wait_ge(*since(mo_d[l], E))
                n = sp.value_load(ownI[0:1, XBLK[l]:XBLK[l] + 1], min_val=0, max_val=XBLK[l])
                with sp.If(n > 0):
                    with sp.Fori(0, n) as b:
                        e = sp.value_load(ownI[0:1, bass.ds(b, 1)], min_val=0, max_val=E - 1)
                        expert(l, 0, e, xt_w[l].sem)
                        wait_alone(sp, *since(xt_d[l], b + 1))
                with sp.Else():
                    sp.nop()
                if l == 0:
                    sp.dma_start(early, early_in[1]).then_inc(s_early[1].sem, 16)
            for c in range(2):
                sp.wait_ge(f_out, KC // 2 * (c + 1))
                n = KC // 2 * LAT
                sp.dma_start(out[:, c * n:(c + 1) * n], fin[:, c * n:(c + 1) * n]).then_inc(s_out, 16)
            sp.wait_ge(s_out, 32)

        @block.tensor
        def _(pe):
            dense = [0]
            unturned = []

            def mm(o, a, b, start=True, stop=True):
                return nc.tensor.matmul(o, a, b, start=start, stop=stop)

            def tr(o, a, p0=0):
                return nc.tensor.transpose(o, a, ident[p0:p0 + a.shape[0], p0:p0 + a.shape[0]])

            def mod_parts(s):
                w = cut(rslot(s), 0, KC, COLS)
                for k2 in range(2):
                    for j in range(4):
                        last = mm(pmod[32 * j:32 * j + 32, 0:COLS], csil[:, 2 * j + k2, :], w[:, 2 * j + k2, :],
                                  start=k2 == 0, stop=k2 == 1)
                last.then_inc(mod_mm, 1)

            def mod_turn():
                for c in range(2):
                    last = mm(pmod[:, COLS + 2 * c:COLS + 2 * c + 2], mraw[:, P * c:P * c + P], const("sel"))
                last.then_inc(mod_t, 1)

            def mod_turn_pending():
                if unturned:
                    pe.wait_ge(mod_ev, unturned.pop() + 1)
                    mod_turn()

            def dense_chunk(l, g, c):
                what, _, _ = WIN[g]
                pos = in_pos(l, g)
                w = cut(rslot(pos % 2), 0, KC, COLS)
                t0 = 0 if what in "kxv" else T0[l]
                if c == 0:
                    pe.wait_ge(ring_full[pos % 2], 16 * (pos // 2 + 1))
                d = dense[0]
                dense[0] += 1
                if d >= 2:
                    pe.wait_ge(dense_out, d - 1)
                b = bank[d % 2]
                if what in ("v", "bv"):
                    tiles = list(range(t0 // P, NTILE))
                    n = len(tiles) // 2
                    for i, t in enumerate(tiles[n * c:n * c + n]):
                        for k in range(KC):
                            last = mm(b[:, COLS * i:COLS * (i + 1)], hT[:, k, P * t:P * t + P], w[:, k, :],
                                      start=k == 0, stop=k == KC - 1)
                else:
                    for k in range(KC):
                        last = mm(b[:, 0:T - t0], w[:, k, P * c:P * c + P], hT[:, k, t0:T], start=k == 0, stop=k == KC - 1)
                last.then_inc(dense_full, 1)
                mod_turn_pending()
                if c == 1 and g < MOD_IN[l]:
                    m, pos = mods_in[l][g], pos + 1
                    pe.wait_ge(ring_full[pos % 2], 16 * (pos // 2 + 1))
                    pe.wait_ge(mod_out, m)
                    mod_parts(pos % 2)
                    unturned.append(m)

            def rope(l, i):
                pe.wait_ge(dense_out, chunk_no(l, first_group("k" if i < WC else "q") + i % WC // 2, i % 2))
                if i >= 2:
                    pe.wait_ge(*since(kq_done[l], i - 1))
                elif l > 0:
                    pe.wait_ge(*since(h_ready[l], KC))
                mm(bank[4 + i % 2][:, 0:LAT], const("rot"), (kT if i < WC else qT)[:, i % WC, CTX:T]).then_inc(rope_mm[l].sem, 1)

            def norm(buf, n, squares, done):
                for c in range(KC):
                    pe.wait_ge(*since(squares, c + 1))
                    mm(bank[7][:, 0:n], ones, cut(buf, 512 * (c % 2), n), start=c == 0, stop=c == KC - 1).then_inc(done.sem, 1)

            def gmlp(l):
                pe.wait_ge(*since(bv_done[l], len(TILES[l])))
                pe.wait_ge(*since(kq_done[l], 2 * WC))
                ws = par("w_sT", WC, P)
                for g in range(WC):
                    if g >= 2:
                        pe.wait_ge(*since(yb_done[l], g - 1))
                    for i, t in enumerate(TILES[l]):
                        last = mm(bank[4 + g % 2][:, P * i:P * i + P], vG[:, t, P * g:P * g + P], ws[:, g, :])
                    last.then_inc(mixg_mm[l].sem, 1)

            def att_scores(l, u):
                h, t = UNITS[l][u]
                keys = CTX if t < 2 else T
                if u == 0:
                    pe.wait_ge(*since(yb_done[l], WC))
                    pe.wait_ge(*since(kq_done[l], 2 * WC))
                else:
                    pe.wait_ge(*since(at_exp[l], 2 * u))
                for m in range(2):
                    r = slice(64 * m, 64 * m + 64)
                    last = mm(bank[4 + m][:, 0:keys], qT[r, h, P * t:P * t + P], kT[r, h, 0:keys])
                last.then_inc(at_s[l].sem, 1)

            def att_trans(l, u):
                h, t = UNITS[l][u]
                pe.wait_ge(*since(at_a[l], u + 1))
                if u >= 1:
                    pe.wait_ge(*since(at_aT[l], u))
                for i in range(2 if t < 2 else NTILE):
                    last = tr(bank[6][:, P * i:P * i + P], attw[:, P * i:P * i + P])
                last.then_inc(at_T[l].sem, 1)

            def att_out(l, u):
                h, t = UNITS[l][u]
                n = 2 if t < 2 else NTILE
                pe.wait_ge(*since(at_aT[l], u + 1))
                if u >= 1:
                    pe.wait_ge(*since(at_on[l], u))
                for i in range(n):
                    last = mm(bank[7][:, 0:P], attT[:, i, :], vA[:, i, P * h:P * h + P], start=i == 0, stop=i == n - 1)
                last.then_inc(at_o[l].sem, 1)

            def att_oT(l, i):
                pe.wait_ge(*since(at_nd[l], i + 1))
                if i >= 1:
                    pe.wait_ge(*since(at_y[l], i))
                for h in range(H):
                    last = tr(bank[2][:, P * h:P * h + P], oN[:, h, :])
                last.then_inc(at_oT[l].sem, 1)

            def ml_features(l, seg):
                wq = par("w_qkv", 3 * WC, P)
                sl = slice(256 * seg, 256 * seg + 256)
                jobs = [(s, src, h) for s, src in ((0, xc), (1, xc), (2, xm)) for h in (0, 2)]
                jobs += [(s, src, -1 - i) for i in range(2) for s, src in ((1, xc), (2, xm))]
                if seg == 0:
                    pe.wait_ge(*since(at_exp[l], 2 * len(UNITS[l])))
                    pe.wait_ge(*since(at_aT[l], len(UNITS[l])))
                    pe.wait_ge(*since(at_on[l], len(UNITS[l])))
                    pe.wait_ge(*since(xc_done[l], 1))
                else:
                    pe.wait_ge(*since(ml_st[l], 4))
                    if with_h(l, 0):
                        pe.wait_ge(*since(ml_y[l], 1))
                for i, (s, src, h) in enumerate(jobs):
                    n = seg * NF + i
                    if n >= 4:
                        pe.wait_ge(*since(ml_fe[l], n - 3))
                    b = bank[4 + n % 4]
                    for k in range(2 if h >= 0 else WC):
                        if h >= 0:
                            last = mm(b[:, 256 * k:256 * k + 256], wq[:, s * WC + h + k, :], src[:, h + k, sl])
                        else:
                            t = 256 * seg + P * (-1 - h)
                            last = mm(b[:, P * k:P * k + P], src[:, k, t:t + P], wq[:, s * WC + k, :])
                    last.then_inc(ml_ff[l].sem, 1)

            def ml_gates(l, seg):
                wif = par("w_if", 3 * WC, 16)
                pe.wait_ge(*since(ml_fe[l], NF * (seg + 1)))
                if seg == 0:
                    pe.wait_ge(*since(at_y[l], len(TILES[l])))
                for t in range(2):
                    for i, f in enumerate((mq, mk, mv)):
                        for h in range(WC):
                            last = mm(bank[2][:, 16 * t:16 * t + 16], f[:, h, P * t:P * t + P], wif[:, WC * i + h, :],
                                      start=(i, h) == (0, 0), stop=(i, h) == (2, WC - 1))
                last.then_inc(ml_gm[l].sem, 1)

            def ml_cumulate(l, seg):
                pe.wait_ge(*since(ml_lf[l], seg + 1))
                for d, tri in enumerate(("tri_f", "tri_b")):
                    mm(bank[2][:, 32 + 8 * d:40 + 8 * d], const(tri), mlf[:, :, d, :])
                mm(bank[2][:, 48:64], ones, mlf.rearrange("p a b c -> p (a b c)")).then_inc(ml_cs[l].sem, 1)
                pe.wait_ge(*since(ml_r[l], seg + 1))
                for d in range(2):
                    last = tr(bank[2][0:8, P * (d + 1):P * (d + 2)], mr[:, d, :, :].rearrange("p a b -> p (a b)"))
                last.then_inc(ml_rT[l].sem, 1)

            def ml_max_turn(l, seg):
                pe.wait_ge(*since(ml_cm[l], seg + 1))
                for d in range(2):
                    last = tr(bank[2][:, 64 + 8 * d:72 + 8 * d], cm_at(1, d))
                last.then_inc(ml_mt[l].sem, 1)

            def ml_open(l, seg, w):
                d, t = MUN[w]
                n = 4 * seg + w
                if n >= 1:
                    pe.wait_ge(*since(ml_st[l], n))
                if w == 0:
                    pe.wait_ge(*since(ml_fe[l], NF * (seg + 1)))
                    pe.wait_ge(*since(ml_cm[l], seg + 1))
                for h in range(H):
                    r = t * H + h
                    last = mm(bank[4][:, P * h:P * h + P], ident[0:8, r:r + 1].to_broadcast([8, P]), cm_at(1, d))
                last.then_inc(ml_bc[l].sem, 1)
                if with_h(l, seg):
                    for h in range(H):
                        last = mm(bank[5][:, P * h:P * h + P], mk[:, h, P * t:P * t + P], mq[:, h, P * t:P * t + P])
                    last.then_inc(ml_qk[l].sem, 1)

            def ml_unit(l, seg, w):
                d, t = MUN[w]
                n, nh = 4 * seg + w, 4 * (seg - l) + w
                if with_h(l, seg):
                    pe.wait_ge(*since(ml_sg[l], nh + 1))
                    if nh >= 1:
                        pe.wait_ge(*since(ml_hr[l], nh))
                    for h in range(H):
                        mm(bank[6][:, P * h:P * h + P], sg[:, h, :], mvt[:, t, h, :])
                        mm(bank[2][:, 80 + h:81 + h], sg[:, h, :], ones[:, 0:1])
                    for h in range(H):
                        mm(bank[7][:, P * h:P * h + P], mq[:, h, P * t:P * t + P], state[:, d, h, :])
                        last = mm(bank[2][:, 84 + h:85 + h], mq[:, h, P * t:P * t + P], nst[:, d, h:h + 1])
                    last.then_inc(ml_num[l].sem, 1)
                pe.wait_ge(*since(ml_vw[l], n + 1))
                for h in range(H):
                    mm(bank[5][:, P * h:P * h + P], mkt[:, t, h, :], vw[:, h, :])
                    last = mm(bank[4][:, h:h + 1], mkt[:, t, h, :], mee[:, 1, h:h + 1])
                last.then_inc(ml_upd[l].sem, 1)

            def ml_turn(l, seg):
                pe.wait_ge(*since(ml_hn[l], seg - l + 1))
                for t in range(2):
                    for h in range(H):
                        last = tr(bank[6 + t][:, P * h:P * h + P], hn[:, t, h, :])
                last.then_inc(ml_hT[l].sem, 1)

            def route(l):
                wr = par("w_route", KC, GROUPS + E)
                pe.wait_ge(*since(h2_ready[l], KC))
                nr = GROUPS + E
                for i, t in enumerate(TILES[l]):
                    for k in range(KC):
                        last = mm(bank[0][:, nr * i:nr * i + nr], hT[:, k, P * t:P * t + P], wr[:, k, :],
                                  start=k == 0, stop=k == KC - 1)
                last.then_inc(ro_mm[l].sem, 1)

            def h2_rows(l):
                for i, t in enumerate(TILES[l]):
                    if i >= 2:
                        pe.wait_ge(*since(h2_row[l], i - 1))
                    for k in range(KC):
                        last = tr(psum[:, 512 * (4 + 2 * (i % 2)) + P * k:512 * (4 + 2 * (i % 2)) + P * (k + 1)],
                                  hT[:, k, P * t:P * t + P])
                    last.then_inc(h2_T[l].sem, 1)

            def positions(l):
                n = len(TILES[l])
                m = ro["m"][l]
                pe.wait_ge(*since(ro_m[l], 1))
                for i in range(n):
                    for k in range(i):
                        mm(bank[1][:, E * i:E * i + E], ones, m[:, k, :], start=k == 0, stop=False)
                    mm(bank[1][:, E * i:E * i + E], const("tri_x"), m[:, i, :], start=i == 0, stop=True)
                for i in range(n):
                    last = mm(bank[1][0:E, 256:257], m[:, i, :], ones[:, 0:1], start=i == 0, stop=i == n - 1)
                last.then_inc(ro_cnt[l].sem, 1)
                pe.wait_ge(*since(ro_obl[l], 1))
                o = ro["obl"][l].to_broadcast([E, P])
                mm(bank[2][:, 0:E], o, const("tri_x", E)[:, 0:E])
                mm(bank[2][:, E:2 * E], o, const("tri_f", E)[:, 0:E]).then_inc(ro_ob[l].sem, 1)
                pe.wait_ge(*since(ro_jb[l], 1))
                for i in range(2 * n):
                    last = mm(bank[3][0:BLK, 0:NBLK[l]], ro["J"][l][:, i, :], ro["BT"][l][:, i, :],
                              start=i == 0, stop=i == 2 * n - 1)
                last.then_inc(ro_ix[l].sem, 1)

            def moe_block(s, wA, wait, sems):
                xT_, xc_, gu_, a_, aT_, ac_, d_ = sems
                g, u = cut(wA, 0, KC, FE), cut(wA, 4096, KC, FE)
                dn = cut(wA, 8192, FE // P, D)
                wait("x")
                for k in range(KC):
                    last = tr(bank[0][:, BLK * k:BLK * k + BLK], xg[s][:, P * k:P * k + P])
                last.then_inc(xT_.sem, 1)
                wait("w")
                wait("xc")
                for k in range(KC):
                    for half, w in ((0, g), (1, u)):
                        last = mm(bank[1][64 * half:64 * half + 64, :], xgT[s][:, k, :], w[:, k, :],
                                  start=k == 0, stop=k == KC - 1)
                last.then_inc(gu_.sem, 1)
                wait("a")
                for k in range(FE // P):
                    last = tr(bank[2][:, BLK * k:BLK * k + BLK], act_[s][64:128, P * k:P * k + P], 64)
                last.then_inc(aT_.sem, 1)
                wait("ac")
                for k in range(FE // P):
                    for half in range(2):
                        last = mm(bank[3 + s][64 * half:64 * half + 64, :], aT[s][:, k, :], dn[:, k, 512 * half:512 * half + 512],
                                  start=k == 0, stop=k == FE // P - 1)
                last.then_inc(d_.sem, 1)

            def moe(l):
                pe.wait_ge(*since(ro_done[l], 1))
                pe.wait_ge(*since(h2_row[l], len(TILES[l])))
                with pe.Fori(0, E // 2) as j:
                    for s in range(2):
                        def wait(what):
                            if what == "x":
                                wait_alone(pe, *since(mo_xg[l][s], 16 * j + 16))
                            elif what == "w":
                                pe.wait_ge(e_full[s], 48 * j + (48 + l * 24 * E))
                            else:
                                wait_alone(pe, *since({"xc": mo_xc, "a": mo_a, "ac": mo_ac}[what][l], 2 * j + (s + 1)))
                        moe_block(s, (slotA, slotB)[s], wait,
                                  (mo_xT[l], mo_xc[l], mo_gu[l], mo_a[l], mo_aT[l], mo_ac[l], mo_d[l]))
                n = pe.value_load(ownI[0:1, XBLK[l]:XBLK[l] + 1], min_val=0, max_val=XBLK[l])
                pe.wait_ge(*since(mo_y[l], E))
                with pe.If(n > 0):
                    with pe.Fori(0, n) as b:
                        def wait(what):
                            if what == "x":
                                wait_alone(pe, *since(xt_xg[l], 16 * b + 16))
                            elif what == "w":
                                pe.wait_ge(*since(xt_w[l], 48 * b + 48))
                            else:
                                wait_alone(pe, *since({"xc": xt_xc, "a": xt_a, "ac": xt_ac}[what][l], b + 1))
                        moe_block(0, slotA, wait, (xt_xT[l], xt_xc[l], xt_gu[l], xt_a[l], xt_aT[l], xt_ac[l], xt_d[l]))
                with pe.Else():
                    pe.nop()

            def combine(l):
                for i in range(len(TILES[l])):
                    pe.wait_ge(*since(cb_w[l], i + 1))
                    if i >= 2:
                        pe.wait_ge(*since(cb_r[l], i - 1))
                    for k in range(KC):
                        o = 512 * (4 + 2 * (i % 2)) + P * k
                        last = tr(psum[:, o:o + P], fw[i % 2][:, P * k:P * k + P])
                    last.then_inc(cb_T[l].sem, 1)

            pe.wait_ge(s_c, 1)
            pe.wait_ge(s_zero, 1)
            pe.wait_ge(s_const, 16)
            with pe.Fori(0, MOD_FIRST // 2) as j:
                for s in range(2):
                    pe.wait_ge(ring_full[s], 16 * j + 16)
                    mod_parts(s)
                    pe.wait_ge(mod_ev, 2 * j + (s + 1))
                    mod_turn()
                    pe.wait_ge(mod_out, 2 * j + (s + 1))
            for l in range(L):
                norm(nbuf1, T, n1_sq[l], n1_mm[l])
                pe.wait_ge(*since(h_ready[l], KC))
                pe.wait_ge(*since(s_small[l], 16))
                for g in range(NDENSE):
                    for c in range(2):
                        dense_chunk(l, g, c)
                    if g == first_group("x") + 1:
                        for i in range(WC):
                            rope(l, i)
                    if g == first_group("u") + 1:
                        for i in range(WC, 2 * WC):
                            rope(l, i)
                gmlp(l)
                nu = len(UNITS[l])
                for u in range(nu):
                    att_scores(l, u)
                    for i in fillers(l, u):
                        dense_chunk(l, NDENSE + i // 2, i % 2)
                    att_trans(l, u)
                    if u >= H and u % H == 0:
                        att_oT(l, u // H - 1)
                    att_out(l, u)
                att_oT(l, nu // H - 1)
                gate = 16
                for seg in range(2):
                    ml_features(l, seg)
                    ml_gates(l, seg)
                    dense_chunk(l, NDENSE + gate // 2, gate % 2)
                    gate += 1
                    ml_cumulate(l, seg)
                    ml_max_turn(l, seg)
                    for w in range(4):
                        ml_open(l, seg, w)
                        if w < 3:
                            dense_chunk(l, NDENSE + gate // 2, gate % 2)
                            gate += 1
                        ml_unit(l, seg, w)
                    if with_h(l, seg):
                        ml_turn(l, seg)
                mod_turn_pending()
                pe.wait_ge(*since(ml_y[l], 2 - l))
                pe.wait_ge(*since(ml_st[l], 8))
                pe.wait_ge(dense_out, dense[0])
                t0 = T0[l]
                with pe.Fori(0, BRG // 2) as j:
                    for s in range(2):
                        pe.wait_ge(ring_full[s], 16 * j + (16 + 8 * base_br[l]))
                        pe.wait_ge(*since(br_done[l], 2 * j + (s + 1)))
                        w = cut(rslot(s), 0, 3 * WC, P)
                        for b, y in enumerate((yaT, uT, zT)):
                            for k in range(WC):
                                last = mm(bank[BRB[s][b]][:, 0:NT[l]], w[:, WC * b + k, :], y[:, k, t0:T],
                                          start=k == 0, stop=k == WC - 1)
                        last.then_inc(br_mm[l].sem, 1)
                pe.wait_ge(*since(br_done[l], BRG + 2))
                with pe.Fori(0, OUTG // 2) as j:
                    for s in range(2):
                        pe.wait_ge(ring_full[s], 16 * j + (16 + 8 * (base_br[l] + BRG)))
                        w = cut(rslot(s), 0, KC, COLS)
                        for c in range(2):
                            for k in range(KC):
                                last = mm(bank[4 + 2 * s + c][:, 0:NT[l]], w[:, k, P * c:P * c + P], hT[:, k, t0:T],
                                          start=k == 0, stop=k == KC - 1)
                            last.then_inc(wo_mm[l].sem, 1)
                    pe.wait_ge(*since(res1[l], 4 * j + 4))
                norm(nbuf2, NT[l], n2_sq[l], n2_mm[l])
                route(l)
                h2_rows(l)
                positions(l)
                moe(l)
                combine(l)
            for c in range(KC):
                pe.wait_ge(f_sq, c + 1)
                if c == 0:
                    pe.wait_ge(*since(cb_r[L - 1], len(TILES[L - 1])))
                mm(bank[0][:, 0:LAT], ones, cut(slotB, 512 * (c % 2), LAT), start=c == 0, stop=c == KC - 1).then_inc(f_mm, 1)

        @block.scalar
        def _(act):
            step = [0]
            count = {}
            copied = [0]
            roots = [0]

            def fn(o, i, f, bias=0.0, scale=1.0, accum=None):
                return nc.scalar.activation(o, i, f, bias=bias, scale=scale, accum_out=accum)

            def done(ins, s):
                ins.then_inc(s, 1)
                count[s.name] = count.get(s.name, 0) + 1
                act.wait_ge(s, count[s.name])

            def link(ins):
                step[0] += 1
                ins.then_inc(act_step, 1)
                act.wait_ge(act_step, step[0])

            def root(v):
                roots[0] += 1
                act.wait_ge(rms_in, roots[0])
                done(fn(v, v, ACT.Sqrt), rms_out)

            def dense_copy(l, g, c):
                what, _, gi = WIN[g]
                d = copied[0]
                copied[0] += 1
                b = bank[d % 2]
                t0 = 0 if what in "kxv" else T0[l]
                act.wait_ge(dense_full, d + 1)
                if what in ("v", "bv"):
                    tiles = list(range(t0 // P, NTILE))
                    n = len(tiles) // 2
                    a = tiles[n * c]
                    o = (vA if what == "v" else vG)[:, a:a + n, COLS * gi:COLS * gi + COLS]
                    i = cut(b, 0, n, COLS)
                else:
                    j = 2 * gi + c
                    o = {"k": kT, "q": qT, "x": xm, "u": uT, "z": zT, "gate": gates}[what][:, j, t0:T]
                    i = b[:, 0:T - t0]
                f, s = {"u": (ACT.Gelu_apprx_tanh, 1.0), "bv": (ACT.Gelu_apprx_tanh, 1.0), "z": (ACT.Tanh, 0.5),
                        "gate": (ACT.Tanh, 0.5)}.get(what, (ACT.Copy, 1.0))
                if what == "q" and gi == c == 0 and l:
                    pass
                done(fn(o, i, f, scale=s), dense_out)

            unstored = []

            def mod_store_pending():
                if unstored:
                    m = unstored.pop()
                    act.wait_ge(mod_t, m + 1)
                    k = 2 * (m % MODG)
                    done(fn(modT[:, m // MODG, k:k + 2, :], cut(pmod, COLS, 2, 2), ACT.Copy), mod_out)

            def chunk(l, g, c):
                dense_copy(l, g, c)
                mod_store_pending()
                if c == 1 and g < MOD_IN[l]:
                    m = mods_in[l][g]
                    act.wait_ge(mod_mm, m + 1)
                    done(fn(mraw, pmod[:, 0:COLS], ACT.Copy), mod_ev)
                    unstored.append(m)

            def norm(buf, t0, t1, squares, summed, scaled, ready, shift, factor):
                n = t1 - t0
                for c in range(KC):
                    if c >= 2:
                        act.wait_ge(*since(summed, c - 1))
                    done(fn(cut(buf, 512 * (c % 2), n), xT[:, c, t0:t1], ACT.Square, scale=D ** -0.5), squares.sem)
                root(cut(buf, 2048, n))
                for c in range(KC):
                    act.wait_ge(*since(scaled, c + 1))
                    for w in range(2):
                        a, b = max(t0, 256 * w), 256 * (w + 1)
                        if a < b:
                            src = cut(buf, 1024 + 512 * (c % 2), n)[:, a - t0:b - t0]
                            last = fn(hT[:, c, a:b], src, ACT.Identity, bias=shift[:, c, w:w + 1], scale=factor[:, c, w:w + 1])
                    done(last, ready.sem)

            def attention_exp(l, u):
                h, t = UNITS[l][u]
                keys = CTX if t < 2 else T
                act.wait_ge(*since(at_nb[l], u + 1))
                if u >= 1:
                    act.wait_ge(*since(at_a[l], u))
                for m in range(2):
                    done(fn(probs[:, m, 0:keys], bank[4 + m][:, 0:keys], ACT.Exp, bias=nbias[:, m:m + 1], scale=SCALE,
                       accum=psum_[:, m:m + 1]), at_exp[l].sem)

            def attention_T(l, u):
                h, t = UNITS[l][u]
                n = 2 if t < 2 else NTILE
                act.wait_ge(*since(at_T[l], u + 1))
                if u >= 1:
                    act.wait_ge(*since(at_o[l], u))
                done(fn(attT[:, 0:n, :], cut(bank[6], 0, n, P), ACT.Copy), at_aT[l].sem)

            def attention_square(l, u):
                act.wait_ge(*since(at_o[l], u + 1))
                h = UNITS[l][u][0]
                done(fn(osq, bank[7][:, 0:P], ACT.Square, scale=DV ** -0.5, accum=oss[:, h:h + 1]), at_sq[l].sem)
                if h == H - 1:
                    root(orms)

            def attention_y(l, i):
                t = TILES[l][i]
                act.wait_ge(*since(at_oT[l], i + 1))
                if i == 0:
                    act.wait_ge(*since(mixg_mm[l], WC))
                done(fn(yaT[:, :, P * t:P * t + P], cut(bank[2], 0, H, P), ACT.Copy, scale=gvec[:, 0:1]), at_y[l].sem)

            def ml_logf(l, seg):
                act.wait_ge(*since(ml_ga[l], seg + 1))
                link(fn(mtmp, mtmp, ACT.Exp, scale=-1.0))
                done(fn(mtmp, mtmp, ACT.Ln, bias=1.0), ml_gl[l].sem)

            def ml_unit(l, seg, w):
                d, t = MUN[w]
                n, nh = 4 * seg + w, 4 * (seg - l) + w
                act.wait_ge(*since(ml_ei[l], n + 1))
                done(fn(mee, mex, ACT.Exp), ml_ex[l].sem)
                if with_h(l, seg):
                    act.wait_ge(*since(ml_nd[l], nh + 1))
                    for h in range(H):
                        last = fn(dmat[:, h, :], nd[:, h, :], ACT.Exp, bias=mr[:, d, t, h:h + 1], scale=-1.0)
                    done(last, ml_d[l].sem)

            def ml_inter(l, seg, w):
                nh = 4 * (seg - l) + w
                act.wait_ge(*since(ml_num[l], nh + 1))
                for h in range(H):
                    last = fn(inter[:, h, :], bank[7][:, P * h:P * h + P], ACT.Copy, scale=mee[:, 2, h:h + 1])
                done(last, ml_int[l].sem)

            def moe_block(s, wait, xc_, s_, ac_):
                wait("xT")
                fn(xgT[s], cut(bank[0], 0, KC, BLK), ACT.Copy).then_inc(xc_.sem, 1)
                wait("gu")
                fn(gs[s][64:128, :], bank[1][0:64, :], ACT.Silu).then_inc(s_.sem, 1)
                wait("aT")
                fn(aT[s], cut(bank[2], 0, FE // P, BLK), ACT.Copy).then_inc(ac_.sem, 1)

            act.wait_ge(*since(s_small[0], 16))
            done(fn(csil[:, :, 0:2], par("c", KC, 2), ACT.Silu), s_c)
            mods = modT.rearrange("p l k w -> p (l k) w")
            with act.Fori(0, MOD_FIRST // 2) as j:
                for s in range(2):
                    act.wait_ge(mod_mm, 2 * j + (s + 1))
                    fn(mraw, pmod[:, 0:COLS], ACT.Copy).then_inc(mod_ev, 1)
                    act.wait_ge(mod_t, 2 * j + (s + 1))
                    fn(mods[:, bass.ds(4 * j + 2 * s, 2), :], cut(pmod, COLS, 2, 2), ACT.Copy).then_inc(mod_out, 1)
            count[mod_ev.name] = count[mod_out.name] = MOD_FIRST
            act.wait_ge(s_x, 16)
            for l in range(L):
                if l:
                    act.wait_ge(*since(cb_r[0], len(TILES[0])))
                norm(nbuf1, 0, T, n1_sq[l], n1_mm[l], n1_nt[l], h_ready[l], modT[:, l, 0:KC, :], normA)
                for g in range(NDENSE):
                    for c in range(2):
                        chunk(l, g, c)
                    if g == first_group("q") + 1:
                        act.wait_ge(*since(conv_done[l], 1))
                        done(fn(xc.rearrange("p c t -> p (c t)"), xc.rearrange("p c t -> p (c t)"), ACT.Silu), xc_done[l].sem)
                    if g == first_group("bv") + 1:
                        act.wait_ge(dense_out, copied[0])
                        for i, t in enumerate(TILES[l]):
                            done(fn(attw, vG[:, t, :], ACT.Square, scale=W ** -0.5, accum=ssq[:, t:t + 1]), bv_sq[l].sem)
                        root(rst[:, TILES[l][0]:NTILE])
                act.wait_ge(*since(lam_in[l], 1))
                done(fn(lamv[:, 2:4], lamv[:, 0:2], ACT.Exp), lam_ex[l].sem)
                nu = len(UNITS[l])
                for u in range(nu):
                    attention_exp(l, u)
                    for i in fillers(l, u):
                        chunk(l, NDENSE + i // 2, i % 2)
                    attention_T(l, u)
                    if u >= H and u % H == 0:
                        attention_y(l, u // H - 1)
                    attention_square(l, u)
                attention_y(l, nu // H - 1)
                gate = 16
                for seg in range(2):
                    chunk(l, NDENSE + gate // 2, gate % 2)
                    gate += 1
                    ml_logf(l, seg)
                    for w in range(4):
                        ml_unit(l, seg, w)
                        if w < 3:
                            chunk(l, NDENSE + gate // 2, gate % 2)
                            gate += 1
                        if with_h(l, seg):
                            ml_inter(l, seg, w)
                    if with_h(l, seg):
                        root(hss)
                mod_store_pending()
                act.wait_ge(*since(res1[l], KC))
                norm(nbuf2, T0[l], T, n2_sq[l], n2_mm[l], n2_nt[l], h2_ready[l], modT[:, l, 3 * KC:4 * KC, :], normA)
                for i, t in enumerate(TILES[l]):
                    act.wait_ge(*since(h2_T[l], i + 1))
                    if i >= 2:
                        act.wait_ge(*since(h2_st[l][i % 2], 16 * (i // 2)))
                    b = 512 * (4 + 2 * (i % 2))
                    done(fn(h2row[i % 2], psum[:, b:b + D], ACT.Copy), h2_row[l].sem)
                    act.wait_ge(*since(h2_row[l], i + 1))
                    act.dma_start(h2_dram[l][P * i:P * i + P, :], h2row[i % 2]).then_inc(h2_st[l][i % 2].sem, 16)
                act.wait_ge(*since(ro_ei[l], 1))
                done(fn(ro["ge"][l], ro["ge"][l], ACT.Exp), ro_ex[l].sem)
                act.wait_ge(*since(ro_ei[l], 2))
                done(fn(ro["e2"][l], ro["e2"][l], ACT.Exp), ro_ex[l].sem)
                with act.Fori(0, E // 2) as j:
                    for s in range(2):
                        def wait(what):
                            act.wait_ge(*since({"xT": mo_xT, "gu": mo_gu, "aT": mo_aT}[what][l], 2 * j + (s + 1)))
                        moe_block(s, wait, mo_xc[l], mo_s[l], mo_ac[l])
                act.wait_ge(*since(ro_done[l], 1))
                n = act.value_load(ownI[0:1, XBLK[l]:XBLK[l] + 1], min_val=0, max_val=XBLK[l])
                with act.If(n > 0):
                    with act.Fori(0, n) as b:
                        def wait(what):
                            act.wait_ge(*since({"xT": xt_xT, "gu": xt_gu, "aT": xt_aT}[what][l], b + 1))
                        moe_block(0, wait, xt_xc[l], xt_s[l], xt_ac[l])
                with act.Else():
                    act.nop()
            act.wait_ge(*since(cb_r[L - 1], len(TILES[L - 1])))
            for c in range(KC):
                if c >= 2:
                    act.wait_ge(f_mm, c - 1)
                done(fn(cut(slotB, 512 * (c % 2), LAT), xT[:, c, CTX:T], ACT.Square, scale=D ** -0.5), f_sq)
            root(cut(slotB, 1024, LAT))

        @block.vector
        def _(dve):
            step = [0]
            count = {}
            roots = [0]
            V = nc.vector

            def done(ins, s):
                ins.then_inc(s, 1)
                count[s.name] = count.get(s.name, 0) + 1
                dve.wait_ge(s, count[s.name])

            def link(ins):
                step[0] += 1
                ins.then_inc(dve_step, 1)
                dve.wait_ge(dve_step, step[0])

            def chain():
                dve.wait_ge(dve_step, step[0])

            def free(ins):
                step[0] += 1
                ins.then_inc(dve_step, 1)

            def bc(ap, *shape):
                return ap.to_broadcast(list(shape))

            def rstd(o, i, scale=1.0):
                done(V.tensor_scalar(o, i, scale, EPS, ALU.mult, ALU.add), rms_in)
                roots[0] += 1
                dve.wait_ge(rms_out, roots[0])
                link(V.reciprocal(o, o))

            def norm(buf, t0, t1, summed, scaled, ready, scale_mod, gain):
                n = t1 - t0
                link(V.scalar_tensor_tensor(normA, scale_mod, 1.0, bc(gain.unsqueeze(2), P, KC, 2), ALU.add, ALU.mult))
                dve.wait_ge(*since(summed, KC))
                rs = cut(buf, 2048, n)
                rstd(rs, bank[7][:, 0:n])
                for c in range(KC):
                    if c >= 2:
                        dve.wait_ge(*since(ready, c - 1))
                    done(V.tensor_tensor(cut(buf, 1024 + 512 * (c % 2), n), xT[:, c, t0:t1], rs, ALU.mult), scaled.sem)

            def rope(l, i):
                src = (kT if i < WC else qT)[:, i % WC, CTX:T]
                dve.wait_ge(*since(rope_mm[l], i + 1))
                free(V.tensor_tensor(rope_c, src, const("cos"), ALU.mult))
                link(V.tensor_tensor(rope_s, bank[4 + i % 2][:, 0:LAT], const("sin"), ALU.mult))
                done(V.tensor_tensor(src, rope_c, rope_s, ALU.add), kq_done[l].sem)

            def conv(l):
                wc, b = par("w_conv", CONV_K, WC), par("b_conv", WC)
                for c in range(WC):
                    dve.wait_ge(dense_out, chunk_no(l, first_group("x") + c // 2, c % 2))
                    x = xm[:, c, :].rearrange("p (s t) -> p s t", s=2)
                    o = xc[:, c, :].rearrange("p (s t) -> p s t", s=2)
                    link(V.tensor_scalar(o, x, wc[:, 1, c:c + 1], b[:, c:c + 1], ALU.mult, ALU.add))
                    link(V.scalar_tensor_tensor(o[:, :, 1:256], x[:, :, 0:255], wc[:, 0, c:c + 1], o[:, :, 1:256], ALU.mult, ALU.add))
                    last = V.scalar_tensor_tensor(o[:, :, 0:255], x[:, :, 1:256], wc[:, 2, c:c + 1], o[:, :, 0:255], ALU.mult, ALU.add)
                    if c < WC - 1:
                        free(last)
                done(last, conv_done[l].sem)

            def gmlp(l):
                dve.wait_ge(*since(bv_sq[l], len(TILES[l])))
                a, b = TILES[l][0], NTILE
                dve.wait_ge(*since(s_early[l], 16))
                rstd(rst[:, a:b], ssq[:, a:b])
                for t in TILES[l]:
                    done(V.tensor_scalar(vG[:, t, :], vG[:, t, :], rst[:, t:t + 1], None, ALU.mult), bv_done[l].sem)
                gv, bs = par("g_v", WC), par("b_s", WC, P)
                n = len(TILES[l])
                for g in range(WC):
                    dve.wait_ge(*since(mixg_mm[l], g + 1))
                    dve.wait_ge(dense_out, chunk_no(l, first_group("u") + 1))
                    link(V.scalar_tensor_tensor(cut(slotA, 7680, n, P), cut(bank[4 + g % 2], 0, n, P), gv[:, g:g + 1],
                                                bc(bs[:, g, :].unsqueeze(1), P, n, P), ALU.mult, ALU.add))
                    o = uT[:, g, T0[l]:T]
                    done(V.tensor_tensor(o, o, attw[:, 0:NT[l]], ALU.mult), yb_done[l].sem)

            def factors(l):
                init = 0.8 - 0.6 * math.exp(-0.3 * l)
                lam = par("lam", 4, DK)
                prod = cut(slotA, 7680, 2, DK)
                link(V.tensor_tensor(prod, lam[:, 0:4:2, :], lam[:, 1:4:2, :], ALU.mult))
                done(V.tensor_reduce(lamv[:, 0:2], prod, AX, ALU.add), lam_in[l].sem)
                free(V.tensor_scalar(gvec[:, 0:1], par("g_diff"), 1.0 - init, None, ALU.mult))
                free(V.tensor_scalar(gvec[:, 1:1 + WC], par("g_ml", WC), 0.5, None, ALU.mult))
                free(V.tensor_scalar(gvec[:, 5:5 + WC], par("skip", WC), 0.5, None, ALU.mult))
                dve.wait_ge(*since(lam_ex[l], 1))
                link(V.scalar_tensor_tensor(lamv[:, 0:1], lamv[:, 2:3], init, lamv[:, 3:4], ALU.add, ALU.subtract))

            def att_weights(l, u):
                h, t = UNITS[l][u]
                keys = CTX if t < 2 else T
                dve.wait_ge(*since(at_s[l], u + 1))
                link(V.tensor_reduce(nmax, cut(psum, 4 * 512, 2, 512)[:, :, 0:keys], AX, ALU.max))
                done(V.tensor_scalar(nbias, nmax, -SCALE, None, ALU.mult), at_nb[l].sem)
                dve.wait_ge(*since(at_exp[l], 2 * u + 2))
                link(V.reciprocal(prec, psum_))
                link(V.tensor_tensor(prec[:, 1:2], prec[:, 1:2], lamv[:, 0:1], ALU.mult))
                link(V.tensor_scalar(probs[:, 1, 0:keys], probs[:, 1, 0:keys], prec[:, 1:2], None, ALU.mult))
                if u >= 1:
                    dve.wait_ge(*since(at_T[l], u))
                done(V.scalar_tensor_tensor(attw[:, 0:keys], probs[:, 0, 0:keys], prec[:, 0:1], probs[:, 1, 0:keys],
                                       ALU.mult, ALU.subtract), at_a[l].sem)

            def att_norm(l, u):
                h, t = UNITS[l][u]
                dve.wait_ge(*since(at_sq[l], u + 1))
                done(V.tensor_copy(oraw[:, h, :], bank[7][:, 0:P]), at_on[l].sem)
                if h == H - 1:
                    dve.wait_ge(*since(at_on[l], u + 1))
                    rstd(orms, oss)
                    if u >= H:
                        dve.wait_ge(*since(at_oT[l], u // H))
                    done(V.tensor_tensor(oN, oraw, bc(orms.unsqueeze(2), P, H, P), ALU.mult), at_nd[l].sem)

            def ml_features(l, seg):
                for i in range(NF):
                    n = seg * NF + i
                    dve.wait_ge(*since(ml_ff[l], n + 1))
                    b = bank[4 + n % 4]
                    if i < 6:
                        o = (mq, mk, mv)[i // 2][:, 2 * (i % 2):2 * (i % 2) + 2, :]
                        done(V.tensor_copy(o, cut(b, 0, 2, 256)), ml_fe[l].sem)
                    elif i % 2 == 0:
                        done(V.tensor_scalar(mkt[:, (i - 6) // 2, :, :], cut(b, 0, WC, P), MSCALE, None, ALU.mult), ml_fe[l].sem)
                    else:
                        done(V.tensor_copy(mvt[:, (i - 6) // 2, :, :], cut(b, 0, WC, P)), ml_fe[l].sem)

            def ml_gates(l, seg):
                dve.wait_ge(*since(ml_gm[l], seg + 1))
                link(V.tensor_tensor(mgate, cut(bank[2], 0, 2, 16), bc(par("b_if", 16).unsqueeze(1), P, 2, 16), ALU.add))
                g4 = mgate.rearrange("p t (d i h) -> p (t d) i h", d=2, i=2)
                f = g4[:, :, 1, :]
                tm = mtmp.rearrange("p t d h -> p (t d) h")
                done(V.scalar_tensor_tensor(tm, f, -1.0, f, ALU.mult, ALU.max), ml_ga[l].sem)
                dve.wait_ge(*since(ml_gl[l], seg + 1))
                done(V.scalar_tensor_tensor(mlf.rearrange("p t d h -> p (t d) h"), f, 0.0, tm, ALU.min, ALU.subtract), ml_lf[l].sem)
                dve.wait_ge(*since(ml_cs[l], seg + 1))
                free(V.tensor_copy(mg, cut(bank[2], 48, 2, 2, H)))
                link(V.tensor_copy(mb, cut(bank[2], 32, 2, 2, H)))
                g5 = mgate.rearrange("p t (d i h) -> p t d i h", d=2, i=2)
                for d in range(2):
                    last = V.tensor_tensor(mr[:, d, :, :], g5[:, :, d, 0, :], mb[:, d, :, :], ALU.subtract)
                    if d == 0:
                        free(last)
                done(last, ml_r[l].sem)
                for i in range(2):
                    free(V.memset(cmax[i][:, 0, 0:PAD], -BIG))
                    free(V.memset(cmax[i][:, 1, P:P + PAD], -BIG))
                dve.wait_ge(*since(ml_rT[l], seg + 1))
                for d in range(2):
                    free(V.tensor_copy(cm_at(0, d), bank[2][0:8, P * (d + 1):P * (d + 2)]))
                chain()
                for i in range(7):
                    for d in range(2):
                        last = V.tensor_tensor(cm_at((i + 1) % 2, d), cm_at(i % 2, d), cm_at(i % 2, d, 2 ** i), ALU.max)
                        if i < 6 or d == 0:
                            free(last)
                    if i < 6:
                        chain()
                done(last, ml_cm[l].sem)
                dve.wait_ge(*since(ml_mt[l], seg + 1))
                link(V.tensor_copy(mMt, cut(bank[2], 64, 2, 2, H)))

            def ml_exponents(l, seg, w):
                d, t = MUN[w]
                n = 4 * seg + w
                m0 = mst[:, d, :]
                dve.wait_ge(*since(ml_bc[l], n + 1))
                link(V.tensor_tensor(mend, m0, cut(bank[4], 0, H, P)[:, :, P - 1 if d == 0 else 0], ALU.max))
                if n >= 1:
                    dve.wait_ge(*since(ml_ex[l], n))
                free(V.tensor_tensor(mex[:, 0, :], m0, mend, ALU.subtract))
                last = V.tensor_tensor(mex[:, 1, :], mr[:, d, t, :], mend, ALU.subtract)
                if with_h(l, seg):
                    free(last)
                    link(V.tensor_tensor(mmax, mMt[:, d, t, :], m0, ALU.max))
                    free(V.tensor_tensor(mex[:, 2, :], m0, mmax, ALU.subtract))
                    last = V.scalar_tensor_tensor(mex[:, 3, :], mb[:, d, t, :], -1.0, mmax, ALU.mult, ALU.subtract)
                done(last, ml_ei[l].sem)
                if with_h(l, seg):
                    for h in range(H):
                        last = V.scalar_tensor_tensor(nd[:, h, :], bank[4][:, P * h:P * h + P], m0[:, h:h + 1],
                                                      const(("mask_f", "mask_b")[d]), ALU.max, ALU.add)
                        if h < H - 1:
                            free(last)
                    done(last, ml_nd[l].sem)
                    dve.wait_ge(*since(ml_nd[l], 4 * (seg - l) + w + 1))
                free(V.tensor_tensor(m0, mg[:, t, d, :], mend, ALU.add))

            def ml_unit(l, seg, w):
                d, t = MUN[w]
                n, nh = 4 * seg + w, 4 * (seg - l) + w
                if with_h(l, seg):
                    dve.wait_ge(*since(ml_d[l], nh + 1))
                    dve.wait_ge(*since(ml_qk[l], nh + 1))
                    done(V.scalar_tensor_tensor(sg, cut(bank[5], 0, H, P), MSCALE, dmat, ALU.mult, ALU.mult), ml_sg[l].sem)
                dve.wait_ge(*since(ml_ex[l], n + 1))
                done(V.tensor_tensor(vw, mvt[:, t, :, :], bc(mee[:, 1, :].unsqueeze(2), P, H, P), ALU.mult), ml_vw[l].sem)
                if with_h(l, seg):
                    dve.wait_ge(*since(ml_int[l], nh + 1))
                    free(V.tensor_tensor(num, inter, cut(bank[6], 0, H, P), ALU.add))
                    link(V.tensor_tensor(mden, bank[2][:, 84:88], mee[:, 2, :], ALU.mult))
                    link(V.tensor_tensor(mden, bank[2][:, 80:84], mden, ALU.add))
                    link(V.scalar_tensor_tensor(mden, mden, -1.0, mden, ALU.mult, ALU.max))
                    link(V.tensor_tensor(mden, mden, mee[:, 3, :], ALU.max))
                    link(V.reciprocal(mden2, mden))
                    r = bc(mden2.unsqueeze(2), P, H, P)
                    if w < 2:
                        done(V.tensor_tensor(hsum[:, t, :, :], num, r, ALU.mult), ml_hr[l].sem)
                    else:
                        link(V.tensor_tensor(num, num, r, ALU.mult))
                        done(V.tensor_tensor(hsum[:, t, :, :], hsum[:, t, :, :], num, ALU.add), ml_hr[l].sem)
                dve.wait_ge(*since(ml_upd[l], n + 1))
                for h in range(H):
                    c = state[:, d, h, :]
                    free(V.scalar_tensor_tensor(c, c, mee[:, 0, h:h + 1], bank[5][:, P * h:P * h + P], ALU.mult, ALU.add))
                link(V.tensor_tensor(nst[:, d, :], nst[:, d, :], mee[:, 0, :], ALU.mult))
                done(V.tensor_tensor(nst[:, d, :], nst[:, d, :], bank[4][:, 0:H], ALU.add), ml_st[l].sem)
                dve.wait_ge(*since(ml_st[l], n + 1))

            def ml_output(l, seg):
                i = seg - l
                dve.wait_ge(*since(ml_hr[l], 4 * (i + 1)))
                for t in range(2):
                    link(V.tensor_tensor(hsq, hsum[:, t, :, :], hsum[:, t, :, :], ALU.mult))
                    link(V.tensor_reduce(hss[:, t, :], hsq, AX, ALU.add))
                rstd(hss, hss, 1.0 / DV)
                for t in range(2):
                    last = V.tensor_tensor(hn[:, t, :, :], hsum[:, t, :, :], bc(hss[:, t, :].unsqueeze(2), P, H, P), ALU.mult)
                    if t == 0:
                        free(last)
                done(last, ml_hn[l].sem)
                sl = slice(256 * seg, 256 * seg + 256)
                for h in range(H):
                    free(V.tensor_scalar(xs[:, h, :], xc[:, h, sl], gvec[:, 5 + h:6 + h], None, ALU.mult))
                chain()
                dve.wait_ge(*since(ml_hT[l], i + 1))
                for h in range(H):
                    src = cut(psum, 6 * 512, 2, 512)[:, :, P * h:P * h + P]
                    free(V.scalar_tensor_tensor(yt[:, h, :].rearrange("p (t e) -> p t e", t=2), src, gvec[:, 1 + h:2 + h],
                                                xs[:, h, :].rearrange("p (t e) -> p t e", t=2), ALU.mult, ALU.add))
                chain()
                dve.wait_ge(dense_out, chunk_no(l, first_group("z") + 1))
                done(V.scalar_tensor_tensor(zT[:, :, sl], zT[:, :, sl], 1.0, yt, ALU.add, ALU.mult), ml_y[l].sem)

            def first_of(o, idx, x, big, iota, n, m):
                tmp = ro["cand"][0][:, 0:n * m].rearrange("p (n m) -> p n m", n=n)
                link(V.tensor_tensor(o, x, bc(big.unsqueeze(2), P, n, m), ALU.is_equal))
                link(V.scalar_tensor_tensor(tmp, o, -1024.0, bc(iota.unsqueeze(1), P, n, m), ALU.mult, ALU.add))
                link(V.tensor_reduce(idx, tmp, AX, ALU.min))
                link(V.tensor_scalar(idx, idx, 1024.0, None, ALU.add))
                link(V.tensor_tensor(o, bc(iota.unsqueeze(1), P, n, m), bc(idx.unsqueeze(2), P, n, m), ALU.is_equal))

            def route(l):
                n = len(TILES[l])
                br = par("b_route", GROUPS + E)
                lg, le, oh1, oh2, m = (ro[k][l] for k in ("lg", "le", "oh1", "oh2", "m"))
                iota = const("iota")
                logits = cut(bank[0], 0, n, GROUPS + E)
                dve.wait_ge(*since(ro_mm[l], 1))
                free(V.tensor_tensor(lg, logits[:, :, 0:GROUPS], bc(br[:, 0:GROUPS].unsqueeze(1), P, n, GROUPS), ALU.add))
                done(V.tensor_tensor(le, logits[:, :, GROUPS:], bc(br[:, GROUPS:].unsqueeze(1), P, n, E), ALU.add), ro_in[l].sem)
                dve.wait_ge(*since(ro_in[l], 1))
                gm, gi, ge = ro["gm"][l], ro["gi"][l], ro["ge"][l]
                link(V.tensor_reduce(gm, lg, AX, ALU.max))
                done(V.tensor_tensor(ge, lg, bc(gm.unsqueeze(2), P, n, GROUPS), ALU.subtract), ro_ei[l].sem)
                oh = ro["goh"][l]
                first_of(oh, gi, lg, gm, iota[:, 0:GROUPS], n, GROUPS)
                link(V.tensor_scalar(oh, oh, 1.0, BIG, ALU.subtract, ALU.mult))
                v = le.rearrange("p n (g e) -> p (n g) e", g=GROUPS)
                link(V.tensor_tensor(v, v, bc(oh.rearrange("p n g -> p (n g)").unsqueeze(2), P, n * GROUPS, PER), ALU.add))
                m1, m2, idx, e2 = ro["m1"][l], ro["m2"][l], ro["idx"][l], ro["e2"][l]
                link(V.tensor_reduce(m1, le, AX, ALU.max))
                first_of(oh1, idx[:, 0, :], le, m1, iota[:, 0:E], n, E)
                link(V.scalar_tensor_tensor(le, oh1, -4.0 * BIG, le, ALU.mult, ALU.add))
                link(V.tensor_reduce(m2, le, AX, ALU.max))
                first_of(oh2, idx[:, 1, :], le, m2, iota[:, 0:E], n, E)
                done(V.tensor_tensor(m, oh1, oh2, ALU.add), ro_m[l].sem)
                done(V.tensor_tensor(e2, m2, m1, ALU.subtract), ro_ei[l].sem)
                dve.wait_ge(*since(ro_ex[l], 1))
                pg = ro["pg"][l]
                link(V.tensor_reduce(pg, ge, AX, ALU.add))
                link(V.reciprocal(pg, pg))
                dve.wait_ge(*since(ro_ex[l], 2))
                t1 = ro["t1"][l]
                wt = ro["wt"][l]
                link(V.tensor_scalar(t1, e2, 1.0, None, ALU.add))
                link(V.reciprocal(t1, t1))
                link(V.tensor_tensor(wt[:, 0, :], pg, t1, ALU.mult))
                link(V.tensor_tensor(wt[:, 1, :], wt[:, 0, :], e2, ALU.mult))
                dve.wait_ge(*since(ro_cnt[l], 1))
                cmp_, cnt = ro["cmp"][l], ro["cnt"][l]
                link(V.tensor_copy(cnt, bank[1][0:E, 256:257]))
                link(V.tensor_scalar(cmp_, const("thr", E), cnt, None, ALU.is_lt))
                done(V.tensor_reduce(ro["obl"][l], cmp_, AX, ALU.add), ro_obl[l].sem)
                rank, ob, fl, jj, bb = (ro[k][l] for k in ("rank", "ob", "fl", "jj", "bb"))
                tmp = ro["cand"][0][:, 0:n * E].rearrange("p (n e) -> p n e", n=n)
                for k, o in ((0, oh1), (1, oh2)):
                    link(V.tensor_tensor(tmp, o, cut(bank[1], 0, n, E), ALU.mult))
                    link(V.tensor_reduce(rank[:, k, :], tmp, AX, ALU.add))
                dve.wait_ge(*since(ro_ob[l], 1))
                oe = ro["oe"][l]
                link(V.tensor_copy(oe, cut(bank[2], 0, 2, E)))
                for k, o in ((0, oh1), (1, oh2)):
                    link(V.tensor_tensor(tmp, o, bc(oe[:, 0, :].unsqueeze(1), P, n, E), ALU.mult))
                    link(V.tensor_reduce(ob[:, k, :], tmp, AX, ALU.add))
                fc = ro["fc"][l]
                f1 = [a.rearrange("p k n -> p (k n)") for a in (rank, ob, fl, jj, bb, idx)]
                rank, ob, fl, jj, bb, ix = f1
                link(V.tensor_tensor(fc, bc(rank.unsqueeze(2), P, 2 * n, STEPS), bc(const("thr").unsqueeze(1), P, 2 * n, STEPS), ALU.is_ge))
                link(V.tensor_reduce(fl, fc, AX, ALU.add))
                link(V.scalar_tensor_tensor(jj, fl, -float(BLK), rank, ALU.mult, ALU.add))
                link(V.tensor_tensor(ob, ob, fl, ALU.add))
                link(V.scalar_tensor_tensor(ob, ob, E - 1.0, ix, ALU.add, ALU.subtract))
                link(V.scalar_tensor_tensor(bb, fl, 1.0, ob, ALU.is_ge, ALU.mult))
                link(V.tensor_tensor(bb, bb, ix, ALU.add))
                free(V.scalar_tensor_tensor(slotI[:, 0:2 * n], bb, float(BLK), jj, ALU.mult, ALU.add))
                J, BT = ro["J"][l], ro["BT"][l]
                nb = NBLK[l]
                free(V.tensor_tensor(J, bc(iota.unsqueeze(1), P, 2 * n, BLK), bc(jj.unsqueeze(2), P, 2 * n, BLK), ALU.is_equal))
                link(V.tensor_tensor(BT, bc(iota[:, 0:nb].unsqueeze(1), P, 2 * n, nb), bc(bb.unsqueeze(2), P, 2 * n, nb), ALU.is_equal))
                tok = const("tok")[:, 0:n]
                for k in range(2):
                    part = BT[:, n * k:n * k + n, :]
                    last = V.tensor_tensor(part, part, bc(tok.unsqueeze(2), P, n, nb), ALU.mult)
                    if k == 0:
                        free(last)
                done(last, ro_jb[l].sem)
                xb = XBLK[l]
                own, owc = ro["own"][l], ro["owc"][l]
                link(V.tensor_tensor(owc, bc(oe[0:1, 1, :].unsqueeze(1), 1, xb, E), bc(iota[0:1, 0:xb].unsqueeze(2), 1, xb, E), ALU.is_le))
                link(V.tensor_reduce(own[:, 0:xb], owc, AX, ALU.add))
                free(V.tensor_scalar(ownI[:, 0:xb], own[:, 0:xb], E - 1.0, None, ALU.min))
                free(V.tensor_copy(ownI[:, xb:xb + 1], oe[0:1, 1, E - 1:E]))
                dve.wait_ge(*since(ro_ix[l], 1))
                done(V.tensor_copy(idxI[:, 0:nb], bank[3][0:BLK, 0:nb]), ro_done[l].sem)

            def moe_act(s, o):
                return V.tensor_tensor(act_[s][64:128, :], gs[s][64:128, :], bank[1][64:128, :], ALU.mult).then_inc(o.sem, 1)

            dve.wait_ge(s_const, 16)
            for l in range(L):
                dve.wait_ge(*since(s_small[l], 16))
                if l == 0:
                    dve.wait_ge(mod_out, MOD_FIRST)
                    dve.wait_ge(s_x, 16)
                else:
                    dve.wait_ge(mod_out, MODG + MOD_FIRST)
                head = modT[:, l, 0:2 * KC, :]
                bm = par("b_mod", NMOD * KC)
                link(V.tensor_tensor(head, head, bc(bm[:, 0:2 * KC].unsqueeze(2), P, 2 * KC, 2), ALU.add))
                norm(nbuf1, 0, T, n1_mm[l], n1_nt[l], h_ready[l], modT[:, l, KC:2 * KC, :], par("g1", KC))
                for i in range(WC):
                    rope(l, i)
                conv(l)
                for i in range(WC, 2 * WC):
                    rope(l, i)
                gmlp(l)
                factors(l)
                for u in range(len(UNITS[l])):
                    att_weights(l, u)
                    att_norm(l, u)
                for seg in range(2):
                    ml_features(l, seg)
                    if seg == 0:
                        free(V.memset(state, 0.0))
                        free(V.memset(nst, 0.0))
                        free(V.memset(mst, 0.0))
                    ml_gates(l, seg)
                    for w in range(4):
                        ml_exponents(l, seg, w)
                        ml_unit(l, seg, w)
                    if with_h(l, seg):
                        ml_output(l, seg)
                dve.wait_ge(mod_out, MODG * (l + 1))
                tail = modT[:, l, 2 * KC:, :]
                link(V.tensor_tensor(tail, tail, bc(bm[:, 2 * KC:].unsqueeze(2), P, 4 * KC, 2), ALU.add))
                link(V.tensor_scalar(gate2, modT[:, l, 2 * KC:3 * KC, :], 0.5, None, ALU.mult))
                dve.wait_ge(dense_out, chunk_no(l, len(WIN) - 1))
                dve.sem_inc(br_done[l].sem, 2)
                t0, n = T0[l], NT[l]
                with dve.Fori(0, BRG // 2) as j:
                    for s in range(2):
                        i = 2 * j + s
                        dve.wait_ge(*since(br_mm[l], i + 1))
                        for b in range(3):
                            g = gates[:, bass.ds(i + KC * b, 1), t0:T].rearrange("p a t -> p (a t)")
                            last = V.scalar_tensor_tensor(mrg[b][:, 0:n], g, 1.0, bank[BRB[s][b]][:, 0:n], ALU.add, ALU.mult)
                        last.then_inc(br_step[l].sem, 1)
                        dve.wait_ge(*since(br_step[l], 4 * j + (2 * s + 1)))
                        V.tensor_tensor(mrg[0][:, 0:n], mrg[0][:, 0:n], mrg[1][:, 0:n], ALU.add).then_inc(br_step[l].sem, 1)
                        dve.wait_ge(*since(br_step[l], 4 * j + (2 * s + 2)))
                        o = hT[:, bass.ds(i, 1), t0:T].rearrange("p a t -> p (a t)")
                        V.tensor_tensor(o, mrg[0][:, 0:n], mrg[2][:, 0:n], ALU.add).then_inc(br_done[l].sem, 1)
                        dve.wait_ge(*since(br_done[l], 2 * j + (s + 3)))
                for c in range(KC):
                    dve.wait_ge(*since(wo_mm[l], c + 1))
                    for w in range(1 if l else 0, 2):
                        x = xT[:, c, 256 * w:256 * w + 256]
                        y = bank[4 + c % 4][:, 256 * w - t0:256 * w - t0 + 256]
                        last = V.scalar_tensor_tensor(x, y, gate2[:, c, w:w + 1], x, ALU.mult, ALU.add)
                    done(last, res1[l].sem)
                dve.wait_ge(*since(res1[l], KC))
                norm(nbuf2, t0, T, n2_mm[l], n2_nt[l], h2_ready[l], modT[:, l, 4 * KC:5 * KC, :], par("g2", KC))
                route(l)
                with dve.Fori(0, E // 2) as j:
                    for s in range(2):
                        dve.wait_ge(*since(mo_s[l], 2 * j + (s + 1)))
                        moe_act(s, mo_a[l])
                        dve.wait_ge(*since(mo_d[l], 2 * j + (s + 1)))
                        dve.wait_ge(*since(mo_st[l][s], 32 * j + 16))
                        V.tensor_copy(yS[s], bank[3 + s]).then_inc(mo_y[l].sem, 1)
                dve.wait_ge(*since(ro_done[l], 1))
                nx = dve.value_load(ownI[0:1, XBLK[l]:XBLK[l] + 1], min_val=0, max_val=XBLK[l])
                with dve.If(nx > 0):
                    with dve.Fori(0, nx) as b:
                        dve.wait_ge(*since(xt_s[l], b + 1))
                        moe_act(0, xt_a[l])
                        dve.wait_ge(*since(xt_d[l], b + 1))
                        dve.wait_ge(*since(xt_xg[l], 16 * b + 16))
                        V.tensor_copy(yS[0], bank[3]).then_inc(xt_y[l].sem, 1)
                with dve.Else():
                    dve.nop()
                nt = len(TILES[l])
                wt = ro["wt"][l]

                def residual2(i):
                    dve.wait_ge(*since(cb_T[l], i + 1))
                    t = TILES[l][i]
                    w = 0 if t < 2 else 1
                    for c in range(KC):
                        x = xT[:, c, P * t:P * t + P]
                        o = 512 * (4 + 2 * (i % 2)) + P * c
                        last = V.scalar_tensor_tensor(x, psum[:, o:o + P], modT[:, l, 5 * KC + c, w:w + 1], x, ALU.mult, ALU.add)
                        if c < KC - 1:
                            free(last)
                    done(last, cb_r[l].sem)
                for i in range(nt):
                    dve.wait_ge(*since(cb_g[l][i % 2], 32 * (i // 2 + 1)))
                    if i >= 2:
                        dve.wait_ge(*since(cb_T[l], i - 1))
                    link(V.tensor_scalar(fw[i % 2], yg[i % 2][:, 0, :], wt[:, 0, i:i + 1], None, ALU.mult))
                    done(V.scalar_tensor_tensor(fw[i % 2], yg[i % 2][:, 1, :], wt[:, 1, i:i + 1], fw[i % 2], ALU.mult, ALU.add), cb_w[l].sem)
                    if i >= 1:
                        residual2(i - 1)
                residual2(nt - 1)
            dve.wait_ge(*since(cb_r[L - 1], len(TILES[L - 1])))
            dve.wait_ge(f_mm, KC)
            rs = cut(slotB, 1024, LAT)
            rstd(rs, bank[0][:, 0:LAT])
            gf = par("g_fin", KC)
            for c in range(KC):
                done(V.scalar_tensor_tensor(fin[:, c * LAT:(c + 1) * LAT], xT[:, c, CTX:T], gf[:, c:c + 1], rs, ALU.mult, ALU.mult), f_out)

        @block.gpsimd
        def _(pool):
            nc.gpsimd.memset(csil[:, :, 2:32], 0.0).then_inc(s_zero, 1)
            n = XBLK[0] * BLK * D // P
            spare = y_flat[E * BLK:, :].rearrange("r n -> (r n)").rearrange("(p n) -> p n", p=P)
            pool.wait_ge(s_const, 16)
            for i in range(SPARE):
                w = n // SPARE
                pool.dma_start(spare[:, w * i:w * i + w], consts[:, 0:w]).then_inc(s_spare, 16)

            def gather(o, src, idx, s_):
                nc.gpsimd.indirect_dma_start(o, None, src[:, :], bass.IndirectOffsetOnAxis(ap=idx, axis=0)).then_inc(s_.sem, 16)

            for l in range(L):
                n = len(TILES[l])
                pool.wait_ge(s_spare, 16 * SPARE)
                pool.wait_ge(*since(ro_done[l], 1))
                for s in range(2):
                    pool.wait_ge(*since(h2_st[l][s], 16 * (n // 2)))
                for s in range(2):
                    nc.gpsimd.tensor_copy(idxS[s][:, :], idxI[:, s:s + 1]).then_inc(mo_ix[l].sem, 1)
                    pool.wait_ge(*since(mo_ix[l], s + 1))
                    gather(xg[s], h2_dram[l], idxS[s][:, :], mo_xg[l][s])
                with pool.Fori(0, E // 2 - 1) as j:
                    for s in range(2):
                        e = 2 * j + s
                        pool.wait_ge(*since(mo_xT[l], e + 1))
                        nc.gpsimd.tensor_copy(idxS[s][:, :], idxI[:, bass.ds(e + 2, 1)]).then_inc(mo_ix[l].sem, 1)
                        wait_alone(pool, *since(mo_ix[l], e + 3))
                        gather(xg[s], h2_dram[l], idxS[s][:, :], mo_xg[l][s])
                for s in range(2):
                    pool.wait_ge(*since(mo_st[l][s], 16 + 16 * E))
                nx = pool.value_load(ownI[0:1, XBLK[l]:XBLK[l] + 1], min_val=0, max_val=XBLK[l])
                with pool.If(nx > 0):
                    with pool.Fori(0, nx) as b:
                        nc.gpsimd.tensor_copy(idxS[0][:, :], idxI[:, bass.ds(b + E, 1)]).then_inc(xt_ix[l].sem, 1)
                        wait_alone(pool, *since(xt_ix[l], b + 1))
                        gather(xg[0], h2_dram[l], idxS[0][:, :], xt_xg[l])
                        pool.wait_ge(*since(xt_y[l], b + 1))
                        store(pool, b + E, yS[0], xt_st[l])
                        pool.wait_ge(*since(xt_st[l], 32 * b + 32))
                with pool.Else():
                    pool.nop()
                for i in range(n):
                    if i >= 2:
                        pool.wait_ge(*since(cb_w[l], i - 1))
                    for k in range(2):
                        q = k * n + i
                        gather(yg[i % 2][:, k, :], y_flat, slotI[:, q:q + 1], cb_g[l][i % 2])



def kernel(**inputs):
    import concourse.bacc as bacc
    from concourse.bass_utils import run_bass_kernel_spmd

    def a(name):
        return np.ascontiguousarray(inputs[name])

    def chan(v, n):
        return v.reshape(-1, n, P).transpose(2, 0, 1).reshape(P, -1)

    def rows(v):
        return np.broadcast_to(v.reshape(1, -1), (P, v.size))

    def groups(w, cols, k=KC):
        l, _, n = w.shape
        return np.ascontiguousarray(w.reshape(l, k, P, n // cols, cols).transpose(0, 3, 2, 1, 4)).reshape(-1, P, k * cols)

    x = np.concatenate([a("ctx")[0], a("x")[0]], 0)
    xt = np.ascontiguousarray(x.reshape(T, KC, P).transpose(2, 1, 0)).reshape(P, KC * T)
    small = np.zeros((L, P, SMALL_W), np.float32)
    for l in range(L):
        parts = {
            "b_mod": chan(a("b_mod")[l], NMOD * KC), "g1": chan(a("g_norm1")[l], KC), "g2": chan(a("g_norm2")[l], KC),
            "g_diff": a("g_diff_subln")[l][:, None], "g_v": chan(a("g_gmlp_v")[l], WC),
            "w_conv": chan(a("w_conv_m")[l], WC), "b_conv": chan(a("b_conv_m")[l], WC),
            "g_ml": chan(a("g_mlstm_norm")[l], WC), "skip": chan(a("skip_m")[l], WC), "g_fin": chan(a("g_final"), KC),
            "c": np.stack([a("c_ctx"), a("c")[0]]).reshape(2, KC, P).transpose(2, 1, 0).reshape(P, -1),
            "w_if": a("w_if_m")[l].reshape(3 * WC, P, 16).transpose(1, 0, 2).reshape(P, -1),
            "w_route": np.concatenate([a("w_route_g")[l], a("w_route_e")[l]], 1)
                .reshape(KC, P, GROUPS + E).transpose(1, 0, 2).reshape(P, -1),
            "b_if": rows(a("b_if_m")[l]), "b_route": rows(np.concatenate([a("b_route_g")[l], a("b_route_e")[l]])),
            "w_sT": a("w_gmlp_s")[l].transpose(2, 0, 1).reshape(P, -1),
            "w_qkv": a("w_qkv_m")[l].transpose(2, 0, 1, 3).reshape(P, -1),
        }
        for k, v in parts.items():
            small[l, :, SMALL[k][0]:SMALL[k][1]] = v
    early = np.stack([np.concatenate([rows(a("b_gmlp_s")[l]), rows(a("diff_lambda")[l])], 1) for l in range(L)])
    w = a("w_in").reshape(L, KC, P, -1)
    win = np.stack([w[..., c:c + COLS] for _, c, _ in WIN], 1).transpose(0, 1, 3, 2, 4)
    arrays = {
        "xt": xt, "consts": constants(), "small": small, "early": early,
        "wmod": groups(a("w_mod"), COLS), "win": np.ascontiguousarray(win).reshape(L * len(WIN), P, RW),
        "wbr": groups(a("w_branch").reshape(L, 3 * W, D), P, 3 * WC), "wout": groups(a("w_out"), COLS),
        "w_gate": a("w_e_gate").reshape(L * E, D, FE), "w_up": a("w_e_up").reshape(L * E, D, FE),
        "w_down": a("w_e_down").reshape(L * E, FE, D),
    }
    nc = bacc.Bacc("TRN2", target_bir_lowering=False, num_devices=1)
    t = {k: nc.dram_tensor(f"{k}_dram", v.shape, F32, kind="ExternalInput").ap() for k, v in arrays.items()}
    out = nc.dram_tensor("out", (P, KC * LAT), F32, kind="ExternalOutput").ap()
    h2 = [nc.dram_tensor(f"h2_{l}", (n, D), F32, kind="Internal").ap() for l, n in enumerate((T, LAT))]
    y = nc.dram_tensor("y_rows", (NBLK[0] * BLK, D), F32, kind="Internal").ap()
    build(nc, *(t[k] for k in ("xt", "consts", "small", "early", "wmod", "win", "wbr", "wout", "w_gate", "w_up", "w_down")), out, h2, y)
    r = run_bass_kernel_spmd(nc, [{f"{k}_dram": v for k, v in arrays.items()}], core_ids=[0])
    got = r.results[0]["out"]
    return got.reshape(P, KC, LAT).transpose(2, 1, 0).reshape(1, LAT, D)
```

```python
import math
from collections import namedtuple
import numpy as np
import concourse.bass as bass
from concourse import mybir
from contextlib import ExitStack

F32 = mybir.dt.float32
I32 = mybir.dt.int32
ALU = mybir.AluOpType
ACT = mybir.ActivationFunctionType
AX = mybir.AxisListType.X

L, D, CTX, LAT = 2, 1024, 256, 256
T = CTX + LAT
GRID_W, ROPE_BASE, EPS = 64, 10000.0, 1e-6
H, DK, DV = 4, 64, 128
W = 512
CONV_K = 3
NMOD = 6
GROUPS, PER, E = 4, 8, 32
FE = 512
P = 128
KC = D // P
WC = W // P
NTILE = T // P
COLS = 256
RW = KC * COLS
MODG = NMOD * D // COLS
BRG = D // P
OUTG = D // COLS
SCALE = DK ** -0.5
MSCALE = DV ** -0.5
BIG = 1e30

Entry = namedtuple("Entry", "sem base")

BLK = 64
XBLK = [(T * 2) // (BLK + 1), (LAT * 2) // (BLK + 1)]
NBLK = [E + n for n in XBLK]
MISC_W = 1372
STEPS = T // BLK - 1


def offsets(parts):
    at, out = 0, {}
    for name, n in parts:
        out[name] = (at, at + n)
        at += n
    return out, at


SMALL, SMALL_W = offsets([
    ("b_mod", NMOD * KC), ("g1", KC), ("g2", KC), ("g_diff", 1), ("g_v", WC), ("w_conv", CONV_K * WC), ("b_conv", WC),
    ("g_ml", WC), ("skip", WC), ("g_fin", KC), ("c", KC * 2), ("w_if", 3 * WC * 16), ("w_route", KC * (GROUPS + E)),
    ("b_if", 16), ("b_route", GROUPS + E), ("w_sT", WC * P), ("w_qkv", 3 * WC * P)])
EARLY, EARLY_W = offsets([("b_s", WC * P), ("lam", 4 * DK)])
CONST, CONST_W = offsets([
    ("ident", P), ("ones", P), ("tri_f", P), ("tri_b", P), ("tri_x", P), ("mask_f", P), ("mask_b", P), ("rot", P),
    ("cos", LAT), ("sin", LAT), ("sel", 2), ("iota", BLK), ("thr", STEPS), ("tok", NTILE)])


def constants():
    t = np.zeros((P, CONST_W), np.float32)

    def put(name, a):
        t[:, CONST[name][0]:CONST[name][1]] = a
    i, j = np.arange(P)[:, None], np.arange(P)[None, :]
    put("ident", i == j)
    put("ones", 1.0)
    put("tri_f", i <= j)
    put("tri_b", i >= j)
    put("tri_x", i < j)
    put("mask_f", np.where(i <= j, 0.0, BIG))
    put("mask_b", np.where(i >= j, 0.0, BIG))
    half = (np.arange(P) // 16) % 2
    rot = np.zeros((P, P), np.float32)
    for p in range(P):
        if half[p] == 0:
            rot[p + 16, p] = -1.0
        else:
            rot[p - 16, p] = 1.0
    put("rot", rot)
    inv = (ROPE_BASE ** (-np.arange(0, 32, 2, dtype=np.float32) / 32)).astype(np.float32)
    tok = np.arange(LAT)
    pos = np.stack([tok // GRID_W, tok % GRID_W]).astype(np.float32)
    ang = pos[(np.arange(P) // 32) % 2] * inv[np.arange(P) % 16][:, None]
    put("cos", np.cos(ang.astype(np.float32)))
    put("sin", np.sin(ang.astype(np.float32)))
    put("sel", np.stack([(np.arange(P) % 32) == 0, (np.arange(P) % 32) == 1], 1))
    put("iota", np.arange(BLK)[None, :])
    put("thr", BLK * (1 + np.arange(STEPS))[None, :])
    put("tok", np.arange(P)[:, None] + P * np.arange(NTILE)[None, :])
    return t


WIN = [(k, c + COLS * g, g) for k, c, n in
       [("k", 0, 2), ("x", 1024, 2), ("v", 512, 2), ("q", 1536, 2), ("u", 2048, 2), ("bv", 2560, 2), ("z", 3072, 2),
        ("gate", 3584, 12)] for g in range(n)]
NGATE = 12
NDENSE = len(WIN) - NGATE
MOD_FIRST = 8
MOD_BEHIND = [sorted([(g, 1) for g in range(NDENSE + 8)] + [(4, 0), (6, 0)]), [(g, 1) for g in range(MODG - MOD_FIRST)]]
MOD_AT = [{place: MOD_FIRST + l * MODG + i for i, place in enumerate(MOD_BEHIND[l])} for l in range(2)]


def build(nc, xt_in, consts_in, small_in, early_in, wmod, win, wbr, wout, w_gate, w_up, w_down, out, h2_dram, y_dram):
    stack = ExitStack()
    with stack:
        def sb(name, cols, dt=F32, rows=P):
            return stack.enter_context(nc.sbuf_tensor(name, [rows, cols], dt))

        def sem(name):
            return stack.enter_context(nc.semaphore(name))

        def cut(buf, at, *dims):
            n = math.prod(dims)
            v = buf[:, at:at + n]
            if len(dims) == 1:
                return v
            names = "abc"[:len(dims)]
            return v.rearrange(f"p ({' '.join(names)}) -> p {' '.join(names)}", **dict(zip(names, dims)))

        xT = cut(sb("xT", KC * T), 0, KC, T)
        hT = cut(sb("hT", KC * T), 0, KC, T)
        slotA = sb("slotA", 3 * 4096)
        slotB = sb("slotB", 3 * 4096)
        ring = sb("ring", 2 * RW)
        mix = sb("mix", 5 * WC * T)
        small = sb("small", SMALL_W)
        consts = sb("consts", CONST_W)
        misc = sb("misc", MISC_W)

        def const(name, rows=P):
            return consts[0:rows, CONST[name][0]:CONST[name][1]]

        def par(name, *dims):
            if name in EARLY:
                return cut(slotA, 9344 + EARLY[name][0], *dims)
            a, _ = SMALL[name]
            return cut(small, a, *dims) if dims else small[:, a:a + 1]

        ident = const("ident")
        ones = const("ones")
        xm = cut(mix, 0, WC, T)
        xc = cut(mix, 1 * WC * T, WC, T)
        uT = cut(mix, 2 * WC * T, WC, T)
        vG = cut(mix, 3 * WC * T, NTILE, W)
        yaT = cut(mix, 3 * WC * T, WC, T)
        zT = cut(mix, 4 * WC * T, WC, T)
        gates = cut(slotB, 0, 3 * KC, T)
        qT = cut(slotA, 0, WC, T)
        kT = cut(slotA, 2048, WC, T)
        vA = cut(slotA, 4096, NTILE, W)
        probs = cut(slotA, 6144, 2, T)
        attT = cut(slotA, 7168, NTILE, P)
        attw = cut(slotA, 7680, T)
        osq = cut(slotA, 8192, P)
        rope_c = cut(slotA, 6144, LAT)
        rope_s = cut(slotA, 6144 + LAT, LAT)
        oraw = cut(slotA, 8320, H, P)
        oN = cut(slotA, 8832, H, P)
        mring = slotA[:, 10240:10240 + RW]
        mq = cut(slotA, 6144, WC, 256)
        mk = cut(slotA, 7168, WC, 256)
        mv = cut(slotA, 8192, WC, 256)
        mkt = cut(slotA, 9216, 2, WC, P)
        mvt = cut(slotA, 10240, 2, WC, P)
        hsum = cut(slotA, 11264, 2, WC, P)
        sg = [cut(slotA, 512 * i, WC, P) for i in range(2)]
        vw = [cut(slotA, 1024 + 512 * i, WC, P) for i in range(2)]
        num = cut(slotA, 2048, WC, P)
        inter = cut(slotA, 2560, WC, P)
        state = cut(slotA, 3072, 2, WC, P)
        hsq = cut(slotA, 4096, WC, P)
        hn = cut(slotA, 4608, 2, WC, P)
        xs = cut(slotA, 0, WC, 256)
        yt = cut(slotA, 1024, WC, 256)
        nbuf1 = slotB
        first_mods = [cut(slotA, i * RW, KC, COLS) for i in range(4)] + [cut(slotB, 4096 + i * RW, KC, COLS) for i in range(4)]
        nbuf2 = mix
        xg = [mix[0:BLK, i * D:(i + 1) * D] for i in range(2)]
        xgT = [cut(mix, 2048 + 512 * i, KC, BLK) for i in range(2)]
        gs = [mix[:, 3072 + 512 * i:3584 + 512 * i] for i in range(2)]
        act_ = [mix[:, 4096 + 512 * i:4608 + 512 * i] for i in range(2)]
        aT = [cut(mix, 5120 + 256 * i, 4, BLK) for i in range(2)]
        yS = [mix[:, 5632 + 512 * i:6144 + 512 * i] for i in range(2)]
        h2row = [mix[:, 6656 + D * i:6656 + D * (i + 1)] for i in range(2)]
        rt = mix[:, 8704:10240]
        yg = [cut(mix, 2 * D * i, 2, D) for i in range(2)]
        fw = [mix[:, 4096 + D * i:4096 + D * (i + 1)] for i in range(2)]

        at = [0]

        def small_tile(*dims):
            v = cut(misc, at[0], *dims)
            at[0] += math.prod(dims)
            assert at[0] <= MISC_W
            return v
        csil = small_tile(KC, 32)
        mraw = [small_tile(COLS) for _ in range(2)]
        modT = small_tile(L, NMOD * KC, 2)
        normA = small_tile(KC, 2)
        gate2 = small_tile(KC, 2)
        lamv = small_tile(4)
        gvec = small_tile(4 * WC)
        ssq = small_tile(NTILE)
        rst = small_tile(NTILE)
        nmax = small_tile(2)
        nbias = small_tile(2)
        psum_ = small_tile(2)
        prec = small_tile(2)
        oss = small_tile(H)
        orms = small_tile(H)
        mgate = small_tile(2, 16)
        mlf = small_tile(2, 2, H)
        mtmp = small_tile(2, 2, H)
        mb = small_tile(2, 2, H)
        mg = small_tile(2, 2, H)
        mr = small_tile(2, 2, H)
        mMt = small_tile(2, 2, H)
        mst = small_tile(2, H)
        mend = small_tile(H)
        mmax = small_tile(H)
        mex = small_tile(4, H)
        mee = [small_tile(4, H) for _ in range(2)]
        nst = small_tile(2, H)
        mden = small_tile(H)
        mden2 = small_tile(H)
        hss = small_tile(2, H)
        PAD = P // 2
        cmax = [slotA[0:8, a:a + 2 * (P + PAD)].rearrange("p (d t) -> p d t", d=2) for a in (4096, 5632)]

        def cm_at(b, d, shift=0):
            a = (PAD - shift) if d == 0 else shift
            return cmax[b][:, d, a:a + P]
        ints = sb("ints", NBLK[0] + 2 * NTILE, I32)
        idxI = ints[0:BLK, 0:NBLK[0]]
        slotI = ints[:, NBLK[0]:]
        idxS = [sb(f"idxS{i}", 1, I32, BLK) for i in range(2)]
        ownI = sb("ownI", XBLK[0] + 1, I32, 1)
        misc_wt = small_tile(2 * NTILE)

        psum = stack.enter_context(nc.psum_tensor("psum", [P, 8 * 512], F32))
        bank = [psum[:, 512 * i:512 * i + 512] for i in range(8)]
        pmod = bank[3]


        BRB = ((4, 5, 6), (0, 1, 7))
        mrg = [mix[:, 512 * b:512 * b + 512] for b in range(3)]
        fin = mix[:, 4096:4096 + KC * LAT]
        y_flat = y_dram
        y_dram = y_dram.rearrange("(b r) n -> b r n", r=BLK)
        ro, used_cols = {}, [0]

        def ro_tile(name, *dims):
            sizes = [[d(l) if callable(d) else d for d in dims] for l in range(L)]
            ro[name] = [cut(rt, used_cols[0], *sizes[l]) for l in range(L)]
            used_cols[0] += max(math.prod(s) for s in sizes)
            assert used_cols[0] <= 1536

        def nt(l):
            return (NTILE, LAT // P)[l]
        for name, *dims in (
                ("lg", nt, GROUPS), ("ge", nt, GROUPS), ("goh", nt, GROUPS), ("gm", nt), ("gi", nt), ("pg", nt), ("t1", nt),
                ("le", nt, E), ("oh1", nt, E), ("oh2", nt, E), ("m", nt, E), ("cand", nt, E), ("m1", nt), ("m2", nt),
                ("idx", 2, nt), ("e2", nt), ("rank", 2, nt), ("ob", 2, nt), ("fl", 2, nt), ("jj", 2, nt), ("bb", 2, nt),
                ("fc", lambda l: 2 * nt(l), STEPS), ("oe", 2, E), ("cmp", STEPS), ("cnt", 1), ("obl", 1)):
            ro_tile(name, *dims)
        for name in ("cmp", "cnt", "obl"):
            ro[name] = [v[0:E] for v in ro[name]]
        ro["own"] = [rt[0:1, 1100:1100 + XBLK[l]] for l in range(L)]
        ro["wt"] = [cut(misc_wt, 0, 2, nt(l)) for l in range(L)]
        ro["cand"] = [cut(rt, 1200, NTILE * E)] * L
        ro["J"] = [cut(mix, 4096, 2 * nt(l), BLK) for l in range(L)]
        ro["BT"] = [cut(mix, 4608, 2 * nt(l), NBLK[l]) for l in range(L)]
        ro["owc"] = [mix[0:1, 5120:5120 + XBLK[l] * E].rearrange("p (a e) -> p a e", e=E) for l in range(L)]

        SPARE = 5
        NU = NTILE * H
        NF = 10
        ML_FILL = (0, 1, 3)
        NFA = 6
        MUN = [(0, 0), (1, 1), (0, 1), (1, 0)]

        def counted(name, n):
            s = sem(name)
            return [Entry(s, n * l) for l in range(L)]

        def apart(name):
            return [Entry(sem(f"{name}_{l}"), 0) for l in range(L)]

        def by_buffer(name, n):
            both = [counted(f"{name}{i}", n) for i in range(2)]
            return [[both[i][l] for i in range(2)] for l in range(L)]

        def since(entry, value):
            return entry.sem, value + entry.base

        s_const = sem("const_loaded")
        s_x = sem("x_loaded")
        s_zero = sem("padding_zeroed")
        s_c = sem("silu_c")
        mod_mm = sem("mod_parts")
        mod_ev = sem("mod_parts_copied")
        mod_t = sem("mod_transposed")
        mod_out = sem("mod_stored")
        act_step = sem("act_step")
        dve_step = sem("dve_step")
        pool_step = sem("pool_step")
        dense_full = sem("dense_chunk_ready")
        dense_out = sem("dense_chunk_copied")
        f_sq = sem("fin_squares")
        f_mm = sem("fin_summed")
        f_out = sem("fin_out")
        s_out = sem("out_stored")
        s_passed = sem("waits_passed")
        s_spare = sem("spare_rows_filled")
        s_head = sem("small_head_loaded")
        first_full = [sem(f"first_mods_full{i}") for i in range(MOD_FIRST // 2)]
        mod_full = sem("mod_group_full")
        ring_full = [sem(f"ring_full{i}") for i in range(2)]
        e_full = [sem(f"expert_full{i}") for i in range(2)]
        rms_in, rms_out = sem("mean_squares"), sem("inverse_roots")
        s_small, s_early = apart("small_loaded"), apart("early_loaded")
        n1_sq = counted("n1_squares", KC)
        n1_mm = counted("n1_summed", KC)
        n1_nt = counted("n1_scaled", KC)
        h_ready = counted("h_ready", KC)
        n1_f = counted("n1_factors", 1)
        rope_mm = counted("rope_mm", 2 * WC)
        kq_done = counted("kq_roped", 2 * WC)
        conv_done = counted("conv_summed", 1)
        xc_done = counted("xconv_ready", 1)
        bv_sq = counted("bv_squares", NTILE)
        bv_done = counted("bv_normed", NTILE)
        mixg_mm = counted("gmlp_mixed", WC)
        yb_done = counted("yb_ready", WC)
        lam_in = counted("lam_sums", 1)
        lam_ex = counted("lam_exps", 1)
        at_s = counted("att_scores", NU)
        at_nb = counted("att_bias", NU)
        at_exp = counted("att_exp", 2 * NU)
        at_a = counted("att_weights", NU)
        at_T = counted("att_T", NU)
        at_aT = counted("att_T_copied", NU)
        at_o = counted("att_out", NU)
        at_sq = counted("att_squares", NU)
        at_on = counted("att_kept", NU)
        at_oT = counted("att_oT", NTILE)
        at_nd = counted("att_normed", NTILE)
        at_y = counted("att_y", NTILE)
        ml_ff = counted("ml_features", 2 * NF)
        ml_fe = counted("ml_features_copied", 2 * (NF - NFA))
        ml_fa = counted("ml_features_copied_act", 2 * NFA)
        ml_gm = counted("ml_gates", 2)
        ml_ga = counted("ml_abs", 2)
        ml_gl = counted("ml_ln", 2)
        ml_lf = counted("ml_logf", 2)
        ml_cs = counted("ml_cumsum", 2)
        ml_r = counted("ml_r", 2)
        ml_rT = counted("ml_rT", 2)
        ml_cm = counted("ml_cummax", 2)
        ml_mt = counted("ml_cummax_T", 2)
        ml_bc = counted("ml_bcast", 2 * len(MUN))
        ml_ei = counted("ml_exponents", 2 * len(MUN))
        ml_nd = counted("ml_neg_d", 2 * len(MUN))
        ml_ex = counted("ml_exps", 2 * len(MUN))
        ml_d = counted("ml_dmat", 2 * len(MUN))
        ml_qk = counted("ml_qk", 2 * len(MUN))
        ml_sg = counted("ml_sg", 2 * len(MUN))
        ml_num = counted("ml_num", 2 * len(MUN))
        ml_int = counted("ml_inter", 2 * len(MUN))
        ml_hr = counted("ml_h", 2 * len(MUN))
        ml_upd = counted("ml_update", 2 * len(MUN))
        ml_st = counted("ml_state", 2 * len(MUN))
        ml_vw = counted("ml_vw", 2 * len(MUN))
        ml_hn = counted("ml_hn", 2)
        ml_hT = counted("ml_hT", 2)
        ml_y = counted("ml_y", 2)
        br_mm = counted("branches_mm", BRG)
        br_step = counted("merge_step", 2 * BRG)
        br_done = counted("merged", BRG + 2)
        wo_mm = counted("out_mm", KC)
        res1 = counted("residual1", KC)
        n2_sq = counted("n2_squares", KC)
        n2_mm = counted("n2_summed", KC)
        n2_nt = counted("n2_scaled", KC)
        h2_ready = counted("h2_ready", KC)
        ro_mm = counted("ro_logits", 1)
        ro_in = counted("ro_biased", 1)
        ro_ei = counted("ro_exp_in", 2)
        ro_ex = counted("ro_exp", 2)
        ro_m = counted("ro_onehots", 1)
        ro_cnt = counted("ro_counts", 1)
        ro_obl = counted("ro_extra", 1)
        ro_ob = counted("ro_bases", 1)
        ro_jb = counted("ro_onehot_jb", 1)
        ro_ix = counted("ro_index_mm", 1)
        ro_done = counted("ro_done", 1)
        h2_T = counted("h2_transposed", NTILE)
        h2_row = counted("h2_row", NTILE)
        mo_ix = counted("mo_index", E)
        mo_xT = counted("mo_xT", E)
        mo_xc = counted("mo_xT_copied", E)
        mo_gu = counted("mo_gate_up", E)
        mo_s = counted("mo_silu", E)
        mo_a = counted("mo_act", E)
        mo_aT = counted("mo_actT", E)
        mo_ac = counted("mo_actT_copied", E)
        mo_d = counted("mo_down", E)
        mo_y = counted("mo_y", E)
        xt_w = apart("xt_weights")
        xt_ix = apart("xt_index")
        xt_xg = apart("xt_x")
        xt_mm = apart("xt_products")
        xt_act = apart("xt_copies")
        xt_a = apart("xt_act")
        xt_y = apart("xt_y")
        xt_st = apart("xt_stored")
        cb_w = counted("cb_weighted", NTILE)
        cb_T = counted("cb_transposed", NTILE)
        cb_r = counted("residual2", NTILE)
        h2_st = by_buffer("h2_stored", 16 * (NTILE // 2))
        mo_xg = by_buffer("mo_x", 16 * (E // 2))
        mo_st = by_buffer("mo_stored", 16 + 32 * (E // 2))
        cb_g = by_buffer("cb_gathered", 32 * (NTILE // 2))

        T0 = [0, CTX]
        NT = [T, LAT]
        TILES = [list(range(T0[l] // P, NTILE)) for l in range(L)]
        UNITS = [[(h, t) for t in TILES[l] for h in range(H)] for l in range(L)]

        def with_h(l, seg):
            return not (l == 1 and seg == 0)

        base_in = [0, 0]
        base_br = [len(WIN), 0]
        base_in[1] = base_br[0] + BRG + OUTG
        base_br[1] = base_in[1] + len(WIN)

        def rslot(s):
            return ring[:, s * RW:(s + 1) * RW]

        def chunk_no(l, g, c=1):
            return 2 * (l * len(WIN) + g) + c + 1

        def first_group(what):
            return next(g for g, (k, _, _) in enumerate(WIN) if k == what)

        def used(n):
            for l in range(L):
                if base_in[l] <= n < base_in[l] + len(WIN):
                    return dense_full, chunk_no(l, n - base_in[l])
                if base_br[l] <= n < base_br[l] + BRG:
                    return since(br_mm[l], n - base_br[l] + 1)
                if base_br[l] + BRG <= n < base_br[l] + BRG + OUTG:
                    return since(wo_mm[l], 2 * (n - base_br[l] - BRG + 1))

        def fillers(l, u):
            n = 16 // len(UNITS[l])
            return range(u * n, (u + 1) * n)

        def store(eng, blk, buf, s_):
            dst = y_dram[bass.ds(blk, 1), :, :].rearrange("a p (h n) -> (a p) h n", h=2)
            for h in range(2):
                eng.dma_start(dst[:, h, :], buf[64 * h:64 * h + 64, :]).then_inc(s_.sem, 16)

        def wait_alone(eng, s, value):
            eng.wait_ge(s, value)
            eng.sem_inc(s_passed, 1)

        pmods = (bank[3], bank[2])

        block = stack.enter_context(nc.Block())

        @block.sync
        def _(sp):
            def load(n, src):
                if n >= 2:
                    sp.wait_ge(*used(n - 2))
                sp.dma_start(rslot(n % 2)[:, 0:src.shape[1]], src).then_inc(ring_full[n % 2], 16)

            def row(src, i):
                return src[bass.ds(i, 1), :, :].rearrange("a p n -> (a p) n")

            def expert(l, s, e, full):
                for w, i, n in ((w_gate, 0, FE), (w_up, 1, FE), (w_down, 2, D)):
                    src = w[bass.ds(l * E + e, 1), :, :].rearrange("a (k p) f -> p (a k) f", p=P)
                    sp.dma_start(cut((slotA, slotB)[s], 4096 * i, 4096 // n, n), src).then_inc(full, 16)

            early = slotA[:, 9344:9344 + EARLY_W]
            n = SMALL["c"][1]
            sp.dma_start(small[:, 0:n], small_in[0][:, 0:n]).then_inc(s_head, 16)
            sp.dma_start(consts[:, :], consts_in).then_inc(s_const, 16)
            sp.dma_start(xT.rearrange("p c t -> p (c t)"), xt_in).then_inc(s_x, 16)
            for i in range(MOD_FIRST // 2):
                o = (slotA, slotB)[i // 2][:, (0, 4096)[i // 2] + 2 * RW * (i % 2):][:, 0:2 * RW]
                sp.dma_start(o.rearrange("p (g n) -> p g n", g=2), wmod[2 * i:2 * i + 2].rearrange("g p n -> p g n")).then_inc(first_full[i], 16)
            sp.dma_start(small[:, n:], small_in[0][:, n:]).then_inc(s_small[0].sem, 16)
            for l in range(L):
                for g in range(len(WIN)):
                    load(base_in[l] + g, win[l * len(WIN) + g])
                    for c in range(2):
                        if (g, c) in MOD_AT[l]:
                            m = MOD_AT[l][g, c]
                            sp.wait_ge(mod_mm, m)
                            sp.dma_start(mring, wmod[m]).then_inc(mod_full, 16)
                    if (l, g) == (0, 1):
                        sp.dma_start(early, early_in[0]).then_inc(s_early[0].sem, 16)
                for s in range(2):
                    load(base_br[l] + s, wbr[l * BRG + s])
                sp.wait_ge(*since(ml_y[l], 2 - l))
                expert(l, 0, 0, e_full[0])
                with sp.Fori(1, BRG // 2) as j:
                    for s in range(2):
                        wait_alone(sp, *since(br_mm[l], 2 * j + (s - 1)))
                        w = row(wbr, 2 * j + (l * BRG + s))
                        sp.dma_start(rslot(s)[:, 0:w.shape[1]], w).then_inc(ring_full[s], 16)
                for s in range(2):
                    load(base_br[l] + BRG + s, wout[l * OUTG + s])
                sp.wait_ge(*since(br_done[l], BRG + 2))
                expert(l, 1, 1, e_full[1])
                for s in range(2, OUTG):
                    load(base_br[l] + BRG + s, wout[l * OUTG + s])
                for s in range(2):
                    sp.sem_inc(mo_st[l][s].sem, 16)
                with sp.Fori(1, E // 2) as j:
                    for s in range(2):
                        wait_alone(sp, *since(mo_d[l], 2 * j + (s - 1)))
                        expert(l, s, 2 * j + s, e_full[s])
                        wait_alone(sp, *since(mo_y[l], 2 * j + (s - 1)))
                        store(sp, 2 * j + (s - 2), yS[s], mo_st[l][s])
                for s in range(2):
                    sp.wait_ge(*since(mo_y[l], E - 1 + s))
                    store(sp, E - 2 + s, yS[s], mo_st[l][s])
                if l == 0:
                    sp.wait_ge(*since(ro_in[l], 1))
                    sp.dma_start(small[:, :], small_in[1]).then_inc(s_small[1].sem, 16)
                sp.wait_ge(*since(ro_done[l], 1))
                sp.wait_ge(*since(mo_d[l], E))
                n = sp.value_load(ownI[0:1, XBLK[l]:XBLK[l] + 1], min_val=0, max_val=XBLK[l])
                with sp.If(n > 0):
                    with sp.Fori(0, n) as b:
                        e = sp.value_load(ownI[0:1, bass.ds(b, 1)], min_val=0, max_val=E - 1)
                        expert(l, 0, e, xt_w[l].sem)
                        wait_alone(sp, *since(xt_mm[l], 4 * b + 4))
                with sp.Else():
                    sp.nop()
                if l == 0:
                    sp.dma_start(early, early_in[1]).then_inc(s_early[1].sem, 16)
            for c in range(2):
                sp.wait_ge(f_out, KC // 2 * (c + 1))
                n = KC // 2 * LAT
                sp.dma_start(out[:, c * n:(c + 1) * n], fin[:, c * n:(c + 1) * n]).then_inc(s_out, 16)
            sp.wait_ge(s_out, 32)

        @block.tensor
        def _(pe):
            dense = [0]
            unturned = []

            def mm(o, a, b, start=True, stop=True):
                return nc.tensor.matmul(o, a, b, start=start, stop=stop)

            def tr(o, a, p0=0):
                return nc.tensor.transpose(o, a, ident[p0:p0 + a.shape[0], p0:p0 + a.shape[0]])

            def mod_parts(w, pmod):
                for k2 in range(2):
                    for j in range(4):
                        last = mm(pmod[32 * j:32 * j + 32, 0:COLS], csil[:, 2 * j + k2, :], w[:, 2 * j + k2, :],
                                  start=k2 == 0, stop=k2 == 1)
                last.then_inc(mod_mm, 1)

            def mod_turn(m):
                pmod = pmods[m % 2 if m < MOD_FIRST else 0]
                for c in range(2):
                    last = mm(pmod[:, COLS + 2 * c:COLS + 2 * c + 2], mraw[m % 2][:, P * c:P * c + P], const("sel"))
                last.then_inc(mod_t, 1)

            def mod_turn_pending():
                if unturned:
                    m = unturned.pop()
                    pe.wait_ge(mod_ev, m + 1)
                    mod_turn(m)

            def dense_chunk(l, g, c):
                what, _, _ = WIN[g]
                pos = base_in[l] + g
                w = cut(rslot(pos % 2), 0, KC, COLS)
                t0 = 0 if what in "kxv" else T0[l]
                if c == 0:
                    pe.wait_ge(ring_full[pos % 2], 16 * (pos // 2 + 1))
                d = dense[0]
                dense[0] += 1
                if d >= 2:
                    pe.wait_ge(dense_out, d - 1)
                b = bank[d % 2]
                if what in ("v", "bv"):
                    tiles = list(range(t0 // P, NTILE))
                    n = len(tiles) // 2
                    for i, t in enumerate(tiles[n * c:n * c + n]):
                        for k in range(KC):
                            last = mm(b[:, COLS * i:COLS * (i + 1)], hT[:, k, P * t:P * t + P], w[:, k, :],
                                      start=k == 0, stop=k == KC - 1)
                else:
                    for k in range(KC):
                        if g == c == 0:
                            pe.wait_ge(*since(h_ready[l], k + 1))
                        last = mm(b[:, 0:T - t0], w[:, k, P * c:P * c + P], hT[:, k, t0:T], start=k == 0, stop=k == KC - 1)
                last.then_inc(dense_full, 1)
                mod_turn_pending()
                if (g, c) in MOD_AT[l]:
                    m = MOD_AT[l][g, c]
                    pe.wait_ge(mod_full, 16 * (m - MOD_FIRST + 1))
                    pe.wait_ge(mod_out, m)
                    mod_parts(cut(mring, 0, KC, COLS), pmod)
                    unturned.append(m)

            def rope(l, i):
                pe.wait_ge(dense_out, chunk_no(l, first_group("k" if i < WC else "q") + i % WC // 2, i % 2))
                if i >= 2:
                    pe.wait_ge(*since(kq_done[l], i - 1))
                elif l > 0:
                    pe.wait_ge(*since(h_ready[l], KC))
                mm(bank[4 + i % 2][:, 0:LAT], const("rot"), (kT if i < WC else qT)[:, i % WC, CTX:T]).then_inc(rope_mm[l].sem, 1)

            def norm(buf, n, squares, done):
                for c in range(KC):
                    pe.wait_ge(*since(squares, c + 1))
                    mm(bank[7][:, 0:n], ones, cut(buf, 512 * (c % 2), n), start=c == 0, stop=c == KC - 1).then_inc(done.sem, 1)

            def gmlp(l):
                pe.wait_ge(*since(s_small[l], 16))
                pe.wait_ge(*since(bv_done[l], len(TILES[l])))
                pe.wait_ge(*since(kq_done[l], 2 * WC))
                ws = par("w_sT", WC, P)
                for g in range(WC):
                    if g >= 2:
                        pe.wait_ge(*since(yb_done[l], g - 1))
                    for i, t in enumerate(TILES[l]):
                        last = mm(bank[4 + g % 2][:, P * i:P * i + P], vG[:, t, P * g:P * g + P], ws[:, g, :])
                    last.then_inc(mixg_mm[l].sem, 1)

            def att_scores(l, u):
                h, t = UNITS[l][u]
                keys = CTX if t < 2 else T
                if u == 0:
                    pe.wait_ge(*since(yb_done[l], WC))
                    pe.wait_ge(*since(kq_done[l], 2 * WC))
                else:
                    pe.wait_ge(*since(at_exp[l], 2 * u))
                for m in range(2):
                    r = slice(64 * m, 64 * m + 64)
                    last = mm(bank[4 + m][:, 0:keys], qT[r, h, P * t:P * t + P], kT[r, h, 0:keys])
                last.then_inc(at_s[l].sem, 1)

            def att_trans(l, u):
                h, t = UNITS[l][u]
                pe.wait_ge(*since(at_a[l], u + 1))
                if u >= 1:
                    pe.wait_ge(*since(at_aT[l], u))
                for i in range(2 if t < 2 else NTILE):
                    last = tr(bank[6][:, P * i:P * i + P], attw[:, P * i:P * i + P])
                last.then_inc(at_T[l].sem, 1)

            def att_out(l, u):
                h, t = UNITS[l][u]
                n = 2 if t < 2 else NTILE
                pe.wait_ge(*since(at_aT[l], u + 1))
                if u >= 1:
                    pe.wait_ge(*since(at_on[l], u))
                for i in range(n):
                    last = mm(bank[7][:, 0:P], attT[:, i, :], vA[:, i, P * h:P * h + P], start=i == 0, stop=i == n - 1)
                last.then_inc(at_o[l].sem, 1)

            def att_oT(l, i):
                pe.wait_ge(*since(at_nd[l], i + 1))
                if i >= 1:
                    pe.wait_ge(*since(at_y[l], i))
                for h in range(H):
                    last = tr(bank[2][:, P * h:P * h + P], oN[:, h, :])
                last.then_inc(at_oT[l].sem, 1)

            def ml_features(l, seg):
                wq = par("w_qkv", 3 * WC, P)
                sl = slice(256 * seg, 256 * seg + 256)
                jobs = [(s, src, h) for s, src in ((0, xc), (1, xc), (2, xm)) for h in (0, 2)]
                jobs += [(s, src, -1 - i) for i in range(2) for s, src in ((1, xc), (2, xm))]
                if seg == 0:
                    pe.wait_ge(*since(at_exp[l], 2 * len(UNITS[l])))
                    pe.wait_ge(*since(at_aT[l], len(UNITS[l])))
                    pe.wait_ge(*since(at_on[l], len(UNITS[l])))
                    pe.wait_ge(*since(xc_done[l], 1))
                else:
                    pe.wait_ge(*since(ml_st[l], 4))
                for i, (s, src, h) in enumerate(jobs):
                    if i >= 4:
                        if i - 4 < NFA:
                            pe.wait_ge(*since(ml_fa[l], seg * NFA + i - 3))
                        else:
                            pe.wait_ge(*since(ml_fe[l], seg * (NF - NFA) + i - 3 - NFA))
                    b = bank[4 + i % 4]
                    for k in range(2 if h >= 0 else WC):
                        if h >= 0:
                            last = mm(b[:, 256 * k:256 * k + 256], wq[:, s * WC + h + k, :], src[:, h + k, sl])
                        else:
                            t = 256 * seg + P * (-1 - h)
                            last = mm(b[:, P * k:P * k + P], src[:, k, t:t + P], wq[:, s * WC + k, :])
                    last.then_inc(ml_ff[l].sem, 1)

            def ml_gates(l, seg):
                wif = par("w_if", 3 * WC, 16)
                pe.wait_ge(*since(ml_fa[l], NFA * (seg + 1)))
                if seg == 0:
                    pe.wait_ge(*since(at_y[l], len(TILES[l])))
                for t in range(2):
                    for i, f in enumerate((mq, mk, mv)):
                        for h in range(WC):
                            last = mm(bank[2][:, 16 * t:16 * t + 16], f[:, h, P * t:P * t + P], wif[:, WC * i + h, :],
                                      start=(i, h) == (0, 0), stop=(i, h) == (2, WC - 1))
                last.then_inc(ml_gm[l].sem, 1)

            def ml_cumulate(l, seg):
                pe.wait_ge(*since(ml_lf[l], seg + 1))
                for d, tri in enumerate(("tri_f", "tri_b")):
                    mm(bank[2][:, 32 + 8 * d:40 + 8 * d], const(tri), mlf[:, :, d, :])
                mm(bank[2][:, 48:64], ones, mlf.rearrange("p a b c -> p (a b c)")).then_inc(ml_cs[l].sem, 1)
                pe.wait_ge(*since(ml_r[l], seg + 1))
                for d in range(2):
                    last = tr(bank[2][0:8, P * (d + 1):P * (d + 2)], mr[:, d, :, :].rearrange("p a b -> p (a b)"))
                last.then_inc(ml_rT[l].sem, 1)

            def ml_max_turn(l, seg):
                pe.wait_ge(*since(ml_cm[l], seg + 1))
                for d in range(2):
                    last = tr(bank[2][:, 64 + 8 * d:72 + 8 * d], cm_at(1, d))
                last.then_inc(ml_mt[l].sem, 1)

            def ml_open(l, seg, w):
                d, t = MUN[w]
                n, nh = 4 * seg + w, 4 * (seg - l) + w
                if w == 0:
                    pe.wait_ge(*since(ml_fe[l], (NF - NFA) * (seg + 1)))
                    pe.wait_ge(*since(ml_cm[l], seg + 1))
                elif with_h(l, seg):
                    pe.wait_ge(*since(ml_nd[l], nh))
                else:
                    pe.wait_ge(*since(ml_ei[l], n))
                for h in range(H):
                    r = t * H + h
                    last = mm(bank[4][:, P * h:P * h + P], ident[0:8, r:r + 1].to_broadcast([8, P]), cm_at(1, d))
                last.then_inc(ml_bc[l].sem, 1)
                if with_h(l, seg):
                    if w > 0:
                        pe.wait_ge(*since(ml_sg[l], nh))
                    for h in range(H):
                        last = mm(bank[5][:, P * h:P * h + P], mk[:, h, P * t:P * t + P], mq[:, h, P * t:P * t + P])
                    last.then_inc(ml_qk[l].sem, 1)

            def ml_unit(l, seg, w):
                d, t = MUN[w]
                n, nh = 4 * seg + w, 4 * (seg - l) + w
                s = sg[w % 2]
                if n >= 1:
                    pe.wait_ge(*since(ml_st[l], n))
                else:
                    pe.wait_ge(mod_out, MOD_FIRST + sum(len(MOD_AT[i]) for i in range(l + 1)))
                if with_h(l, seg):
                    pe.wait_ge(*since(ml_sg[l], nh + 1))
                    for h in range(H):
                        mm(bank[6][:, P * h:P * h + P], s[:, h, :], mvt[:, t, h, :])
                        mm(bank[2][:, 80 + h:81 + h], s[:, h, :], ones[:, 0:1])
                    for h in range(H):
                        mm(bank[7][:, P * h:P * h + P], mq[:, h, P * t:P * t + P], state[:, d, h, :])
                        last = mm(bank[2][:, 84 + h:85 + h], mq[:, h, P * t:P * t + P], nst[:, d, h:h + 1])
                    last.then_inc(ml_num[l].sem, 1)
                pe.wait_ge(*since(ml_vw[l], n + 1))
                for h in range(H):
                    mm(bank[3][:, P * h:P * h + P], mkt[:, t, h, :], vw[w % 2][:, h, :])
                    last = mm(bank[2][:, 88 + h:89 + h], mkt[:, t, h, :], mee[w % 2][:, 1, h:h + 1])
                last.then_inc(ml_upd[l].sem, 1)

            def ml_turn(l, seg):
                pe.wait_ge(*since(ml_hn[l], seg - l + 1))
                for t in range(2):
                    for h in range(H):
                        last = tr(bank[2 + t][:, P * h:P * h + P], hn[:, t, h, :])
                last.then_inc(ml_hT[l].sem, 1)

            def route(l):
                wr = par("w_route", KC, GROUPS + E)
                pe.wait_ge(*since(h2_ready[l], KC))
                nr = GROUPS + E
                for i, t in enumerate(TILES[l]):
                    for k in range(KC):
                        last = mm(bank[0][:, nr * i:nr * i + nr], hT[:, k, P * t:P * t + P], wr[:, k, :],
                                  start=k == 0, stop=k == KC - 1)
                last.then_inc(ro_mm[l].sem, 1)

            def h2_rows(l):
                for i, t in enumerate(TILES[l]):
                    if i >= 2:
                        pe.wait_ge(*since(h2_row[l], i - 1))
                    for k in range(KC):
                        last = tr(psum[:, 512 * (4 + 2 * (i % 2)) + P * k:512 * (4 + 2 * (i % 2)) + P * (k + 1)],
                                  hT[:, k, P * t:P * t + P])
                    last.then_inc(h2_T[l].sem, 1)

            def positions(l):
                n = len(TILES[l])
                m = ro["m"][l]
                pe.wait_ge(*since(ro_m[l], 1))
                for i in range(n):
                    for k in range(i):
                        mm(bank[1][:, E * i:E * i + E], ones, m[:, k, :], start=k == 0, stop=False)
                    mm(bank[1][:, E * i:E * i + E], const("tri_x"), m[:, i, :], start=i == 0, stop=True)
                for i in range(n):
                    last = mm(bank[1][0:E, 256:257], m[:, i, :], ones[:, 0:1], start=i == 0, stop=i == n - 1)
                last.then_inc(ro_cnt[l].sem, 1)
                pe.wait_ge(*since(ro_obl[l], 1))
                o = ro["obl"][l].to_broadcast([E, P])
                mm(bank[2][:, 0:E], o, const("tri_x", E)[:, 0:E])
                mm(bank[2][:, E:2 * E], o, const("tri_f", E)[:, 0:E]).then_inc(ro_ob[l].sem, 1)
                pe.wait_ge(*since(ro_jb[l], 1))
                for i in range(2 * n):
                    last = mm(bank[3][0:BLK, 0:NBLK[l]], ro["J"][l][:, i, :], ro["BT"][l][:, i, :],
                              start=i == 0, stop=i == 2 * n - 1)
                last.then_inc(ro_ix[l].sem, 1)

            def moe_block(s, wA, wait, sems):
                xT_, gu_, aT_, d_ = sems
                g, u = cut(wA, 0, KC, FE), cut(wA, 4096, KC, FE)
                dn = cut(wA, 8192, FE // P, D)
                wait("x")
                for k in range(KC):
                    last = tr(bank[0][:, BLK * k:BLK * k + BLK], xg[s][:, P * k:P * k + P])
                last.then_inc(xT_.sem, 1)
                wait("w")
                wait("xc")
                for k in range(KC):
                    for half, w in ((0, g), (1, u)):
                        last = mm(bank[1][64 * half:64 * half + 64, :], xgT[s][:, k, :], w[:, k, :],
                                  start=k == 0, stop=k == KC - 1)
                last.then_inc(gu_.sem, 1)
                wait("a")
                for k in range(FE // P):
                    last = tr(bank[2][:, BLK * k:BLK * k + BLK], act_[s][64:128, P * k:P * k + P], 64)
                last.then_inc(aT_.sem, 1)
                wait("ac")
                for k in range(FE // P):
                    for half in range(2):
                        last = mm(bank[3 + s][64 * half:64 * half + 64, :], aT[s][:, k, :], dn[:, k, 512 * half:512 * half + 512],
                                  start=k == 0, stop=k == FE // P - 1)
                last.then_inc(d_.sem, 1)

            def moe(l):
                pe.wait_ge(*since(ro_done[l], 1))
                pe.wait_ge(*since(h2_row[l], len(TILES[l])))
                with pe.Fori(0, E // 2) as j:
                    for s in range(2):
                        def wait(what):
                            if what == "x":
                                wait_alone(pe, *since(mo_xg[l][s], 16 * j + 16))
                            elif what == "w":
                                pe.wait_ge(e_full[s], 48 * j + (48 + l * 24 * E))
                            else:
                                wait_alone(pe, *since({"xc": mo_xc, "a": mo_a, "ac": mo_ac}[what][l], 2 * j + (s + 1)))
                        moe_block(s, (slotA, slotB)[s], wait,
                                  (mo_xT[l], mo_gu[l], mo_aT[l], mo_d[l]))
                n = pe.value_load(ownI[0:1, XBLK[l]:XBLK[l] + 1], min_val=0, max_val=XBLK[l])
                pe.wait_ge(*since(mo_y[l], E))
                with pe.If(n > 0):
                    with pe.Fori(0, n) as b:
                        def wait(what):
                            if what == "x":
                                wait_alone(pe, *since(xt_xg[l], 16 * b + 16))
                            elif what == "w":
                                pe.wait_ge(*since(xt_w[l], 48 * b + 48))
                            elif what == "a":
                                wait_alone(pe, *since(xt_a[l], b + 1))
                            else:
                                wait_alone(pe, *since(xt_act[l], 3 * b + {"xc": 1, "ac": 3}[what]))
                        moe_block(0, slotA, wait, (xt_mm[l],) * 4)
                with pe.Else():
                    pe.nop()

            def combine(l):
                for i in range(len(TILES[l])):
                    pe.wait_ge(*since(cb_w[l], i + 1))
                    if i >= 2:
                        pe.wait_ge(*since(cb_r[l], i - 1))
                    for k in range(KC):
                        o = 512 * (4 + 2 * (i % 2)) + P * k
                        last = tr(psum[:, o:o + P], fw[i % 2][:, P * k:P * k + P])
                    last.then_inc(cb_T[l].sem, 1)

            pe.wait_ge(s_const, 16)
            norm(nbuf1, T, n1_sq[0], n1_mm[0])
            pe.wait_ge(s_c, 1)
            pe.wait_ge(s_zero, 1)
            for m in range(MOD_FIRST):
                if m % 2 == 0:
                    pe.wait_ge(first_full[m // 2], 16)
                if m >= 2:
                    pe.wait_ge(mod_out, m - 1)
                mod_parts(first_mods[m], pmods[m % 2])
                mod_turn_pending()
                unturned.append(m)
            mod_turn_pending()
            for l in range(L):
                if l:
                    norm(nbuf1, T, n1_sq[l], n1_mm[l])
                for g in range(NDENSE):
                    for c in range(2):
                        dense_chunk(l, g, c)
                    if g == first_group("x") + 1:
                        for i in range(WC):
                            rope(l, i)
                    if g == first_group("u") + 1:
                        for i in range(WC, 2 * WC):
                            rope(l, i)
                gmlp(l)
                nu = len(UNITS[l])
                att_scores(l, 0)
                for u in range(nu):
                    for i in fillers(l, u):
                        dense_chunk(l, NDENSE + i // 2, i % 2)
                    att_trans(l, u)
                    if u + 1 < nu:
                        att_scores(l, u + 1)
                    if u >= H and u % H == 0:
                        att_oT(l, u // H - 1)
                    att_out(l, u)
                att_oT(l, nu // H - 1)
                gate = 16
                for seg in range(2):
                    ml_features(l, seg)
                    if seg == 1 and with_h(l, 0):
                        ml_turn(l, 0)
                        pe.wait_ge(*since(ml_y[l], 1))
                    ml_gates(l, seg)
                    dense_chunk(l, NDENSE + gate // 2, gate % 2)
                    gate += 1
                    ml_cumulate(l, seg)
                    ml_max_turn(l, seg)
                    for w in range(5):
                        if w < 4:
                            ml_open(l, seg, w)
                        if w > 0:
                            ml_unit(l, seg, w - 1)
                        if w in ML_FILL:
                            dense_chunk(l, NDENSE + gate // 2, gate % 2)
                            gate += 1
                mod_turn_pending()
                t0 = T0[l]

                def branch(s, bs):
                    w = cut(rslot(s), 0, 3 * WC, P)
                    for b in bs:
                        y = (yaT, uT, zT)[b]
                        for k in range(WC):
                            last = mm(bank[BRB[s][b]][:, 0:NT[l]], w[:, WC * b + k, :], y[:, k, t0:T],
                                      start=k == 0, stop=k == WC - 1)
                    return last
                pe.wait_ge(*since(ml_sg[l], 4 * (2 - l)))
                pe.wait_ge(dense_out, dense[0])
                pe.wait_ge(*since(at_y[l], len(TILES[l])))
                for s in range(2):
                    pe.wait_ge(ring_full[s], 16 + 8 * base_br[l])
                    branch(s, (0, 1))
                ml_turn(l, 1)
                pe.wait_ge(*since(ml_y[l], 2 - l))
                pe.wait_ge(*since(br_done[l], 2))
                for s in range(2):
                    branch(s, (2,)).then_inc(br_mm[l].sem, 1)
                with pe.Fori(1, BRG // 2) as j:
                    for s in range(2):
                        pe.wait_ge(ring_full[s], 16 * j + (16 + 8 * base_br[l]))
                        pe.wait_ge(*since(br_done[l], 2 * j + (s + 1)))
                        branch(s, (0, 1, 2)).then_inc(br_mm[l].sem, 1)
                pe.wait_ge(*since(br_done[l], BRG + 2))
                with pe.Fori(0, OUTG // 2) as j:
                    for s in range(2):
                        pe.wait_ge(ring_full[s], 16 * j + (16 + 8 * (base_br[l] + BRG)))
                        w = cut(rslot(s), 0, KC, COLS)
                        for c in range(2):
                            for k in range(KC):
                                last = mm(bank[4 + 2 * s + c][:, 0:NT[l]], w[:, k, P * c:P * c + P], hT[:, k, t0:T],
                                          start=k == 0, stop=k == KC - 1)
                            last.then_inc(wo_mm[l].sem, 1)
                    pe.wait_ge(*since(res1[l], 4 * j + 4))
                norm(nbuf2, NT[l], n2_sq[l], n2_mm[l])
                route(l)
                h2_rows(l)
                positions(l)
                moe(l)
                combine(l)
            for c in range(KC):
                pe.wait_ge(f_sq, c + 1)
                if c == 0:
                    pe.wait_ge(*since(cb_r[L - 1], len(TILES[L - 1])))
                mm(bank[0][:, 0:LAT], ones, cut(slotB, 512 * (c % 2), LAT), start=c == 0, stop=c == KC - 1).then_inc(f_mm, 1)

        @block.scalar
        def _(act):
            step = [0]
            count = {}
            copied = [0]
            roots = [0]

            def fn(o, i, f, bias=0.0, scale=1.0, accum=None):
                return nc.scalar.activation(o, i, f, bias=bias, scale=scale, accum_out=accum)

            def done(ins, s):
                ins.then_inc(s, 1)
                count[s.name] = count.get(s.name, 0) + 1
                act.wait_ge(s, count[s.name])

            def link(ins):
                step[0] += 1
                ins.then_inc(act_step, 1)
                act.wait_ge(act_step, step[0])

            def root(v):
                roots[0] += 1
                act.wait_ge(rms_in, roots[0])
                done(fn(v, v, ACT.Sqrt), rms_out)

            def dense_copy(l, g, c):
                what, _, gi = WIN[g]
                d = copied[0]
                copied[0] += 1
                b = bank[d % 2]
                t0 = 0 if what in "kxv" else T0[l]
                act.wait_ge(dense_full, d + 1)
                if what in ("v", "bv"):
                    tiles = list(range(t0 // P, NTILE))
                    n = len(tiles) // 2
                    a = tiles[n * c]
                    o = (vA if what == "v" else vG)[:, a:a + n, COLS * gi:COLS * gi + COLS]
                    i = cut(b, 0, n, COLS)
                else:
                    j = 2 * gi + c
                    o = {"k": kT, "q": qT, "x": xm, "u": uT, "z": zT, "gate": gates}[what][:, j, t0:T]
                    i = b[:, 0:T - t0]
                f, s = {"u": (ACT.Gelu_apprx_tanh, 1.0), "bv": (ACT.Gelu_apprx_tanh, 1.0), "z": (ACT.Tanh, 0.5),
                        "gate": (ACT.Tanh, 0.5)}.get(what, (ACT.Copy, 1.0))
                done(fn(o, i, f, scale=s), dense_out)

            unstored = []

            def mod_store_pending():
                if unstored:
                    m = unstored.pop()
                    act.wait_ge(mod_t, m + 1)
                    k = 2 * (m % MODG)
                    done(fn(modT[:, m // MODG, k:k + 2, :], cut(pmods[m % 2 if m < MOD_FIRST else 0], COLS, 2, 2), ACT.Copy), mod_out)

            def chunk(l, g, c):
                dense_copy(l, g, c)
                mod_store_pending()
                if (g, c) in MOD_AT[l]:
                    m = MOD_AT[l][g, c]
                    act.wait_ge(mod_mm, m + 1)
                    done(fn(mraw[m % 2], pmod[:, 0:COLS], ACT.Copy), mod_ev)
                    unstored.append(m)

            def squares(buf, t0, t1, summed, out, ready=None):
                n = t1 - t0
                for c in range(KC):
                    if ready:
                        act.wait_ge(*since(ready, c + 1))
                    if c >= 2:
                        act.wait_ge(*since(summed, c - 1))
                    done(fn(cut(buf, 512 * (c % 2), n), xT[:, c, t0:t1], ACT.Square, scale=D ** -0.5), out.sem)
                root(cut(buf, 1024, n))

            def modulate(t0, t1, scaled, ready, shift, factor):
                for c in range(KC):
                    act.wait_ge(*since(scaled, c + 1))
                    for w in range(2):
                        a, b = max(t0, 256 * w), 256 * (w + 1)
                        if a < b:
                            last = fn(hT[:, c, a:b], hT[:, c, a:b], ACT.Identity, bias=shift[:, c, w:w + 1], scale=factor[:, c, w:w + 1])
                    done(last, ready.sem)

            def attention_exp(l, u):
                h, t = UNITS[l][u]
                keys = CTX if t < 2 else T
                act.wait_ge(*since(at_nb[l], u + 1))
                if u >= 1:
                    act.wait_ge(*since(at_a[l], u))
                for m in range(2):
                    done(fn(probs[:, m, 0:keys], bank[4 + m][:, 0:keys], ACT.Exp, bias=nbias[:, m:m + 1], scale=SCALE,
                       accum=psum_[:, m:m + 1]), at_exp[l].sem)

            def attention_T(l, u):
                h, t = UNITS[l][u]
                n = 2 if t < 2 else NTILE
                act.wait_ge(*since(at_T[l], u + 1))
                if u >= 1:
                    act.wait_ge(*since(at_o[l], u))
                done(fn(attT[:, 0:n, :], cut(bank[6], 0, n, P), ACT.Copy), at_aT[l].sem)

            def attention_square(l, u):
                act.wait_ge(*since(at_o[l], u + 1))
                h = UNITS[l][u][0]
                done(fn(osq, bank[7][:, 0:P], ACT.Square, scale=DV ** -0.5, accum=oss[:, h:h + 1]), at_sq[l].sem)
                if h == H - 1:
                    root(orms)

            def attention_y(l, i):
                t = TILES[l][i]
                act.wait_ge(*since(at_oT[l], i + 1))
                if i == 0:
                    act.wait_ge(*since(mixg_mm[l], WC))
                done(fn(yaT[:, :, P * t:P * t + P], cut(bank[2], 0, H, P), ACT.Copy, scale=gvec[:, 0:1]), at_y[l].sem)

            def ml_features(l, seg):
                for i in range(NFA):
                    act.wait_ge(*since(ml_ff[l], seg * NF + i + 1))
                    done(fn((mq, mk, mv)[i // 2][:, 2 * (i % 2):2 * (i % 2) + 2, :], cut(bank[4 + i % 4], 0, 2, 256), ACT.Copy), ml_fa[l].sem)

            def ml_logf(l, seg):
                act.wait_ge(*since(ml_ga[l], seg + 1))
                link(fn(mtmp, mtmp, ACT.Exp, scale=-1.0))
                done(fn(mtmp, mtmp, ACT.Ln, bias=1.0), ml_gl[l].sem)

            def ml_unit(l, seg, w):
                d, t = MUN[w]
                n, nh = 4 * seg + w, 4 * (seg - l) + w
                act.wait_ge(*since(ml_ei[l], n + 1))
                done(fn(mee[w % 2], mex, ACT.Exp), ml_ex[l].sem)
                if with_h(l, seg):
                    act.wait_ge(*since(ml_nd[l], nh + 1))
                    s = sg[w % 2]
                    for h in range(H):
                        last = fn(s[:, h, :], s[:, h, :], ACT.Exp, bias=mr[:, d, t, h:h + 1], scale=-1.0)
                    done(last, ml_d[l].sem)

            def ml_inter(l, seg, w):
                nh = 4 * (seg - l) + w
                act.wait_ge(*since(ml_num[l], nh + 1))
                for h in range(H):
                    last = fn(inter[:, h, :], bank[7][:, P * h:P * h + P], ACT.Copy, scale=mee[w % 2][:, 2, h:h + 1])
                done(last, ml_int[l].sem)

            def moe_block(s, wait, xc_, s_, ac_):
                wait("xT")
                fn(xgT[s], cut(bank[0], 0, KC, BLK), ACT.Copy).then_inc(xc_.sem, 1)
                wait("gu")
                fn(gs[s][64:128, :], bank[1][0:64, :], ACT.Silu).then_inc(s_.sem, 1)
                wait("aT")
                fn(aT[s], cut(bank[2], 0, FE // P, BLK), ACT.Copy).then_inc(ac_.sem, 1)

            act.wait_ge(s_head, 16)
            done(fn(csil[:, :, 0:2], par("c", KC, 2), ACT.Silu), s_c)
            act.wait_ge(s_x, 16)
            squares(nbuf1, 0, T, n1_mm[0], n1_sq[0])
            for m in range(MOD_FIRST):
                act.wait_ge(mod_mm, m + 1)
                done(fn(mraw[m % 2], pmods[m % 2][:, 0:COLS], ACT.Copy), mod_ev)
                mod_store_pending()
                unstored.append(m)
            mod_store_pending()
            for l in range(L):
                if l:
                    act.wait_ge(*since(cb_r[0], len(TILES[0])))
                    squares(nbuf1, 0, T, n1_mm[l], n1_sq[l])
                act.wait_ge(*since(n1_f[l], 1))
                modulate(0, T, n1_nt[l], h_ready[l], modT[:, l, 0:KC, :], normA)
                for g in range(NDENSE):
                    for c in range(2):
                        chunk(l, g, c)
                    if g == first_group("q") + 1:
                        act.wait_ge(*since(conv_done[l], 1))
                        done(fn(xc.rearrange("p c t -> p (c t)"), xc.rearrange("p c t -> p (c t)"), ACT.Silu), xc_done[l].sem)
                    if g == first_group("bv") + 1:
                        act.wait_ge(dense_out, copied[0])
                        for i, t in enumerate(TILES[l]):
                            done(fn(attw, vG[:, t, :], ACT.Square, scale=W ** -0.5, accum=ssq[:, t:t + 1]), bv_sq[l].sem)
                        root(rst[:, TILES[l][0]:NTILE])
                act.wait_ge(*since(lam_in[l], 1))
                done(fn(lamv[:, 2:4], lamv[:, 0:2], ACT.Exp), lam_ex[l].sem)
                nu = len(UNITS[l])
                for u in range(nu):
                    attention_exp(l, u)
                    for i in fillers(l, u):
                        chunk(l, NDENSE + i // 2, i % 2)
                    attention_T(l, u)
                    if u >= H and u % H == 0:
                        attention_y(l, u // H - 1)
                    attention_square(l, u)
                attention_y(l, nu // H - 1)
                gate = 16
                for seg in range(2):
                    ml_features(l, seg)
                    chunk(l, NDENSE + gate // 2, gate % 2)
                    gate += 1
                    ml_logf(l, seg)
                    for w in range(5):
                        if w < 4:
                            ml_unit(l, seg, w)
                        if w > 0 and with_h(l, seg):
                            ml_inter(l, seg, w - 1)
                        if w in ML_FILL:
                            chunk(l, NDENSE + gate // 2, gate % 2)
                            gate += 1
                    if with_h(l, seg):
                        root(hss)
                mod_store_pending()
                act.wait_ge(*since(br_done[l], BRG + 2))
                squares(nbuf2, T0[l], T, n2_mm[l], n2_sq[l], res1[l])
                modulate(T0[l], T, n2_nt[l], h2_ready[l], modT[:, l, 3 * KC:4 * KC, :], normA)
                for i, t in enumerate(TILES[l]):
                    act.wait_ge(*since(h2_T[l], i + 1))
                    if i >= 2:
                        act.wait_ge(*since(h2_st[l][i % 2], 16 * (i // 2)))
                    b = 512 * (4 + 2 * (i % 2))
                    done(fn(h2row[i % 2], psum[:, b:b + D], ACT.Copy), h2_row[l].sem)
                    act.wait_ge(*since(h2_row[l], i + 1))
                    act.dma_start(h2_dram[l][P * i:P * i + P, :], h2row[i % 2]).then_inc(h2_st[l][i % 2].sem, 16)
                act.wait_ge(*since(ro_ei[l], 1))
                done(fn(ro["ge"][l], ro["ge"][l], ACT.Exp), ro_ex[l].sem)
                act.wait_ge(*since(ro_ei[l], 2))
                done(fn(ro["e2"][l], ro["e2"][l], ACT.Exp), ro_ex[l].sem)
                with act.Fori(0, E // 2) as j:
                    for s in range(2):
                        def wait(what):
                            act.wait_ge(*since({"xT": mo_xT, "gu": mo_gu, "aT": mo_aT}[what][l], 2 * j + (s + 1)))
                        moe_block(s, wait, mo_xc[l], mo_s[l], mo_ac[l])
                act.wait_ge(*since(ro_done[l], 1))
                n = act.value_load(ownI[0:1, XBLK[l]:XBLK[l] + 1], min_val=0, max_val=XBLK[l])
                with act.If(n > 0):
                    with act.Fori(0, n) as b:
                        def wait(what):
                            act.wait_ge(*since(xt_mm[l], 4 * b + {"xT": 1, "gu": 2, "aT": 3}[what]))
                        moe_block(0, wait, xt_act[l], xt_act[l], xt_act[l])
                with act.Else():
                    act.nop()
            act.wait_ge(*since(cb_r[L - 1], len(TILES[L - 1])))
            for c in range(KC):
                if c >= 2:
                    act.wait_ge(f_mm, c - 1)
                done(fn(cut(slotB, 512 * (c % 2), LAT), xT[:, c, CTX:T], ACT.Square, scale=D ** -0.5), f_sq)
            root(cut(slotB, 1024, LAT))

        @block.vector
        def _(dve):
            step = [0]
            count = {}
            roots = [0]
            V = nc.vector

            def done(ins, s):
                ins.then_inc(s, 1)
                count[s.name] = count.get(s.name, 0) + 1
                dve.wait_ge(s, count[s.name])

            def link(ins):
                step[0] += 1
                ins.then_inc(dve_step, 1)
                dve.wait_ge(dve_step, step[0])

            def chain():
                dve.wait_ge(dve_step, step[0])

            def free(ins):
                step[0] += 1
                ins.then_inc(dve_step, 1)

            def bc(ap, *shape):
                return ap.to_broadcast(list(shape))

            def rstd(o, i, scale=1.0):
                done(V.tensor_scalar(o, i, scale, EPS, ALU.mult, ALU.add), rms_in)
                roots[0] += 1
                dve.wait_ge(rms_out, roots[0])
                link(V.reciprocal(o, o))

            def norm(buf, t0, t1, summed, scaled):
                n = t1 - t0
                dve.wait_ge(*since(summed, KC))
                rs = cut(buf, 1024, n)
                rstd(rs, bank[7][:, 0:n])
                for c in range(KC):
                    done(V.tensor_tensor(hT[:, c, t0:t1], xT[:, c, t0:t1], rs, ALU.mult), scaled.sem)

            def factor(scale_mod, gain):
                return V.scalar_tensor_tensor(normA, scale_mod, 1.0, bc(gain.unsqueeze(2), P, KC, 2), ALU.add, ALU.mult)

            def rope(l, i):
                src = (kT if i < WC else qT)[:, i % WC, CTX:T]
                dve.wait_ge(*since(rope_mm[l], i + 1))
                free(V.tensor_tensor(rope_c, src, const("cos"), ALU.mult))
                link(V.tensor_tensor(rope_s, bank[4 + i % 2][:, 0:LAT], const("sin"), ALU.mult))
                done(V.tensor_tensor(src, rope_c, rope_s, ALU.add), kq_done[l].sem)

            def conv(l):
                dve.wait_ge(*since(s_small[l], 16))
                wc, b = par("w_conv", CONV_K, WC), par("b_conv", WC)
                for c in range(WC):
                    dve.wait_ge(dense_out, chunk_no(l, first_group("x") + c // 2, c % 2))
                    x = xm[:, c, :].rearrange("p (s t) -> p s t", s=2)
                    o = xc[:, c, :].rearrange("p (s t) -> p s t", s=2)
                    link(V.tensor_scalar(o, x, wc[:, 1, c:c + 1], b[:, c:c + 1], ALU.mult, ALU.add))
                    link(V.scalar_tensor_tensor(o[:, :, 1:256], x[:, :, 0:255], wc[:, 0, c:c + 1], o[:, :, 1:256], ALU.mult, ALU.add))
                    last = V.scalar_tensor_tensor(o[:, :, 0:255], x[:, :, 1:256], wc[:, 2, c:c + 1], o[:, :, 0:255], ALU.mult, ALU.add)
                    if c < WC - 1:
                        free(last)
                done(last, conv_done[l].sem)

            def gmlp(l):
                dve.wait_ge(*since(bv_sq[l], len(TILES[l])))
                a, b = TILES[l][0], NTILE
                dve.wait_ge(*since(s_early[l], 16))
                rstd(rst[:, a:b], ssq[:, a:b])
                for t in TILES[l]:
                    done(V.tensor_scalar(vG[:, t, :], vG[:, t, :], rst[:, t:t + 1], None, ALU.mult), bv_done[l].sem)
                gv, bs = par("g_v", WC), par("b_s", WC, P)
                n = len(TILES[l])
                for g in range(WC):
                    dve.wait_ge(*since(mixg_mm[l], g + 1))
                    dve.wait_ge(dense_out, chunk_no(l, first_group("u") + 1))
                    link(V.scalar_tensor_tensor(cut(slotA, 7680, n, P), cut(bank[4 + g % 2], 0, n, P), gv[:, g:g + 1],
                                                bc(bs[:, g, :].unsqueeze(1), P, n, P), ALU.mult, ALU.add))
                    o = uT[:, g, T0[l]:T]
                    done(V.tensor_tensor(o, o, attw[:, 0:NT[l]], ALU.mult), yb_done[l].sem)

            def factors(l):
                init = 0.8 - 0.6 * math.exp(-0.3 * l)
                lam = par("lam", 4, DK)
                prod = cut(slotA, 7680, 2, DK)
                link(V.tensor_tensor(prod, lam[:, 0:4:2, :], lam[:, 1:4:2, :], ALU.mult))
                done(V.tensor_reduce(lamv[:, 0:2], prod, AX, ALU.add), lam_in[l].sem)
                free(V.tensor_scalar(gvec[:, 0:1], par("g_diff"), 1.0 - init, None, ALU.mult))
                free(V.tensor_scalar(gvec[:, 1:1 + WC], par("g_ml", WC), 0.5, None, ALU.mult))
                free(V.tensor_scalar(gvec[:, 5:5 + WC], par("skip", WC), 0.5, None, ALU.mult))
                dve.wait_ge(*since(lam_ex[l], 1))
                link(V.scalar_tensor_tensor(lamv[:, 0:1], lamv[:, 2:3], init, lamv[:, 3:4], ALU.add, ALU.subtract))

            def att_weights(l, u):
                h, t = UNITS[l][u]
                keys = CTX if t < 2 else T
                dve.wait_ge(*since(at_s[l], u + 1))
                link(V.tensor_reduce(nmax, cut(psum, 4 * 512, 2, 512)[:, :, 0:keys], AX, ALU.max))
                done(V.tensor_scalar(nbias, nmax, -SCALE, None, ALU.mult), at_nb[l].sem)
                dve.wait_ge(*since(at_exp[l], 2 * u + 2))
                link(V.reciprocal(prec, psum_))
                link(V.tensor_tensor(prec[:, 1:2], prec[:, 1:2], lamv[:, 0:1], ALU.mult))
                link(V.tensor_scalar(probs[:, 1, 0:keys], probs[:, 1, 0:keys], prec[:, 1:2], None, ALU.mult))
                if u >= 1:
                    dve.wait_ge(*since(at_T[l], u))
                done(V.scalar_tensor_tensor(attw[:, 0:keys], probs[:, 0, 0:keys], prec[:, 0:1], probs[:, 1, 0:keys],
                                       ALU.mult, ALU.subtract), at_a[l].sem)

            def att_norm(l, u):
                h, t = UNITS[l][u]
                dve.wait_ge(*since(at_sq[l], u + 1))
                done(V.tensor_copy(oraw[:, h, :], bank[7][:, 0:P]), at_on[l].sem)
                if h == H - 1:
                    dve.wait_ge(*since(at_on[l], u + 1))
                    rstd(orms, oss)
                    if u >= H:
                        dve.wait_ge(*since(at_oT[l], u // H))
                    done(V.tensor_tensor(oN, oraw, bc(orms.unsqueeze(2), P, H, P), ALU.mult), at_nd[l].sem)

            def ml_features(l, seg):
                for i in range(NFA, NF):
                    dve.wait_ge(*since(ml_ff[l], seg * NF + i + 1))
                    b = cut(bank[4 + i % 4], 0, WC, P)
                    t = (i - NFA) // 2
                    if i % 2 == 0:
                        done(V.tensor_scalar(mkt[:, t, :, :], b, MSCALE, None, ALU.mult), ml_fe[l].sem)
                    else:
                        done(V.tensor_copy(mvt[:, t, :, :], b), ml_fe[l].sem)

            def ml_gates(l, seg):
                dve.wait_ge(*since(ml_gm[l], seg + 1))
                link(V.tensor_tensor(mgate, cut(bank[2], 0, 2, 16), bc(par("b_if", 16).unsqueeze(1), P, 2, 16), ALU.add))
                g4 = mgate.rearrange("p t (d i h) -> p (t d) i h", d=2, i=2)
                f = g4[:, :, 1, :]
                tm = mtmp.rearrange("p t d h -> p (t d) h")
                done(V.scalar_tensor_tensor(tm, f, -1.0, f, ALU.mult, ALU.max), ml_ga[l].sem)
                dve.wait_ge(*since(ml_gl[l], seg + 1))
                done(V.scalar_tensor_tensor(mlf.rearrange("p t d h -> p (t d) h"), f, 0.0, tm, ALU.min, ALU.subtract), ml_lf[l].sem)
                dve.wait_ge(*since(ml_cs[l], seg + 1))
                free(V.tensor_copy(mg, cut(bank[2], 48, 2, 2, H)))
                link(V.tensor_copy(mb, cut(bank[2], 32, 2, 2, H)))
                g5 = mgate.rearrange("p t (d i h) -> p t d i h", d=2, i=2)
                for d in range(2):
                    last = V.tensor_tensor(mr[:, d, :, :], g5[:, :, d, 0, :], mb[:, d, :, :], ALU.subtract)
                    if d == 0:
                        free(last)
                done(last, ml_r[l].sem)
                for i in range(2):
                    free(V.memset(cmax[i][:, 0, 0:PAD], -BIG))
                    free(V.memset(cmax[i][:, 1, P:P + PAD], -BIG))
                dve.wait_ge(*since(ml_rT[l], seg + 1))
                for d in range(2):
                    free(V.tensor_copy(cm_at(0, d), bank[2][0:8, P * (d + 1):P * (d + 2)]))
                chain()
                for i in range(7):
                    for d in range(2):
                        last = V.tensor_tensor(cm_at((i + 1) % 2, d), cm_at(i % 2, d), cm_at(i % 2, d, 2 ** i), ALU.max)
                        if i < 6 or d == 0:
                            free(last)
                    if i < 6:
                        chain()
                done(last, ml_cm[l].sem)
                dve.wait_ge(*since(ml_mt[l], seg + 1))
                link(V.tensor_copy(mMt, cut(bank[2], 64, 2, 2, H)))

            def ml_exponents(l, seg, w):
                d, t = MUN[w]
                n = 4 * seg + w
                m0 = mst[:, d, :]
                dve.wait_ge(*since(ml_bc[l], n + 1))
                link(V.tensor_tensor(mend, m0, cut(bank[4], 0, H, P)[:, :, P - 1 if d == 0 else 0], ALU.max))
                if n >= 1:
                    dve.wait_ge(*since(ml_ex[l], n))
                free(V.tensor_tensor(mex[:, 0, :], m0, mend, ALU.subtract))
                last = V.tensor_tensor(mex[:, 1, :], mr[:, d, t, :], mend, ALU.subtract)
                if with_h(l, seg):
                    free(last)
                    link(V.tensor_tensor(mmax, mMt[:, d, t, :], m0, ALU.max))
                    free(V.tensor_tensor(mex[:, 2, :], m0, mmax, ALU.subtract))
                    last = V.scalar_tensor_tensor(mex[:, 3, :], mb[:, d, t, :], -1.0, mmax, ALU.mult, ALU.subtract)
                done(last, ml_ei[l].sem)
                if with_h(l, seg):
                    for h in range(H):
                        last = V.scalar_tensor_tensor(sg[w % 2][:, h, :], bank[4][:, P * h:P * h + P], m0[:, h:h + 1],
                                                      const(("mask_f", "mask_b")[d]), ALU.max, ALU.add)
                        if h < H - 1:
                            free(last)
                    done(last, ml_nd[l].sem)
                    dve.wait_ge(*since(ml_nd[l], 4 * (seg - l) + w + 1))
                free(V.tensor_tensor(m0, mg[:, t, d, :], mend, ALU.add))

            def ml_weights(l, seg, w):
                d, t = MUN[w]
                n, nh = 4 * seg + w, 4 * (seg - l) + w
                s = sg[w % 2]
                if with_h(l, seg):
                    dve.wait_ge(*since(ml_d[l], nh + 1))
                    dve.wait_ge(*since(ml_qk[l], nh + 1))
                    done(V.scalar_tensor_tensor(s, cut(bank[5], 0, H, P), MSCALE, s, ALU.mult, ALU.mult), ml_sg[l].sem)
                dve.wait_ge(*since(ml_ex[l], n + 1))
                done(V.tensor_tensor(vw[w % 2], mvt[:, t, :, :], bc(mee[w % 2][:, 1, :].unsqueeze(2), P, H, P), ALU.mult), ml_vw[l].sem)

            def ml_unit(l, seg, w):
                d, t = MUN[w]
                n, nh = 4 * seg + w, 4 * (seg - l) + w
                e = mee[w % 2]
                if with_h(l, seg):
                    dve.wait_ge(*since(ml_int[l], nh + 1))
                    free(V.tensor_tensor(num, inter, cut(bank[6], 0, H, P), ALU.add))
                dve.wait_ge(*since(ml_upd[l], n + 1))
                if with_h(l, seg):
                    link(V.tensor_tensor(mden, bank[2][:, 84:88], e[:, 2, :], ALU.mult))
                    link(V.tensor_tensor(mden, bank[2][:, 80:84], mden, ALU.add))
                    link(V.scalar_tensor_tensor(mden, mden, -1.0, mden, ALU.mult, ALU.max))
                    link(V.tensor_tensor(mden, mden, e[:, 3, :], ALU.max))
                    link(V.reciprocal(mden2, mden))
                    r = bc(mden2.unsqueeze(2), P, H, P)
                    if w < 2:
                        done(V.tensor_tensor(hsum[:, t, :, :], num, r, ALU.mult), ml_hr[l].sem)
                    else:
                        link(V.tensor_tensor(num, num, r, ALU.mult))
                        done(V.tensor_tensor(hsum[:, t, :, :], hsum[:, t, :, :], num, ALU.add), ml_hr[l].sem)
                for h in range(H):
                    c = state[:, d, h, :]
                    free(V.scalar_tensor_tensor(c, c, e[:, 0, h:h + 1], bank[3][:, P * h:P * h + P], ALU.mult, ALU.add))
                link(V.tensor_tensor(nst[:, d, :], nst[:, d, :], e[:, 0, :], ALU.mult))
                done(V.tensor_tensor(nst[:, d, :], nst[:, d, :], bank[2][:, 88:88 + H], ALU.add), ml_st[l].sem)

            def ml_output(l, seg):
                i = seg - l
                dve.wait_ge(*since(ml_hr[l], 4 * (i + 1)))
                for t in range(2):
                    link(V.tensor_tensor(hsq, hsum[:, t, :, :], hsum[:, t, :, :], ALU.mult))
                    link(V.tensor_reduce(hss[:, t, :], hsq, AX, ALU.add))
                rstd(hss, hss, 1.0 / DV)
                for t in range(2):
                    last = V.tensor_tensor(hn[:, t, :, :], hsum[:, t, :, :], bc(hss[:, t, :].unsqueeze(2), P, H, P), ALU.mult)
                    if t == 0:
                        free(last)
                done(last, ml_hn[l].sem)

            def ml_finish(l, seg):
                i = seg - l
                sl = slice(256 * seg, 256 * seg + 256)
                for h in range(H):
                    free(V.tensor_scalar(xs[:, h, :], xc[:, h, sl], gvec[:, 5 + h:6 + h], None, ALU.mult))
                chain()
                dve.wait_ge(*since(ml_hT[l], i + 1))
                for h in range(H):
                    src = cut(psum, 2 * 512, 2, 512)[:, :, P * h:P * h + P]
                    free(V.scalar_tensor_tensor(yt[:, h, :].rearrange("p (t e) -> p t e", t=2), src, gvec[:, 1 + h:2 + h],
                                                xs[:, h, :].rearrange("p (t e) -> p t e", t=2), ALU.mult, ALU.add))
                chain()
                dve.wait_ge(dense_out, chunk_no(l, first_group("z") + 1))
                done(V.scalar_tensor_tensor(zT[:, :, sl], zT[:, :, sl], 1.0, yt, ALU.add, ALU.mult), ml_y[l].sem)

            def first_of(o, idx, x, big, iota, n, m):
                tmp = ro["cand"][0][:, 0:n * m].rearrange("p (n m) -> p n m", n=n)
                link(V.tensor_tensor(o, x, bc(big.unsqueeze(2), P, n, m), ALU.is_equal))
                link(V.scalar_tensor_tensor(tmp, o, -1024.0, bc(iota.unsqueeze(1), P, n, m), ALU.mult, ALU.add))
                link(V.tensor_reduce(idx, tmp, AX, ALU.min))
                link(V.tensor_scalar(idx, idx, 1024.0, None, ALU.add))
                link(V.tensor_tensor(o, bc(iota.unsqueeze(1), P, n, m), bc(idx.unsqueeze(2), P, n, m), ALU.is_equal))

            def route(l):
                n = len(TILES[l])
                br = par("b_route", GROUPS + E)
                lg, le, oh1, oh2, m = (ro[k][l] for k in ("lg", "le", "oh1", "oh2", "m"))
                iota = const("iota")
                logits = cut(bank[0], 0, n, GROUPS + E)
                dve.wait_ge(*since(ro_mm[l], 1))
                free(V.tensor_tensor(lg, logits[:, :, 0:GROUPS], bc(br[:, 0:GROUPS].unsqueeze(1), P, n, GROUPS), ALU.add))
                done(V.tensor_tensor(le, logits[:, :, GROUPS:], bc(br[:, GROUPS:].unsqueeze(1), P, n, E), ALU.add), ro_in[l].sem)
                dve.wait_ge(*since(ro_in[l], 1))
                gm, gi, ge = ro["gm"][l], ro["gi"][l], ro["ge"][l]
                link(V.tensor_reduce(gm, lg, AX, ALU.max))
                done(V.tensor_tensor(ge, lg, bc(gm.unsqueeze(2), P, n, GROUPS), ALU.subtract), ro_ei[l].sem)
                oh = ro["goh"][l]
                first_of(oh, gi, lg, gm, iota[:, 0:GROUPS], n, GROUPS)
                link(V.tensor_scalar(oh, oh, 1.0, BIG, ALU.subtract, ALU.mult))
                v = le.rearrange("p n (g e) -> p (n g) e", g=GROUPS)
                link(V.tensor_tensor(v, v, bc(oh.rearrange("p n g -> p (n g)").unsqueeze(2), P, n * GROUPS, PER), ALU.add))
                m1, m2, idx, e2 = ro["m1"][l], ro["m2"][l], ro["idx"][l], ro["e2"][l]
                link(V.tensor_reduce(m1, le, AX, ALU.max))
                first_of(oh1, idx[:, 0, :], le, m1, iota[:, 0:E], n, E)
                link(V.scalar_tensor_tensor(le, oh1, -4.0 * BIG, le, ALU.mult, ALU.add))
                link(V.tensor_reduce(m2, le, AX, ALU.max))
                first_of(oh2, idx[:, 1, :], le, m2, iota[:, 0:E], n, E)
                done(V.tensor_tensor(m, oh1, oh2, ALU.add), ro_m[l].sem)
                done(V.tensor_tensor(e2, m2, m1, ALU.subtract), ro_ei[l].sem)
                dve.wait_ge(*since(ro_ex[l], 1))
                pg = ro["pg"][l]
                link(V.tensor_reduce(pg, ge, AX, ALU.add))
                link(V.reciprocal(pg, pg))
                dve.wait_ge(*since(ro_ex[l], 2))
                t1 = ro["t1"][l]
                wt = ro["wt"][l]
                link(V.tensor_scalar(t1, e2, 1.0, None, ALU.add))
                link(V.reciprocal(t1, t1))
                link(V.tensor_tensor(wt[:, 0, :], pg, t1, ALU.mult))
                link(V.tensor_tensor(wt[:, 1, :], wt[:, 0, :], e2, ALU.mult))
                dve.wait_ge(*since(ro_cnt[l], 1))
                cmp_, cnt = ro["cmp"][l], ro["cnt"][l]
                link(V.tensor_copy(cnt, bank[1][0:E, 256:257]))
                link(V.tensor_scalar(cmp_, const("thr", E), cnt, None, ALU.is_lt))
                done(V.tensor_reduce(ro["obl"][l], cmp_, AX, ALU.add), ro_obl[l].sem)
                rank, ob, fl, jj, bb = (ro[k][l] for k in ("rank", "ob", "fl", "jj", "bb"))
                tmp = ro["cand"][0][:, 0:n * E].rearrange("p (n e) -> p n e", n=n)
                for k, o in ((0, oh1), (1, oh2)):
                    link(V.tensor_tensor(tmp, o, cut(bank[1], 0, n, E), ALU.mult))
                    link(V.tensor_reduce(rank[:, k, :], tmp, AX, ALU.add))
                dve.wait_ge(*since(ro_ob[l], 1))
                oe = ro["oe"][l]
                link(V.tensor_copy(oe, cut(bank[2], 0, 2, E)))
                for k, o in ((0, oh1), (1, oh2)):
                    link(V.tensor_tensor(tmp, o, bc(oe[:, 0, :].unsqueeze(1), P, n, E), ALU.mult))
                    link(V.tensor_reduce(ob[:, k, :], tmp, AX, ALU.add))
                fc = ro["fc"][l]
                f1 = [a.rearrange("p k n -> p (k n)") for a in (rank, ob, fl, jj, bb, idx)]
                rank, ob, fl, jj, bb, ix = f1
                link(V.tensor_tensor(fc, bc(rank.unsqueeze(2), P, 2 * n, STEPS), bc(const("thr").unsqueeze(1), P, 2 * n, STEPS), ALU.is_ge))
                link(V.tensor_reduce(fl, fc, AX, ALU.add))
                link(V.scalar_tensor_tensor(jj, fl, -float(BLK), rank, ALU.mult, ALU.add))
                link(V.tensor_tensor(ob, ob, fl, ALU.add))
                link(V.scalar_tensor_tensor(ob, ob, E - 1.0, ix, ALU.add, ALU.subtract))
                link(V.scalar_tensor_tensor(bb, fl, 1.0, ob, ALU.is_ge, ALU.mult))
                link(V.tensor_tensor(bb, bb, ix, ALU.add))
                free(V.scalar_tensor_tensor(slotI[:, 0:2 * n], bb, float(BLK), jj, ALU.mult, ALU.add))
                J, BT = ro["J"][l], ro["BT"][l]
                nb = NBLK[l]
                free(V.tensor_tensor(J, bc(iota.unsqueeze(1), P, 2 * n, BLK), bc(jj.unsqueeze(2), P, 2 * n, BLK), ALU.is_equal))
                link(V.tensor_tensor(BT, bc(iota[:, 0:nb].unsqueeze(1), P, 2 * n, nb), bc(bb.unsqueeze(2), P, 2 * n, nb), ALU.is_equal))
                tok = const("tok")[:, 0:n]
                for k in range(2):
                    part = BT[:, n * k:n * k + n, :]
                    last = V.tensor_tensor(part, part, bc(tok.unsqueeze(2), P, n, nb), ALU.mult)
                    if k == 0:
                        free(last)
                done(last, ro_jb[l].sem)
                xb = XBLK[l]
                own, owc = ro["own"][l], ro["owc"][l]
                link(V.tensor_tensor(owc, bc(oe[0:1, 1, :].unsqueeze(1), 1, xb, E), bc(iota[0:1, 0:xb].unsqueeze(2), 1, xb, E), ALU.is_le))
                link(V.tensor_reduce(own[:, 0:xb], owc, AX, ALU.add))
                free(V.tensor_scalar(ownI[:, 0:xb], own[:, 0:xb], E - 1.0, None, ALU.min))
                free(V.tensor_copy(ownI[:, xb:xb + 1], oe[0:1, 1, E - 1:E]))
                dve.wait_ge(*since(ro_ix[l], 1))
                done(V.tensor_copy(idxI[:, 0:nb], bank[3][0:BLK, 0:nb]), ro_done[l].sem)

            def moe_act(s, o):
                return V.tensor_tensor(act_[s][64:128, :], gs[s][64:128, :], bank[1][64:128, :], ALU.mult).then_inc(o.sem, 1)

            dve.wait_ge(s_const, 16)
            for l in range(L):
                if l == 0:
                    dve.wait_ge(s_x, 16)
                    norm(nbuf1, 0, T, n1_mm[l], n1_nt[l])
                    dve.wait_ge(s_head, 16)
                    dve.wait_ge(mod_out, MOD_FIRST)
                else:
                    dve.wait_ge(*since(s_small[l], 16))
                    dve.wait_ge(mod_out, MODG + MOD_FIRST)
                head = modT[:, l, 0:2 * KC, :]
                bm = par("b_mod", NMOD * KC)
                link(V.tensor_tensor(head, head, bc(bm[:, 0:2 * KC].unsqueeze(2), P, 2 * KC, 2), ALU.add))
                done(factor(modT[:, l, KC:2 * KC, :], par("g1", KC)), n1_f[l].sem)
                if l:
                    norm(nbuf1, 0, T, n1_mm[l], n1_nt[l])
                for i in range(WC):
                    rope(l, i)
                conv(l)
                for i in range(WC, 2 * WC):
                    rope(l, i)
                gmlp(l)
                factors(l)
                for u in range(len(UNITS[l])):
                    att_weights(l, u)
                    att_norm(l, u)
                for seg in range(2):
                    ml_features(l, seg)
                    if seg == 1 and with_h(l, 0):
                        ml_finish(l, 0)
                    if seg == 0:
                        free(V.memset(state, 0.0))
                        free(V.memset(nst, 0.0))
                        free(V.memset(mst, 0.0))
                    ml_gates(l, seg)
                    for w in range(5):
                        if w < 4:
                            ml_exponents(l, seg, w)
                            ml_weights(l, seg, w)
                        if w > 0:
                            ml_unit(l, seg, w - 1)
                    if with_h(l, seg):
                        ml_output(l, seg)
                ml_finish(l, 1)
                dve.wait_ge(mod_out, MODG * (l + 1))
                tail = modT[:, l, 2 * KC:, :]
                link(V.tensor_tensor(tail, tail, bc(bm[:, 2 * KC:].unsqueeze(2), P, 4 * KC, 2), ALU.add))
                link(V.tensor_scalar(gate2, modT[:, l, 2 * KC:3 * KC, :], 0.5, None, ALU.mult))
                dve.wait_ge(dense_out, chunk_no(l, len(WIN) - 1))
                dve.sem_inc(br_done[l].sem, 2)
                t0, n = T0[l], NT[l]
                with dve.Fori(0, BRG // 2) as j:
                    for s in range(2):
                        i = 2 * j + s
                        dve.wait_ge(*since(br_mm[l], i + 1))
                        for b in range(3):
                            g = gates[:, bass.ds(i + KC * b, 1), t0:T].rearrange("p a t -> p (a t)")
                            last = V.scalar_tensor_tensor(mrg[b][:, 0:n], g, 1.0, bank[BRB[s][b]][:, 0:n], ALU.add, ALU.mult)
                        last.then_inc(br_step[l].sem, 1)
                        dve.wait_ge(*since(br_step[l], 4 * j + (2 * s + 1)))
                        V.tensor_tensor(mrg[0][:, 0:n], mrg[0][:, 0:n], mrg[1][:, 0:n], ALU.add).then_inc(br_step[l].sem, 1)
                        dve.wait_ge(*since(br_step[l], 4 * j + (2 * s + 2)))
                        o = hT[:, bass.ds(i, 1), t0:T].rearrange("p a t -> p (a t)")
                        V.tensor_tensor(o, mrg[0][:, 0:n], mrg[2][:, 0:n], ALU.add).then_inc(br_done[l].sem, 1)
                        dve.wait_ge(*since(br_done[l], 2 * j + (s + 3)))
                for c in range(KC):
                    dve.wait_ge(*since(wo_mm[l], c + 1))
                    for w in range(1 if l else 0, 2):
                        x = xT[:, c, 256 * w:256 * w + 256]
                        y = bank[4 + c % 4][:, 256 * w - t0:256 * w - t0 + 256]
                        last = V.scalar_tensor_tensor(x, y, gate2[:, c, w:w + 1], x, ALU.mult, ALU.add)
                    done(last, res1[l].sem)
                dve.wait_ge(*since(res1[l], KC))
                link(factor(modT[:, l, 4 * KC:5 * KC, :], par("g2", KC)))
                norm(nbuf2, t0, T, n2_mm[l], n2_nt[l])
                route(l)
                with dve.Fori(0, E // 2) as j:
                    for s in range(2):
                        dve.wait_ge(*since(mo_s[l], 2 * j + (s + 1)))
                        moe_act(s, mo_a[l])
                        dve.wait_ge(*since(mo_d[l], 2 * j + (s + 1)))
                        dve.wait_ge(*since(mo_st[l][s], 32 * j + 16))
                        V.tensor_copy(yS[s], bank[3 + s]).then_inc(mo_y[l].sem, 1)
                dve.wait_ge(*since(ro_done[l], 1))
                nx = dve.value_load(ownI[0:1, XBLK[l]:XBLK[l] + 1], min_val=0, max_val=XBLK[l])
                with dve.If(nx > 0):
                    with dve.Fori(0, nx) as b:
                        dve.wait_ge(*since(xt_act[l], 3 * b + 2))
                        moe_act(0, xt_a[l])
                        dve.wait_ge(*since(xt_mm[l], 4 * b + 4))
                        dve.wait_ge(*since(xt_xg[l], 16 * b + 16))
                        V.tensor_copy(yS[0], bank[3]).then_inc(xt_y[l].sem, 1)
                with dve.Else():
                    dve.nop()
                nt = len(TILES[l])
                wt = ro["wt"][l]

                def residual2(i):
                    dve.wait_ge(*since(cb_T[l], i + 1))
                    t = TILES[l][i]
                    w = 0 if t < 2 else 1
                    for c in range(KC):
                        x = xT[:, c, P * t:P * t + P]
                        o = 512 * (4 + 2 * (i % 2)) + P * c
                        last = V.scalar_tensor_tensor(x, psum[:, o:o + P], modT[:, l, 5 * KC + c, w:w + 1], x, ALU.mult, ALU.add)
                        if c < KC - 1:
                            free(last)
                    done(last, cb_r[l].sem)
                for i in range(nt):
                    dve.wait_ge(*since(cb_g[l][i % 2], 32 * (i // 2 + 1)))
                    if i >= 2:
                        dve.wait_ge(*since(cb_T[l], i - 1))
                    link(V.tensor_scalar(fw[i % 2], yg[i % 2][:, 0, :], wt[:, 0, i:i + 1], None, ALU.mult))
                    done(V.scalar_tensor_tensor(fw[i % 2], yg[i % 2][:, 1, :], wt[:, 1, i:i + 1], fw[i % 2], ALU.mult, ALU.add), cb_w[l].sem)
                    if i >= 1:
                        residual2(i - 1)
                residual2(nt - 1)
            dve.wait_ge(*since(cb_r[L - 1], len(TILES[L - 1])))
            dve.wait_ge(f_mm, KC)
            rs = cut(slotB, 1024, LAT)
            rstd(rs, bank[0][:, 0:LAT])
            gf = par("g_fin", KC)
            for c in range(KC):
                done(V.scalar_tensor_tensor(fin[:, c * LAT:(c + 1) * LAT], xT[:, c, CTX:T], gf[:, c:c + 1], rs, ALU.mult, ALU.mult), f_out)

        @block.gpsimd
        def _(pool):
            nc.gpsimd.memset(csil[:, :, 2:32], 0.0).then_inc(s_zero, 1)
            n = XBLK[0] * BLK * D // P
            spare = y_flat[E * BLK:, :].rearrange("r n -> (r n)").rearrange("(p n) -> p n", p=P)
            pool.wait_ge(s_const, 16)
            for i in range(SPARE):
                w = n // SPARE
                pool.dma_start(spare[:, w * i:w * i + w], consts[:, 0:w]).then_inc(s_spare, 16)

            def gather(o, src, idx, s_):
                nc.gpsimd.indirect_dma_start(o, None, src[:, :], bass.IndirectOffsetOnAxis(ap=idx, axis=0)).then_inc(s_.sem, 16)

            for l in range(L):
                n = len(TILES[l])
                pool.wait_ge(s_spare, 16 * SPARE)
                pool.wait_ge(*since(ro_done[l], 1))
                for s in range(2):
                    pool.wait_ge(*since(h2_st[l][s], 16 * (n // 2)))
                for s in range(2):
                    nc.gpsimd.tensor_copy(idxS[s][:, :], idxI[:, s:s + 1]).then_inc(mo_ix[l].sem, 1)
                    pool.wait_ge(*since(mo_ix[l], s + 1))
                    gather(xg[s], h2_dram[l], idxS[s][:, :], mo_xg[l][s])
                with pool.Fori(0, E // 2 - 1) as j:
                    for s in range(2):
                        e = 2 * j + s
                        pool.wait_ge(*since(mo_xT[l], e + 1))
                        nc.gpsimd.tensor_copy(idxS[s][:, :], idxI[:, bass.ds(e + 2, 1)]).then_inc(mo_ix[l].sem, 1)
                        wait_alone(pool, *since(mo_ix[l], e + 3))
                        gather(xg[s], h2_dram[l], idxS[s][:, :], mo_xg[l][s])
                for s in range(2):
                    pool.wait_ge(*since(mo_st[l][s], 16 + 16 * E))
                nx = pool.value_load(ownI[0:1, XBLK[l]:XBLK[l] + 1], min_val=0, max_val=XBLK[l])
                with pool.If(nx > 0):
                    with pool.Fori(0, nx) as b:
                        nc.gpsimd.tensor_copy(idxS[0][:, :], idxI[:, bass.ds(b + E, 1)]).then_inc(xt_ix[l].sem, 1)
                        wait_alone(pool, *since(xt_ix[l], b + 1))
                        gather(xg[0], h2_dram[l], idxS[0][:, :], xt_xg[l])
                        pool.wait_ge(*since(xt_y[l], b + 1))
                        store(pool, b + E, yS[0], xt_st[l])
                        pool.wait_ge(*since(xt_st[l], 32 * b + 32))
                with pool.Else():
                    pool.nop()
                for i in range(n):
                    if i >= 2:
                        pool.wait_ge(*since(cb_w[l], i - 1))
                    for k in range(2):
                        q = k * n + i
                        gather(yg[i % 2][:, k, :], y_flat, slotI[:, q:q + 1], cb_g[l][i % 2])



def kernel(**inputs):
    import concourse.bacc as bacc
    from concourse.bass_utils import run_bass_kernel_spmd

    def a(name):
        return np.ascontiguousarray(inputs[name])

    def chan(v, n):
        return v.reshape(-1, n, P).transpose(2, 0, 1).reshape(P, -1)

    def rows(v):
        return np.broadcast_to(v.reshape(1, -1), (P, v.size))

    def groups(w, cols, k=KC):
        l, _, n = w.shape
        return np.ascontiguousarray(w.reshape(l, k, P, n // cols, cols).transpose(0, 3, 2, 1, 4)).reshape(-1, P, k * cols)

    x = np.concatenate([a("ctx")[0], a("x")[0]], 0)
    xt = np.ascontiguousarray(x.reshape(T, KC, P).transpose(2, 1, 0)).reshape(P, KC * T)
    small = np.zeros((L, P, SMALL_W), np.float32)
    for l in range(L):
        parts = {
            "b_mod": chan(a("b_mod")[l], NMOD * KC), "g1": chan(a("g_norm1")[l], KC), "g2": chan(a("g_norm2")[l], KC),
            "g_diff": a("g_diff_subln")[l][:, None], "g_v": chan(a("g_gmlp_v")[l], WC),
            "w_conv": chan(a("w_conv_m")[l], WC), "b_conv": chan(a("b_conv_m")[l], WC),
            "g_ml": chan(a("g_mlstm_norm")[l], WC), "skip": chan(a("skip_m")[l], WC), "g_fin": chan(a("g_final"), KC),
            "c": np.stack([a("c_ctx"), a("c")[0]]).reshape(2, KC, P).transpose(2, 1, 0).reshape(P, -1),
            "w_if": a("w_if_m")[l].reshape(3 * WC, P, 16).transpose(1, 0, 2).reshape(P, -1),
            "w_route": np.concatenate([a("w_route_g")[l], a("w_route_e")[l]], 1)
                .reshape(KC, P, GROUPS + E).transpose(1, 0, 2).reshape(P, -1),
            "b_if": rows(a("b_if_m")[l]), "b_route": rows(np.concatenate([a("b_route_g")[l], a("b_route_e")[l]])),
            "w_sT": a("w_gmlp_s")[l].transpose(2, 0, 1).reshape(P, -1),
            "w_qkv": a("w_qkv_m")[l].transpose(2, 0, 1, 3).reshape(P, -1),
        }
        for k, v in parts.items():
            small[l, :, SMALL[k][0]:SMALL[k][1]] = v
    early = np.stack([np.concatenate([rows(a("b_gmlp_s")[l]), rows(a("diff_lambda")[l])], 1) for l in range(L)])
    w = a("w_in").reshape(L, KC, P, -1)
    win = np.stack([w[..., c:c + COLS] for _, c, _ in WIN], 1).transpose(0, 1, 3, 2, 4)
    arrays = {
        "xt": xt, "consts": constants(), "small": small, "early": early,
        "wmod": groups(a("w_mod"), COLS), "win": np.ascontiguousarray(win).reshape(L * len(WIN), P, RW),
        "wbr": groups(a("w_branch").reshape(L, 3 * W, D), P, 3 * WC), "wout": groups(a("w_out"), COLS),
        "w_gate": a("w_e_gate").reshape(L * E, D, FE), "w_up": a("w_e_up").reshape(L * E, D, FE),
        "w_down": a("w_e_down").reshape(L * E, FE, D),
    }
    nc = bacc.Bacc("TRN2", target_bir_lowering=False, num_devices=1)
    t = {k: nc.dram_tensor(f"{k}_dram", v.shape, F32, kind="ExternalInput").ap() for k, v in arrays.items()}
    out = nc.dram_tensor("out", (P, KC * LAT), F32, kind="ExternalOutput").ap()
    h2 = [nc.dram_tensor(f"h2_{l}", (n, D), F32, kind="Internal").ap() for l, n in enumerate((T, LAT))]
    y = nc.dram_tensor("y_rows", (NBLK[0] * BLK, D), F32, kind="Internal").ap()
    build(nc, *(t[k] for k in ("xt", "consts", "small", "early", "wmod", "win", "wbr", "wout", "w_gate", "w_up", "w_down")), out, h2, y)
    r = run_bass_kernel_spmd(nc, [{f"{k}_dram": v for k, v in arrays.items()}], core_ids=[0])
    got = r.results[0]["out"]
    return got.reshape(P, KC, LAT).transpose(2, 1, 0).reshape(1, LAT, D)
```

```python
import math
from collections import namedtuple
import numpy as np
import concourse.bass as bass
from concourse import mybir
from contextlib import ExitStack

F32 = mybir.dt.float32
I32 = mybir.dt.int32
ALU = mybir.AluOpType
ACT = mybir.ActivationFunctionType
AX = mybir.AxisListType.X

L, D, CTX, LAT = 2, 1024, 256, 256
T = CTX + LAT
GRID_W, ROPE_BASE, EPS = 64, 10000.0, 1e-6
H, DK, DV = 4, 64, 128
W = 512
CONV_K = 3
NMOD = 6
GROUPS, PER, E = 4, 8, 32
FE = 512
P = 128
KC = D // P
WC = W // P
NTILE = T // P
COLS = 256
RW = KC * COLS
MODG = NMOD * D // COLS
BRG = D // P
OUTG = D // COLS
SCALE = DK ** -0.5
MSCALE = DV ** -0.5
BIG = 1e30

Entry = namedtuple("Entry", "sem base")

BLK = 64
XBLK = [(T * 2) // (BLK + 1), (LAT * 2) // (BLK + 1)]
NBLK = [E + n for n in XBLK]
MISC_W = 1372
STEPS = T // BLK - 1


def offsets(parts):
    at, out = 0, {}
    for name, n in parts:
        out[name] = (at, at + n)
        at += n
    return out, at


SMALL, SMALL_W = offsets([
    ("b_mod", NMOD * KC), ("g1", KC), ("g2", KC), ("g_diff", 1), ("g_v", WC), ("w_conv", CONV_K * WC), ("b_conv", WC),
    ("g_ml", WC), ("skip", WC), ("g_fin", KC), ("c", KC * 2), ("w_if", 3 * WC * 16), ("w_route", KC * (GROUPS + E)),
    ("b_if", 16), ("b_route", GROUPS + E), ("w_sT", WC * P), ("w_qkv", 3 * WC * P)])
EARLY, EARLY_W = offsets([("b_s", WC * P), ("lam", 4 * DK)])
CONST, CONST_W = offsets([
    ("ident", P), ("ones", P), ("tri_f", P), ("tri_b", P), ("tri_x", P), ("mask_f", P), ("mask_b", P), ("rot", P),
    ("cos", LAT), ("sin", LAT), ("sel", 2), ("iota", BLK), ("thr", STEPS)])


def constants():
    t = np.zeros((P, CONST_W), np.float32)

    def put(name, a):
        t[:, CONST[name][0]:CONST[name][1]] = a
    i, j = np.arange(P)[:, None], np.arange(P)[None, :]
    put("ident", i == j)
    put("ones", 1.0)
    put("tri_f", i <= j)
    put("tri_b", i >= j)
    put("tri_x", i < j)
    put("mask_f", np.where(i <= j, 0.0, BIG))
    put("mask_b", np.where(i >= j, 0.0, BIG))
    half = (np.arange(P) // 16) % 2
    rot = np.zeros((P, P), np.float32)
    for p in range(P):
        if half[p] == 0:
            rot[p + 16, p] = -1.0
        else:
            rot[p - 16, p] = 1.0
    put("rot", rot)
    inv = (ROPE_BASE ** (-np.arange(0, 32, 2, dtype=np.float32) / 32)).astype(np.float32)
    tok = np.arange(LAT)
    pos = np.stack([tok // GRID_W, tok % GRID_W]).astype(np.float32)
    ang = pos[(np.arange(P) // 32) % 2] * inv[np.arange(P) % 16][:, None]
    put("cos", np.cos(ang.astype(np.float32)))
    put("sin", np.sin(ang.astype(np.float32)))
    put("sel", np.stack([(np.arange(P) % 32) == 0, (np.arange(P) % 32) == 1], 1))
    put("iota", np.arange(BLK)[None, :])
    put("thr", BLK * (1 + np.arange(STEPS))[None, :])
    return t


WIN = [(k, c + COLS * g, g) for k, c, n in
       [("k", 0, 2), ("x", 1024, 2), ("v", 512, 2), ("q", 1536, 2), ("u", 2048, 2), ("bv", 2560, 2), ("z", 3072, 2),
        ("gate", 3584, 12)] for g in range(n)]
NGATE = 12
NDENSE = len(WIN) - NGATE
MOD_FIRST = 8
MOD_BEHIND = [sorted([(g, 1) for g in range(NDENSE + 8)] + [(4, 0), (6, 0)]), [(g, 1) for g in [0, 1, 2, 3, 4, 5, 7, 10] + list(range(NDENSE, NDENSE + 8))]]
MOD_AT = [{place: MOD_FIRST + l * MODG + i for i, place in enumerate(MOD_BEHIND[l])} for l in range(2)]


def build(nc, xt_in, consts_in, small_in, early_in, wmod, win, wbr, wout, w_gate, w_up, w_down, out, y_dram):
    stack = ExitStack()
    with stack:
        def sb(name, cols, dt=F32, rows=P):
            return stack.enter_context(nc.sbuf_tensor(name, [rows, cols], dt))

        def sem(name):
            return stack.enter_context(nc.semaphore(name))

        def cut(buf, at, *dims):
            n = math.prod(dims)
            v = buf[:, at:at + n]
            if len(dims) == 1:
                return v
            names = "abc"[:len(dims)]
            return v.rearrange(f"p ({' '.join(names)}) -> p {' '.join(names)}", **dict(zip(names, dims)))

        xT = cut(sb("xT", KC * T), 0, KC, T)
        hT = cut(sb("hT", KC * T), 0, KC, T)
        slotA = sb("slotA", 3 * 4096)
        slotB = sb("slotB", 3 * 4096)
        ring = sb("ring", 2 * RW)
        mix = sb("mix", 5 * WC * T)
        small = sb("small", SMALL_W)
        consts = sb("consts", CONST_W)
        misc = sb("misc", MISC_W)

        def const(name, rows=P):
            return consts[0:rows, CONST[name][0]:CONST[name][1]]

        def par(name, *dims):
            if name in EARLY:
                return cut(slotA, 9344 + EARLY[name][0], *dims)
            a, _ = SMALL[name]
            return cut(small, a, *dims) if dims else small[:, a:a + 1]

        ident = const("ident")
        ones = const("ones")
        xm = cut(mix, 0, WC, T)
        xc = cut(mix, 1 * WC * T, WC, T)
        uT = cut(mix, 2 * WC * T, WC, T)
        vG = cut(mix, 3 * WC * T, NTILE, W)
        yaT = cut(mix, 3 * WC * T, WC, T)
        zT = cut(mix, 4 * WC * T, WC, T)
        gates = cut(slotB, 0, 3 * KC, T)
        qT = cut(slotA, 0, WC, T)
        kT = cut(slotA, 2048, WC, T)
        vA = cut(slotA, 4096, NTILE, W)
        probs = cut(slotA, 6144, 2, T)
        attT = cut(slotA, 7168, NTILE, P)
        attw = cut(slotA, 7680, T)
        osq = cut(slotA, 8192, P)
        rope_c = cut(slotA, 6144, LAT)
        rope_s = cut(slotA, 6144 + LAT, LAT)
        oraw = cut(slotA, 8320, H, P)
        oN = cut(slotA, 8832, H, P)
        mring = slotA[:, 10240:10240 + RW]
        DV1 = DV + 1
        mq = cut(slotA, 6040, WC, 256)
        mk = cut(slotA, 7064, WC, 256)
        mv = cut(slotA, 8088, WC, 256)
        mkt = cut(slotA, 9112, 2, WC, P)
        mvt = cut(slotA, 10136, 2, WC, DV1)
        hsum = cut(slotA, 11168, 2, WC, P)
        sg = [cut(slotA, 512 * i, WC, P) for i in range(2)]
        vw = [cut(slotA, 1024 + 516 * i, WC, DV1) for i in range(2)]
        num = cut(slotA, 2056, WC, DV1)
        inter = cut(slotA, 2572, WC, DV1)
        state = cut(slotA, 3088, 2, WC, DV1)
        grow = slotA[0:16, 2056:2056 + 256]
        hsq = cut(slotA, 4120, WC, P)
        hn = cut(slotA, 4632, 2, WC, P)
        xs = cut(slotA, 0, WC, 256)
        yt = cut(slotA, 1024, WC, 256)
        tsq = [cut(slotB, KC * P * i, KC, P) for i in range(2)]
        trs = slotA[:, 8192:8192 + T]
        nbuf1 = slotB
        first_mods = [cut(slotA, i * RW, KC, COLS) for i in range(4)] + [cut(slotB, 4096 + i * RW, KC, COLS) for i in range(4)]
        nbuf2 = mix
        onehot = [cut(mix, 256 + 256 * i, NTILE, BLK) for i in range(2)]
        xrow = mix[:, 1024:1536]
        xgT = [cut(mix, 2048 + 512 * i, KC, BLK) for i in range(2)]
        gs = [mix[:, 3072 + 512 * i:3584 + 512 * i] for i in range(2)]
        act_ = [mix[:, 4096 + 512 * i:4608 + 512 * i] for i in range(2)]
        aT = [cut(mix, 5120 + 256 * i, 4, BLK) for i in range(2)]
        yS = [mix[:, 5632 + 512 * i:6144 + 512 * i] for i in range(2)]
        lgT = mix[0:GROUPS + E, 8192:8704]
        rt = mix[:, 8704:10240]
        yg = [cut(mix, 2 * D * i, 2, D) for i in range(NTILE)]
        fw = [mix[:, 8192 + D * i:8192 + D * (i + 1)] for i in range(2)]

        at = [0]

        def small_tile(*dims):
            v = cut(misc, at[0], *dims)
            at[0] += math.prod(dims)
            assert at[0] <= MISC_W
            return v
        csil = small_tile(KC, 32)
        mraw = [small_tile(COLS) for _ in range(2)]
        modT = small_tile(L, NMOD * KC, 2)
        normA = small_tile(KC, 2)
        gate2 = small_tile(KC, 2)
        lamv = small_tile(4)
        gvec = small_tile(4 * WC)
        ssq = small_tile(NTILE)
        rst = small_tile(NTILE)
        nmax = small_tile(2)
        nbias = small_tile(2)
        psum_ = small_tile(2)
        prec = small_tile(2)
        oss = small_tile(H)
        orms = small_tile(H)
        mgate = small_tile(2, 16)
        mlf = small_tile(2, 2, H)
        mtmp = small_tile(2, 2, H)
        mb = small_tile(2, 2, H)
        mg = small_tile(2, 2, H)
        mr = small_tile(2, 2, H)
        mMt = small_tile(2, 2, H)
        mst = small_tile(2, H)
        mend = small_tile(H)
        mmax = small_tile(H)
        mex = small_tile(4, H)
        mee = [small_tile(4, H) for _ in range(2)]
        mden = small_tile(H)
        mden2 = small_tile(H)
        hss = small_tile(2, H)
        PAD = P // 2
        cmax = [slotA[0:8, a:a + 2 * (P + PAD)].rearrange("p (d t) -> p d t", d=2) for a in (4120, 5656)]

        def cm_at(b, d, shift=0):
            a = (PAD - shift) if d == 0 else shift
            return cmax[b][:, d, a:a + P]
        slotI = sb("slotI", 2 * NTILE, I32)
        ownI = sb("ownI", XBLK[0] + 1, I32, 1)
        misc_wt = small_tile(2 * NTILE)

        psum = stack.enter_context(nc.psum_tensor("psum", [P, 8 * 512], F32))
        bank = [psum[:, 512 * i:512 * i + 512] for i in range(8)]
        pmod = bank[3]

        def heads(b, part):
            return [bank[b][:, DV1 * i:DV1 * (i + 1)] for i in range(3)] + [bank[2][:, 96 + DV1 * part:96 + DV1 * (part + 1)]]
        num_ps, inter_ps, upd_ps = heads(6, 0), heads(7, 1), heads(3, 2)


        BRB = ((4, 5, 6), (0, 1, 7))
        mrg = [mix[:, 512 * b:512 * b + 512] for b in range(3)]
        fin = mix[:, 4096:4096 + KC * LAT]
        y_flat = y_dram
        y_dram = y_dram.rearrange("(b r) n -> b r n", r=BLK)
        ro, used_cols = {}, [0]

        def ro_tile(name, *dims):
            sizes = [[d(l) if callable(d) else d for d in dims] for l in range(L)]
            ro[name] = [cut(rt, used_cols[0], *sizes[l]) for l in range(L)]
            used_cols[0] += max(math.prod(s) for s in sizes)
            assert used_cols[0] <= 1536

        def nt(l):
            return (NTILE, LAT // P)[l]
        for name, *dims in (
                ("lg", nt, GROUPS), ("ge", nt, GROUPS), ("goh", nt, GROUPS), ("gm", nt), ("gi", nt), ("pg", nt), ("t1", nt),
                ("le", nt, E), ("oh", 2, nt, E), ("m", nt, E), ("cand", nt, E), ("m1", nt), ("m2", nt),
                ("idx", 2, nt), ("e2", nt), ("rank", 2, nt), ("ob", 2, nt), ("fl", 2, nt), ("jj", 2, nt), ("bb", 2, nt),
                ("fc", lambda l: 2 * nt(l), STEPS), ("oe", 2, E), ("cmp", STEPS), ("cnt", 1), ("obl", 1)):
            ro_tile(name, *dims)
        for name in ("cmp", "cnt", "obl"):
            ro[name] = [v[0:E] for v in ro[name]]
        ro["own"] = [rt[0:1, 1100:1100 + XBLK[l]] for l in range(L)]
        ro["wt"] = [cut(misc_wt, 0, 2, nt(l)) for l in range(L)]
        ro["cand"] = [cut(rt, 1200, NTILE * E)] * L
        ro["cand2"] = [cut(mix, 5632, 2, nt(l), E) for l in range(L)]
        ro["places"] = [cut(mix, 0, nt(l), NBLK[l]) for l in range(L)]
        ro["BT"] = [cut(mix, 4608, 2 * nt(l), NBLK[l]) for l in range(L)]
        ro["owc"] = [mix[0:1, 5120:5120 + XBLK[l] * E].rearrange("p (a e) -> p a e", e=E) for l in range(L)]

        SPARE = 5
        NU = NTILE * H
        NF = 10
        ML_FILL = (2, 3)
        NFA = 6
        MUN = [(0, 0), (1, 1), (0, 1), (1, 0)]

        def counted(name, n):
            s = sem(name)
            return [Entry(s, n * l) for l in range(L)]

        def apart(name):
            return [Entry(sem(f"{name}_{l}"), 0) for l in range(L)]

        def by_buffer(name, n):
            both = [counted(f"{name}{i}", n) for i in range(2)]
            return [[both[i][l] for i in range(2)] for l in range(L)]

        def since(entry, value):
            return entry.sem, value + entry.base

        s_const = sem("const_loaded")
        s_x = sem("x_loaded")
        s_zero = sem("padding_zeroed")
        s_c = sem("silu_c")
        mod_mm = sem("mod_parts")
        mod_ev = sem("mod_parts_copied")
        mod_t = sem("mod_transposed")
        mod_out = sem("mod_stored")
        act_step = sem("act_step")
        dve_step = sem("dve_step")
        pool_step = sem("pool_step")
        dense_full = sem("dense_chunk_ready")
        dense_out = sem("dense_chunk_copied")
        f_sq = [Entry(sem("fin_squares"), 0)]
        f_mm = sem("fin_summed")
        f_out = sem("fin_out")
        s_out = sem("out_stored")
        s_passed = sem("waits_passed")
        s_spare = sem("spare_rows_filled")
        s_head = sem("small_head_loaded")
        first_full = [sem(f"first_mods_full{i}") for i in range(MOD_FIRST // 2)]
        mod_full = sem("mod_group_full")
        ring_full = [sem(f"ring_full{i}") for i in range(2)]
        e_full = [sem(f"expert_full{i}") for i in range(2)]
        rms_in, rms_out = sem("mean_squares"), sem("inverse_roots")
        s_small, s_early = apart("small_loaded"), apart("early_loaded")
        n1_sq = counted("n1_squares", KC)
        n1_ac = counted("n1_accumulated", KC - 1)
        n1_mm = counted("n1_summed", 1)
        n1_nt = counted("n1_scaled", KC)
        h_ready = counted("h_ready", KC)
        n1_f = counted("n1_factors", 1)
        rope_mm = counted("rope_mm", 2 * WC)
        kq_done = counted("kq_roped", 2 * WC)
        conv_done = counted("conv_summed", 1)
        xc_done = counted("xconv_ready", 1)
        bv_sq = counted("bv_squares", NTILE)
        bv_done = counted("bv_normed", NTILE)
        mixg_mm = counted("gmlp_mixed", WC)
        yb_done = counted("yb_ready", WC)
        lam_in = counted("lam_sums", 1)
        lam_ex = counted("lam_exps", 1)
        at_s = counted("att_scores", NU)
        at_nb = counted("att_bias", NU)
        at_exp = counted("att_exp", 2 * NU)
        at_a = counted("att_weights", NU)
        at_T = counted("att_T", NU)
        at_aT = counted("att_T_copied", NU)
        at_o = counted("att_out", NU)
        at_sq = counted("att_squares", NU)
        at_on = counted("att_kept", NU)
        at_oT = counted("att_oT", NTILE)
        at_nd = counted("att_normed", NTILE)
        at_y = counted("att_y", NTILE)
        ml_ff = counted("ml_features", 2 * NF)
        ml_fe = counted("ml_features_copied", 2 * (NF - NFA))
        ml_fa = counted("ml_features_copied_act", 2 * NFA)
        ml_gc = counted("ml_gates_rows", 2)
        ml_gr = counted("ml_gates_copied", 2)
        ml_gm = counted("ml_gates", 2)
        ml_ga = counted("ml_abs", 2)
        ml_gl = counted("ml_ln", 2)
        ml_lf = counted("ml_logf", 2)
        ml_cs = counted("ml_cumsum", 2)
        ml_r = counted("ml_r", 2)
        ml_rT = counted("ml_rT", 2)
        ml_cm = counted("ml_cummax", 2)
        ml_mt = counted("ml_cummax_T", 2)
        ml_bc = counted("ml_bcast", 2 * len(MUN))
        ml_ei = counted("ml_exponents", 2 * len(MUN))
        ml_nd = counted("ml_neg_d", 2 * len(MUN))
        ml_ex = counted("ml_exps", 2 * len(MUN))
        ml_d = counted("ml_dmat", 2 * len(MUN))
        ml_qk = counted("ml_qk", 2 * len(MUN))
        ml_sg = counted("ml_sg", 2 * len(MUN))
        ml_num = counted("ml_num", 2 * len(MUN))
        ml_int = counted("ml_inter", 2 * len(MUN))
        ml_hr = counted("ml_h", 2 * len(MUN))
        ml_upd = counted("ml_update", 2 * len(MUN))
        ml_st = counted("ml_state", 2 * len(MUN))
        ml_vw = counted("ml_vw", 2 * len(MUN))
        ml_hn = counted("ml_hn", 2)
        ml_hT = counted("ml_hT", 2)
        ml_y = counted("ml_y", 2)
        br_mm = counted("branches_mm", BRG)
        br_step = counted("merge_step", 2 * BRG)
        br_done = counted("merged", BRG + 2)
        wo_mm = counted("out_mm", KC)
        res1 = counted("residual1", KC)
        n2_sq = counted("n2_squares", KC)
        n2_ac = counted("n2_accumulated", KC - 1)
        n2_mm = counted("n2_summed", 1)
        n2_nt = counted("n2_scaled", KC)
        h2_ready = counted("h2_ready", KC)
        ro_cm = counted("ro_logits", 1)
        ro_cc = counted("ro_logits_copied", 1)
        ro_mm = counted("ro_logits_turned", 1)
        ro_in = counted("ro_biased", 1)
        ro_ei = counted("ro_exp_in", 2)
        ro_ex = counted("ro_exp", 2)
        ro_m = counted("ro_onehots", 1)
        ro_cnt = counted("ro_counts", 1)
        ro_obl = counted("ro_extra", 1)
        ro_ob = counted("ro_bases", 1)
        ro_done = counted("ro_done", 1)
        h2_T = counted("h2_transposed", NTILE)
        h2_row = counted("h2_row", NTILE)
        mo_oh = counted("mo_onehot", E)
        mo_xs = counted("mo_rows", E)
        mo_xk = counted("mo_rows_copied", E)
        mo_xT = counted("mo_xT", E)
        mo_xc = counted("mo_xT_copied", E)
        mo_gu = counted("mo_gate_up", E)
        mo_s = counted("mo_silu", E)
        mo_a = counted("mo_act", E)
        mo_aT = counted("mo_actT", E)
        mo_ac = counted("mo_actT_copied", E)
        mo_d = counted("mo_down", E)
        mo_y = counted("mo_y", E)
        xt_w = apart("xt_weights")
        xt_oh = apart("xt_onehot")
        xt_mm = apart("xt_products")
        xt_act = apart("xt_copies")
        xt_a = apart("xt_act")
        xt_y = apart("xt_y")
        xt_end = sem("further_blocks_done")
        xt_st = apart("xt_stored")
        cb_s = counted("cb_first_weighted", NTILE)
        cb_w = counted("cb_weighted", NTILE)
        cb_T = counted("cb_transposed", NTILE)
        cb_r = counted("residual2", NTILE)
        mo_st = by_buffer("mo_stored", 16 + 32 * (E // 2))
        cb_g = [sem(f"cb_gathered{i}") for i in range(NTILE)]

        T0 = [0, CTX]
        NT = [T, LAT]
        TILES = [list(range(T0[l] // P, NTILE)) for l in range(L)]
        UNITS = [[(h, t) for t in TILES[l] for h in range(H)] for l in range(L)]

        def with_h(l, seg):
            return not (l == 1 and seg == 0)

        base_in = [0, 0]
        base_br = [len(WIN), 0]
        base_in[1] = base_br[0] + BRG + OUTG
        base_br[1] = base_in[1] + len(WIN)

        def rslot(s):
            return ring[:, s * RW:(s + 1) * RW]

        def chunk_no(l, g, c=1):
            return 2 * (l * len(WIN) + g) + c + 1

        def first_group(what):
            return next(g for g, (k, _, _) in enumerate(WIN) if k == what)

        def used(n):
            for l in range(L):
                if base_in[l] <= n < base_in[l] + len(WIN):
                    return dense_full, chunk_no(l, n - base_in[l])
                if base_br[l] <= n < base_br[l] + BRG:
                    return since(br_mm[l], n - base_br[l] + 1)
                if base_br[l] + BRG <= n < base_br[l] + BRG + OUTG:
                    return since(wo_mm[l], 2 * (n - base_br[l] - BRG + 1))

        def fillers(l, u):
            n = 16 // len(UNITS[l])
            return range(u * n, (u + 1) * n)

        def store(eng, blk, buf, s_):
            dst = y_dram[bass.ds(blk, 1), :, :].rearrange("a p (h n) -> (a p) h n", h=2)
            for h in range(2):
                eng.dma_start(dst[:, h, :], buf[64 * h:64 * h + 64, :]).then_inc(s_.sem, 16)

        def wait_alone(eng, s, value):
            eng.wait_ge(s, value)
            eng.sem_inc(s_passed, 1)

        pmods = (bank[3], bank[2], bank[1], bank[0])

        block = stack.enter_context(nc.Block())

        @block.sync
        def _(sp):
            def load(n, src):
                if n >= 2:
                    sp.wait_ge(*used(n - 2))
                sp.dma_start(rslot(n % 2)[:, 0:src.shape[1]], src).then_inc(ring_full[n % 2], 16)

            def row(src, i):
                return src[bass.ds(i, 1), :, :].rearrange("a p n -> (a p) n")

            def expert(l, s, e, full, parts=(0, 1, 2)):
                for i in parts:
                    w, n = ((w_gate, FE), (w_up, FE), (w_down, D))[i]
                    src = w[bass.ds(l * E + e, 1), :, :].rearrange("a (k p) f -> p (a k) f", p=P)
                    sp.dma_start(cut((slotA, slotB)[s], 4096 * i, 4096 // n, n), src).then_inc(full, 16)

            early = slotA[:, 9344:9344 + EARLY_W]
            n = SMALL["c"][1]
            sp.dma_start(small[:, 0:n], small_in[0][:, 0:n]).then_inc(s_head, 16)
            sp.dma_start(consts[:, :], consts_in).then_inc(s_const, 16)
            sp.dma_start(xT.rearrange("p c t -> p (c t)"), xt_in).then_inc(s_x, 16)
            for i in range(MOD_FIRST // 2):
                o = (slotA, slotB)[i // 2][:, (0, 4096)[i // 2] + 2 * RW * (i % 2):][:, 0:2 * RW]
                sp.dma_start(o.rearrange("p (g n) -> p g n", g=2), wmod[2 * i:2 * i + 2].rearrange("g p n -> p g n")).then_inc(first_full[i], 16)
            sp.dma_start(small[:, n:], small_in[0][:, n:]).then_inc(s_small[0].sem, 16)
            for l in range(L):
                if l == 0:
                    for g in range(2):
                        load(base_in[0] + g, win[g])
                for g in range(len(WIN)):
                    if g >= 2:
                        load(base_in[l] + g, win[l * len(WIN) + g])
                    for c in range(2):
                        if (g, c) in MOD_AT[l]:
                            m = MOD_AT[l][g, c]
                            sp.wait_ge(mod_mm, m)
                            sp.dma_start(mring, wmod[m]).then_inc(mod_full, 16)
                    if (l, g) == (0, 1):
                        sp.dma_start(early, early_in[0]).then_inc(s_early[0].sem, 16)
                for s in range(2):
                    load(base_br[l] + s, wbr[l * BRG + s])
                for i in range(1, BRG // 2):
                    for s in range(2):
                        load(base_br[l] + 2 * i + s, wbr[l * BRG + 2 * i + s])
                    if i == 1:
                        sp.wait_ge(*since(ml_y[l], 2 - l))
                    expert(l, 0, 0, e_full[0], (i - 1,))
                for s in range(2):
                    load(base_br[l] + BRG + s, wout[l * OUTG + s])
                sp.wait_ge(*since(br_done[l], BRG + 2))
                for i in range(3):
                    expert(l, 1, 1, e_full[1], (i,))
                    if i + 2 < OUTG:
                        load(base_br[l] + BRG + 2 + i, wout[l * OUTG + 2 + i])
                for s in range(2):
                    sp.sem_inc(mo_st[l][s].sem, 16)
                if l == 0:
                    for g in range(2):
                        load(base_in[1] + g, win[len(WIN) + g])
                    sp.wait_ge(*since(ro_in[l], 1))
                    sp.dma_start(small[:, :], small_in[1]).then_inc(s_small[1].sem, 16)
                sp.wait_ge(*since(ro_done[l], 1))
                with sp.Fori(1, E // 2) as j:
                    for s in range(2):
                        wait_alone(sp, *since(mo_gu[l], 2 * j + (s - 1)))
                        expert(l, s, 2 * j + s, e_full[s], (0, 1))
                        wait_alone(sp, *since(mo_d[l], 2 * j + (s - 1)))
                        expert(l, s, 2 * j + s, e_full[s], (2,))
                        wait_alone(sp, *since(mo_y[l], 2 * j + (s - 1)))
                        store(sp, 2 * j + (s - 2), yS[s], mo_st[l][s])
                sp.wait_ge(*since(mo_y[l], E - 1))
                store(sp, E - 2, yS[0], mo_st[l][0])
                n = sp.value_load(ownI[0:1, XBLK[l]:XBLK[l] + 1], min_val=0, max_val=XBLK[l])
                with sp.If(n > 0):
                    with sp.Fori(0, n) as b:
                        e = sp.value_load(ownI[0:1, bass.ds(b, 1)], min_val=0, max_val=E - 1)
                        wait_alone(sp, *since(xt_mm[l], 5 * b))
                        expert(l, 0, e, xt_w[l].sem)
                with sp.Else():
                    sp.nop()
                sp.wait_ge(*since(mo_y[l], E))
                store(sp, E - 1, yS[1], mo_st[l][1])
                if l == 0:
                    sp.wait_ge(xt_end, 1)
                    sp.wait_ge(cb_g[NTILE - 1], 32)
                if l == 0:
                    sp.dma_start(early, early_in[1]).then_inc(s_early[1].sem, 16)
            for c in range(2):
                sp.wait_ge(f_out, KC // 2 * (c + 1))
                n = KC // 2 * LAT
                sp.dma_start(out[:, c * n:(c + 1) * n], fin[:, c * n:(c + 1) * n]).then_inc(s_out, 16)
            sp.wait_ge(s_out, 32)

        @block.tensor
        def _(pe):
            dense = [0]
            unturned = []

            def mm(o, a, b, start=True, stop=True):
                return nc.tensor.matmul(o, a, b, start=start, stop=stop)

            def tr(o, a, p0=0):
                return nc.tensor.transpose(o, a, ident[p0:p0 + a.shape[0], p0:p0 + a.shape[0]])

            def mod_parts(w, pmod):
                for k2 in range(2):
                    for j in range(4):
                        last = mm(pmod[32 * j:32 * j + 32, 0:COLS], csil[:, 2 * j + k2, :], w[:, 2 * j + k2, :],
                                  start=k2 == 0, stop=k2 == 1)
                last.then_inc(mod_mm, 1)

            def mod_turn(m):
                pmod = pmods[m % 4 if m < MOD_FIRST else 0]
                for c in range(2):
                    last = mm(pmod[:, COLS + 2 * c:COLS + 2 * c + 2], mraw[m % 2][:, P * c:P * c + P], const("sel"))
                last.then_inc(mod_t, 1)

            def mod_turn_pending():
                if unturned:
                    m = unturned.pop()
                    pe.wait_ge(mod_ev, m + 1)
                    mod_turn(m)

            def dense_chunk(l, g, c):
                what, _, _ = WIN[g]
                pos = base_in[l] + g
                w = cut(rslot(pos % 2), 0, KC, COLS)
                t0 = 0 if what in "kxv" else T0[l]
                if c == 0:
                    pe.wait_ge(ring_full[pos % 2], 16 * (pos // 2 + 1))
                d = dense[0]
                dense[0] += 1
                if d >= 2:
                    pe.wait_ge(dense_out, d - 1)
                b = bank[d % 2]
                if what in ("v", "bv"):
                    tiles = list(range(t0 // P, NTILE))
                    n = len(tiles) // 2
                    for i, t in enumerate(tiles[n * c:n * c + n]):
                        for k in range(KC):
                            last = mm(b[:, COLS * i:COLS * (i + 1)], hT[:, k, P * t:P * t + P], w[:, k, :],
                                      start=k == 0, stop=k == KC - 1)
                else:
                    for k in range(KC):
                        if g == c == 0:
                            pe.wait_ge(*since(h_ready[l], k + 1))
                        last = mm(b[:, 0:T - t0], w[:, k, P * c:P * c + P], hT[:, k, t0:T], start=k == 0, stop=k == KC - 1)
                last.then_inc(dense_full, 1)
                mod_turn_pending()
                if (g, c) in MOD_AT[l]:
                    m = MOD_AT[l][g, c]
                    pe.wait_ge(mod_full, 16 * (m - MOD_FIRST + 1))
                    pe.wait_ge(mod_out, m)
                    mod_parts(cut(mring, 0, KC, COLS), pmod)
                    unturned.append(m)

            def rope(l, i):
                pe.wait_ge(dense_out, chunk_no(l, first_group("k" if i < WC else "q") + i % WC // 2, i % 2))
                if i >= 2:
                    pe.wait_ge(*since(kq_done[l], i - 1))
                elif l > 0:
                    pe.wait_ge(*since(h_ready[l], KC))
                mm(bank[4 + i % 2][:, 0:LAT], const("rot"), (kT if i < WC else qT)[:, i % WC, CTX:T]).then_inc(rope_mm[l].sem, 1)

            def norm(acc, n, b, accumulated, done):
                pe.wait_ge(*since(accumulated, KC - 1))
                mm(b[:, 0:n], ones, acc, start=True, stop=True).then_inc(done.sem, 1)

            def gmlp(l):
                pe.wait_ge(*since(s_small[l], 16))
                pe.wait_ge(*since(bv_done[l], len(TILES[l])))
                pe.wait_ge(*since(kq_done[l], 2 * WC))
                ws = par("w_sT", WC, P)
                for g in range(WC):
                    if g >= 2:
                        pe.wait_ge(*since(yb_done[l], g - 1))
                    for i, t in enumerate(TILES[l]):
                        last = mm(bank[4 + g % 2][:, P * i:P * i + P], vG[:, t, P * g:P * g + P], ws[:, g, :])
                    last.then_inc(mixg_mm[l].sem, 1)

            def att_scores(l, u):
                h, t = UNITS[l][u]
                keys = CTX if t < 2 else T
                if u == 0:
                    pe.wait_ge(*since(yb_done[l], WC))
                    pe.wait_ge(*since(kq_done[l], 2 * WC))
                else:
                    pe.wait_ge(*since(at_exp[l], 2 * u))
                for m in range(2):
                    r = slice(64 * m, 64 * m + 64)
                    last = mm(bank[4 + m][:, 0:keys], qT[r, h, P * t:P * t + P], kT[r, h, 0:keys])
                last.then_inc(at_s[l].sem, 1)

            def att_trans(l, u):
                h, t = UNITS[l][u]
                pe.wait_ge(*since(at_a[l], u + 1))
                if u >= 1:
                    pe.wait_ge(*since(at_aT[l], u))
                for i in range(2 if t < 2 else NTILE):
                    last = tr(bank[6][:, P * i:P * i + P], attw[:, P * i:P * i + P])
                last.then_inc(at_T[l].sem, 1)

            def att_out(l, u):
                h, t = UNITS[l][u]
                n = 2 if t < 2 else NTILE
                pe.wait_ge(*since(at_aT[l], u + 1))
                if u >= 1:
                    pe.wait_ge(*since(at_on[l], u))
                for i in range(n):
                    last = mm(bank[7][:, 0:P], attT[:, i, :], vA[:, i, P * h:P * h + P], start=i == 0, stop=i == n - 1)
                last.then_inc(at_o[l].sem, 1)

            def att_oT(l, i):
                pe.wait_ge(*since(at_nd[l], i + 1))
                if i >= 1:
                    pe.wait_ge(*since(at_y[l], i))
                for h in range(H):
                    last = tr(bank[2][:, P * h:P * h + P], oN[:, h, :])
                last.then_inc(at_oT[l].sem, 1)

            def ml_features(l, seg):
                wq = par("w_qkv", 3 * WC, P)
                sl = slice(256 * seg, 256 * seg + 256)
                jobs = [(s, src, h) for s, src in ((0, xc), (1, xc), (2, xm)) for h in (0, 2)]
                jobs += [(s, src, -1 - i) for i in range(2) for s, src in ((1, xc), (2, xm))]
                if seg == 0:
                    pe.wait_ge(*since(at_exp[l], 2 * len(UNITS[l])))
                    pe.wait_ge(*since(at_aT[l], len(UNITS[l])))
                    pe.wait_ge(*since(at_on[l], len(UNITS[l])))
                    pe.wait_ge(*since(xc_done[l], 1))
                else:
                    pe.wait_ge(*since(ml_st[l], 4))
                for i, (s, src, h) in enumerate(jobs):
                    if i == 4 and seg == 0:
                        att_oT(l, len(UNITS[l]) // H - 1)
                    if i >= 4:
                        if i - 4 < NFA:
                            pe.wait_ge(*since(ml_fa[l], seg * NFA + i - 3))
                        else:
                            pe.wait_ge(*since(ml_fe[l], seg * (NF - NFA) + i - 3 - NFA))
                    b = bank[4 + i % 4]
                    for k in range(2 if h >= 0 else WC):
                        if h >= 0:
                            last = mm(b[:, 256 * k:256 * k + 256], wq[:, s * WC + h + k, :], src[:, h + k, sl])
                        else:
                            t = 256 * seg + P * (-1 - h)
                            last = mm(b[:, P * k:P * k + P], src[:, k, t:t + P], wq[:, s * WC + k, :])
                    last.then_inc(ml_ff[l].sem, 1)

            def ml_gates(l, seg):
                wif = par("w_if", 3 * WC, 16)
                pe.wait_ge(*since(ml_fa[l], NFA * (seg + 1)))
                pe.wait_ge(*since(ml_fe[l], (NF - NFA) * seg + 2))
                for i, f in enumerate((mq, mk, mv)):
                    for h in range(WC):
                        last = mm(bank[7][0:16, 0:256], wif[:, WC * i + h, :], f[:, h, :],
                                  start=(i, h) == (0, 0), stop=(i, h) == (2, WC - 1))
                last.then_inc(ml_gc[l].sem, 1)
                if seg == 0:
                    pe.wait_ge(*since(at_y[l], len(TILES[l])))
                elif with_h(l, 0):
                    pe.wait_ge(*since(ml_y[l], 1))
                pe.wait_ge(*since(ml_gr[l], seg + 1))
                for t in range(2):
                    last = tr(bank[2][:, 16 * t:16 * t + 16], grow[:, P * t:P * t + P])
                last.then_inc(ml_gm[l].sem, 1)

            def ml_cumulate(l, seg):
                pe.wait_ge(*since(ml_lf[l], seg + 1))
                for d, tri in enumerate(("tri_f", "tri_b")):
                    mm(bank[2][:, 32 + 8 * d:40 + 8 * d], const(tri), mlf[:, :, d, :])
                mm(bank[2][:, 48:64], ones, mlf.rearrange("p a b c -> p (a b c)")).then_inc(ml_cs[l].sem, 1)
                pe.wait_ge(*since(ml_r[l], seg + 1))
                for d in range(2):
                    last = tr(bank[2][0:8, P * (d + 1):P * (d + 2)], mr[:, d, :, :].rearrange("p a b -> p (a b)"))
                last.then_inc(ml_rT[l].sem, 1)

            def ml_max_turn(l, seg):
                pe.wait_ge(*since(ml_cm[l], seg + 1))
                for d in range(2):
                    last = tr(bank[2][:, 64 + 8 * d:72 + 8 * d], cm_at(1, d))
                last.then_inc(ml_mt[l].sem, 1)

            def ml_open(l, seg, w):
                d, t = MUN[w]
                n, nh = 4 * seg + w, 4 * (seg - l) + w
                if w == 0:
                    pe.wait_ge(*since(ml_fe[l], (NF - NFA) * (seg + 1)))
                    pe.wait_ge(*since(ml_cm[l], seg + 1))
                elif with_h(l, seg):
                    pe.wait_ge(*since(ml_nd[l], nh))
                else:
                    pe.wait_ge(*since(ml_ei[l], n))
                for h in range(H):
                    r = t * H + h
                    last = mm(bank[4][:, P * h:P * h + P], ident[0:8, r:r + 1].to_broadcast([8, P]), cm_at(1, d))
                last.then_inc(ml_bc[l].sem, 1)
                if with_h(l, seg):
                    if w > 0:
                        pe.wait_ge(*since(ml_sg[l], nh))
                    for h in range(H):
                        last = mm(bank[5][:, P * h:P * h + P], mk[:, h, P * t:P * t + P], mq[:, h, P * t:P * t + P])
                    last.then_inc(ml_qk[l].sem, 1)

            def ml_unit(l, seg, w):
                d, t = MUN[w]
                n, nh = 4 * seg + w, 4 * (seg - l) + w
                s = sg[w % 2]
                if n >= 1:
                    pe.wait_ge(*since(ml_st[l], n))
                else:
                    pe.wait_ge(mod_out, MOD_FIRST + sum(len(MOD_AT[i]) for i in range(l + 1)))
                if with_h(l, seg):
                    pe.wait_ge(*since(ml_sg[l], nh + 1))
                    for h in range(H):
                        mm(num_ps[h], s[:, h, :], mvt[:, t, h, :])
                    for h in range(H):
                        last = mm(inter_ps[h], mq[:, h, P * t:P * t + P], state[:, d, h, :])
                    last.then_inc(ml_num[l].sem, 1)
                pe.wait_ge(*since(ml_vw[l], n + 1))
                for h in range(H):
                    last = mm(upd_ps[h], mkt[:, t, h, :], vw[w % 2][:, h, :])
                last.then_inc(ml_upd[l].sem, 1)

            def ml_turn(l, seg):
                pe.wait_ge(*since(ml_hn[l], seg - l + 1))
                for t in range(2):
                    for h in range(H):
                        last = tr(bank[2 + t][:, P * h:P * h + P], hn[:, t, h, :])
                last.then_inc(ml_hT[l].sem, 1)

            def route(l):
                wr = par("w_route", KC, GROUPS + E)
                nr = GROUPS + E
                for k in range(KC):
                    pe.wait_ge(*since(h2_ready[l], k + 1))
                    last = mm(bank[0][0:nr, 0:NT[l]], wr[:, k, :], hT[:, k, T0[l]:T], start=k == 0, stop=k == KC - 1)
                last.then_inc(ro_cm[l].sem, 1)
                pe.wait_ge(*since(ro_cc[l], 1))
                for i in range(len(TILES[l])):
                    last = tr(bank[1][:, nr * i:nr * i + nr], lgT[:, P * i:P * i + P])
                last.then_inc(ro_mm[l].sem, 1)

            def h2_rows(l):
                for i, t in enumerate(TILES[l]):
                    if i >= 2:
                        pe.wait_ge(*since(h2_row[l], i - 1))
                    for k in range(KC):
                        last = tr(psum[:, 512 * (4 + 2 * (i % 2)) + P * k:512 * (4 + 2 * (i % 2)) + P * (k + 1)],
                                  hT[:, k, P * t:P * t + P])
                    last.then_inc(h2_T[l].sem, 1)

            def positions(l):
                n = len(TILES[l])
                m = ro["m"][l]
                pe.wait_ge(*since(ro_m[l], 1))
                for i in range(n):
                    for k in range(i):
                        mm(bank[1][:, E * i:E * i + E], ones, m[:, k, :], start=k == 0, stop=False)
                    mm(bank[1][:, E * i:E * i + E], const("tri_x"), m[:, i, :], start=i == 0, stop=True)
                for i in range(n):
                    last = mm(bank[1][0:E, 256:257], m[:, i, :], ones[:, 0:1], start=i == 0, stop=i == n - 1)
                last.then_inc(ro_cnt[l].sem, 1)
                pe.wait_ge(*since(ro_obl[l], 1))
                o = ro["obl"][l].to_broadcast([E, P])
                mm(bank[2][:, 0:E], o, const("tri_x", E)[:, 0:E])
                mm(bank[2][:, E:2 * E], o, const("tri_f", E)[:, 0:E]).then_inc(ro_ob[l].sem, 1)

            def moe_rows(l, s, done_):
                n = len(TILES[l])
                for i, t in enumerate(TILES[l]):
                    for half in range(2):
                        last = mm(bank[5][64 * half:64 * half + 64, :], onehot[s][:, i, :],
                                  hT[:, 4 * half:4 * half + 4, P * t:P * t + P], start=i == 0, stop=i == n - 1)
                last.then_inc(done_.sem, 1)

            def moe_x(done_):
                for c in range(KC // 2):
                    last = tr(bank[0][:, P * c:P * c + P], xrow[:, P * c:P * c + P])
                last.then_inc(done_.sem, 1)

            def moe_gate_up(s, wA, done_):
                for k in range(KC):
                    for half in range(2):
                        last = mm(bank[1][64 * half:64 * half + 64, :], xgT[s][:, k, :], cut(wA, 4096 * half, KC, FE)[:, k, :],
                                  start=k == 0, stop=k == KC - 1)
                last.then_inc(done_.sem, 1)

            def moe_turn(s, done_):
                for k in range(FE // P):
                    last = tr(bank[2][:, BLK * k:BLK * k + BLK], act_[s][64:128, P * k:P * k + P], 64)
                last.then_inc(done_.sem, 1)

            def moe_down(s, wA, done_):
                dn = cut(wA, 8192, FE // P, D)
                for k in range(FE // P):
                    for half in range(2):
                        last = mm(bank[3 + s][64 * half:64 * half + 64, :], aT[s][:, k, :], dn[:, k, 512 * half:512 * half + 512],
                                  start=k == 0, stop=k == FE // P - 1)
                last.then_inc(done_.sem, 1)

            def moe(l):
                pe.wait_ge(*since(h2_row[l], len(TILES[l])))
                pe.wait_ge(*since(mo_oh[l], 1))
                moe_rows(l, 0, mo_xs[l])
                pe.wait_ge(*since(mo_xk[l], 1))
                moe_x(mo_xT[l])

                def pair(j, last):
                    for s in range(2):
                        e = 2 * j + s
                        w = (slotA, slotB)[s]
                        pe.wait_ge(e_full[s], 48 * j + (48 + l * 24 * E))
                        wait_alone(pe, *since(mo_xc[l], e + 1))
                        moe_gate_up(s, w, mo_gu[l])
                        if not (last and s == 1):
                            wait_alone(pe, *since(mo_oh[l], e + 2))
                            moe_rows(l, 1 - s, mo_xs[l])
                        wait_alone(pe, *since(mo_a[l], e + 1))
                        moe_turn(s, mo_aT[l])
                        if not (last and s == 1):
                            wait_alone(pe, *since(mo_xk[l], e + 2))
                            moe_x(mo_xT[l])
                        wait_alone(pe, *since(mo_ac[l], e + 1))
                        moe_down(s, w, mo_d[l])
                with pe.Fori(0, E // 2 - 1) as j:
                    pair(j, False)
                pair(E // 2 - 1, True)
                pe.wait_ge(*since(ro_done[l], 1))
                n = pe.value_load(ownI[0:1, XBLK[l]:XBLK[l] + 1], min_val=0, max_val=XBLK[l])
                pe.wait_ge(*since(mo_y[l], E - 1))
                with pe.If(n > 0):
                    with pe.Fori(0, n) as b:
                        wait_alone(pe, *since(xt_oh[l], b + 1))
                        moe_rows(l, 0, xt_mm[l])
                        wait_alone(pe, *since(xt_act[l], 4 * b + 1))
                        moe_x(xt_mm[l])
                        pe.wait_ge(*since(xt_w[l], 48 * b + 48))
                        wait_alone(pe, *since(xt_act[l], 4 * b + 2))
                        moe_gate_up(0, slotA, xt_mm[l])
                        wait_alone(pe, *since(xt_a[l], b + 1))
                        moe_turn(0, xt_mm[l])
                        wait_alone(pe, *since(xt_act[l], 4 * b + 4))
                        moe_down(0, slotA, xt_mm[l])
                with pe.Else():
                    pe.nop()
                if l == 0:
                    pe.sem_inc(xt_end, 1)

            def combine(l):
                n = len(TILES[l])
                sq, summed = ((n1_sq[1], n1_mm[1].sem), (f_sq[0], f_mm))[l]

                def sums(i):
                    pe.wait_ge(*since(sq, i + 1))
                    for c in range(KC):
                        last = mm(bank[i][:, 0:P], ones, tsq[i % 2][:, c, :], start=c == 0, stop=c == KC - 1)
                    last.then_inc(summed, 1)
                for i in range(n):
                    pe.wait_ge(*since(cb_w[l], i + 1))
                    if i >= 2:
                        pe.wait_ge(*since(cb_r[l], i - 1))
                    for k in range(KC):
                        o = 512 * (4 + 2 * (i % 2)) + P * k
                        last = tr(psum[:, o:o + P], fw[i % 2][:, P * k:P * k + P])
                    last.then_inc(cb_T[l].sem, 1)
                    if i >= 2:
                        sums(i - 2)
                for i in range(n - 2, n):
                    sums(i)

            pe.wait_ge(s_const, 16)
            norm(nbuf1[:, 0:T], T, bank[7], n1_ac[0], n1_mm[0])
            pe.wait_ge(s_c, 1)
            pe.wait_ge(s_zero, 1)
            for m in range(MOD_FIRST):
                if m % 2 == 0:
                    pe.wait_ge(first_full[m // 2], 16)
                if m >= 4:
                    pe.wait_ge(mod_out, m - 3)
                mod_parts(first_mods[m], pmods[m % 4])
                mod_turn_pending()
                unturned.append(m)
            mod_turn_pending()
            for l in range(L):
                for g in range(NDENSE):
                    for c in range(2):
                        dense_chunk(l, g, c)
                    if g == first_group("x") + 1:
                        for i in range(WC):
                            rope(l, i)
                    if g == first_group("u") + 1:
                        for i in range(WC, 2 * WC):
                            rope(l, i)
                gmlp(l)
                nu = len(UNITS[l])
                att_scores(l, 0)
                for u in range(nu):
                    for i in fillers(l, u):
                        dense_chunk(l, NDENSE + i // 2, i % 2)
                    att_trans(l, u)
                    if u + 1 < nu:
                        att_scores(l, u + 1)
                    if u >= H and u % H == 0:
                        att_oT(l, u // H - 1)
                    att_out(l, u)
                gate = 16
                for seg in range(2):
                    ml_features(l, seg)
                    if seg == 1 and with_h(l, 0):
                        ml_turn(l, 0)
                    ml_gates(l, seg)
                    dense_chunk(l, NDENSE + gate // 2, gate % 2)
                    gate += 1
                    ml_cumulate(l, seg)
                    dense_chunk(l, NDENSE + gate // 2, gate % 2)
                    gate += 1
                    ml_max_turn(l, seg)
                    for w in range(5):
                        if w < 4:
                            ml_open(l, seg, w)
                        if w > 0:
                            ml_unit(l, seg, w - 1)
                        if w in ML_FILL:
                            dense_chunk(l, NDENSE + gate // 2, gate % 2)
                            gate += 1
                mod_turn_pending()
                t0 = T0[l]

                def branch(s, bs):
                    w = cut(rslot(s), 0, 3 * WC, P)
                    for b in bs:
                        y = (yaT, uT, zT)[b]
                        for k in range(WC):
                            last = mm(bank[BRB[s][b]][:, 0:NT[l]], w[:, WC * b + k, :], y[:, k, t0:T],
                                      start=k == 0, stop=k == WC - 1)
                    return last
                pe.wait_ge(*since(ml_sg[l], 4 * (2 - l)))
                pe.wait_ge(dense_out, dense[0])
                pe.wait_ge(*since(at_y[l], len(TILES[l])))
                for s in range(2):
                    pe.wait_ge(ring_full[s], 16 + 8 * base_br[l])
                    branch(s, (0, 1))
                ml_turn(l, 1)
                pe.wait_ge(*since(ml_y[l], 2 - l))
                pe.wait_ge(*since(br_done[l], 2))
                for s in range(2):
                    branch(s, (2,)).then_inc(br_mm[l].sem, 1)
                with pe.Fori(1, BRG // 2) as j:
                    for s in range(2):
                        pe.wait_ge(ring_full[s], 16 * j + (16 + 8 * base_br[l]))
                        pe.wait_ge(*since(br_done[l], 2 * j + (s + 1)))
                        branch(s, (0, 1, 2)).then_inc(br_mm[l].sem, 1)
                pe.wait_ge(*since(br_done[l], BRG + 2))
                for c in range(KC):
                    n = base_br[l] + BRG + c // 2
                    if c % 2 == 0:
                        pe.wait_ge(ring_full[n % 2], 16 * (n // 2 + 1))
                    if c >= 4:
                        pe.wait_ge(*since(res1[l], c - 3))
                    w = cut(rslot(n % 2), 0, KC, COLS)
                    for k in range(KC):
                        last = mm(bank[4 + c % 4][:, 0:NT[l]], w[:, k, P * (c % 2):P * (c % 2) + P], hT[:, k, t0:T],
                                  start=k == 0, stop=k == KC - 1)
                    last.then_inc(wo_mm[l].sem, 1)
                norm(nbuf2[:, 1536:1536 + NT[l]], NT[l], bank[3], n2_ac[l], n2_mm[l])
                route(l)
                h2_rows(l)
                positions(l)
                moe(l)
                combine(l)
        @block.scalar
        def _(act):
            step = [0]
            count = {}
            copied = [0]
            roots = [0]

            def fn(o, i, f, bias=0.0, scale=1.0, accum=None):
                return nc.scalar.activation(o, i, f, bias=bias, scale=scale, accum_out=accum)

            def done(ins, s):
                ins.then_inc(s, 1)
                count[s.name] = count.get(s.name, 0) + 1
                act.wait_ge(s, count[s.name])

            def link(ins):
                step[0] += 1
                ins.then_inc(act_step, 1)
                act.wait_ge(act_step, step[0])

            def root(v):
                roots[0] += 1
                act.wait_ge(rms_in, roots[0])
                done(fn(v, v, ACT.Sqrt), rms_out)

            def dense_copy(l, g, c):
                what, _, gi = WIN[g]
                d = copied[0]
                copied[0] += 1
                b = bank[d % 2]
                t0 = 0 if what in "kxv" else T0[l]
                act.wait_ge(dense_full, d + 1)
                if what in ("v", "bv"):
                    tiles = list(range(t0 // P, NTILE))
                    n = len(tiles) // 2
                    a = tiles[n * c]
                    o = (vA if what == "v" else vG)[:, a:a + n, COLS * gi:COLS * gi + COLS]
                    i = cut(b, 0, n, COLS)
                else:
                    j = 2 * gi + c
                    o = {"k": kT, "q": qT, "x": xm, "u": uT, "z": zT, "gate": gates}[what][:, j, t0:T]
                    i = b[:, 0:T - t0]
                f, s = {"u": (ACT.Gelu_apprx_tanh, 1.0), "bv": (ACT.Gelu_apprx_tanh, 1.0), "z": (ACT.Tanh, 0.5),
                        "gate": (ACT.Tanh, 0.5)}.get(what, (ACT.Copy, 1.0))
                done(fn(o, i, f, scale=s), dense_out)

            unstored = []

            def mod_store_pending():
                if unstored:
                    m = unstored.pop()
                    act.wait_ge(mod_t, m + 1)
                    k = 2 * (m % MODG)
                    done(fn(modT[:, m // MODG, k:k + 2, :], cut(pmods[m % 4 if m < MOD_FIRST else 0], COLS, 2, 2), ACT.Copy), mod_out)

            def chunk(l, g, c):
                dense_copy(l, g, c)
                mod_store_pending()
                if (g, c) in MOD_AT[l]:
                    m = MOD_AT[l][g, c]
                    act.wait_ge(mod_mm, m + 1)
                    done(fn(mraw[m % 2], pmod[:, 0:COLS], ACT.Copy), mod_ev)
                    unstored.append(m)

            def squares(buf, n_buf, t0, t1, accumulated, out, ready=None):
                n = t1 - t0
                for c in range(KC):
                    if ready:
                        act.wait_ge(*since(ready, c + 1))
                    if c >= n_buf:
                        act.wait_ge(*since(accumulated, max(c - n_buf, 1)))
                    done(fn(cut(buf, 512 * (c % n_buf), n), xT[:, c, t0:t1], ACT.Square, scale=D ** -0.5), out.sem)
                root(trs if buf is slotB else cut(buf, 1024, n))

            def weights_and_squares(l, sq, summed):
                n = len(TILES[l])

                def weight(i):
                    act.wait_ge(cb_g[TILES[l][i]], 32 * (l + 1))
                    if i >= 2:
                        act.wait_ge(*since(cb_T[l], i - 1))
                    done(fn(fw[i % 2], yg[i][:, 0, :], ACT.Copy, scale=ro["wt"][l][:, 0, i:i + 1]), cb_s[l].sem)
                weight(0)
                for i, t in enumerate(TILES[l]):
                    if i + 1 < n:
                        weight(i + 1)
                    act.wait_ge(*since(cb_r[l], i + 1))
                    if i >= 2:
                        act.wait_ge(summed[0], summed[1] + i - 1)
                    done(fn(tsq[i % 2], xT[:, :, P * t:P * t + P], ACT.Square, scale=D ** -0.5), sq)
                root(trs[:, 0:P * (n - 1)])
                root(trs[:, P * (n - 1):P * n])

            def modulate(t0, t1, scaled, ready, shift, factor):
                for c in range(KC):
                    act.wait_ge(*since(scaled, c + 1))
                    for w in range(2):
                        a, b = max(t0, 256 * w), 256 * (w + 1)
                        if a < b:
                            last = fn(hT[:, c, a:b], hT[:, c, a:b], ACT.Identity, bias=shift[:, c, w:w + 1], scale=factor[:, c, w:w + 1])
                    done(last, ready.sem)

            def attention_exp(l, u):
                h, t = UNITS[l][u]
                keys = CTX if t < 2 else T
                act.wait_ge(*since(at_nb[l], u + 1))
                if u >= 1:
                    act.wait_ge(*since(at_a[l], u))
                for m in range(2):
                    done(fn(probs[:, m, 0:keys], bank[4 + m][:, 0:keys], ACT.Exp, bias=nbias[:, m:m + 1], scale=SCALE,
                       accum=psum_[:, m:m + 1]), at_exp[l].sem)

            def attention_T(l, u):
                h, t = UNITS[l][u]
                n = 2 if t < 2 else NTILE
                act.wait_ge(*since(at_T[l], u + 1))
                if u >= 1:
                    act.wait_ge(*since(at_o[l], u))
                done(fn(attT[:, 0:n, :], cut(bank[6], 0, n, P), ACT.Copy), at_aT[l].sem)

            def attention_square(l, u):
                act.wait_ge(*since(at_o[l], u + 1))
                h = UNITS[l][u][0]
                done(fn(osq, bank[7][:, 0:P], ACT.Square, scale=DV ** -0.5, accum=oss[:, h:h + 1]), at_sq[l].sem)
                if h == H - 1:
                    root(orms)

            def attention_y(l, i):
                t = TILES[l][i]
                act.wait_ge(*since(at_oT[l], i + 1))
                if i == 0:
                    act.wait_ge(*since(mixg_mm[l], WC))
                done(fn(yaT[:, :, P * t:P * t + P], cut(bank[2], 0, H, P), ACT.Copy, scale=gvec[:, 0:1]), at_y[l].sem)

            def ml_features(l, seg):
                for i in range(NFA):
                    act.wait_ge(*since(ml_ff[l], seg * NF + i + 1))
                    done(fn((mq, mk, mv)[i // 2][:, 2 * (i % 2):2 * (i % 2) + 2, :], cut(bank[4 + i % 4], 0, 2, 256), ACT.Copy), ml_fa[l].sem)

            def ml_logf(l, seg):
                act.wait_ge(*since(ml_ga[l], seg + 1))
                link(fn(mtmp, mtmp, ACT.Exp, scale=-1.0))
                done(fn(mtmp, mtmp, ACT.Ln, bias=1.0), ml_gl[l].sem)

            def ml_unit(l, seg, w):
                d, t = MUN[w]
                n, nh = 4 * seg + w, 4 * (seg - l) + w
                act.wait_ge(*since(ml_ei[l], n + 1))
                done(fn(mee[w % 2], mex, ACT.Exp), ml_ex[l].sem)
                if with_h(l, seg):
                    act.wait_ge(*since(ml_nd[l], nh + 1))
                    s = sg[w % 2]
                    for h in range(H):
                        last = fn(s[:, h, :], s[:, h, :], ACT.Exp, bias=mr[:, d, t, h:h + 1], scale=-1.0)
                    done(last, ml_d[l].sem)

            def ml_inter(l, seg, w):
                nh = 4 * (seg - l) + w
                act.wait_ge(*since(ml_num[l], nh + 1))
                act.wait_ge(*since(ml_upd[l], 4 * seg + w + 1))
                for h in range(H):
                    last = fn(inter[:, h, :], inter_ps[h], ACT.Copy, scale=mee[w % 2][:, 2, h:h + 1])
                done(last, ml_int[l].sem)

            def moe_rows(done_):
                fn(xrow, bank[5], ACT.Copy).then_inc(done_.sem, 1)

            def moe_x(s, done_):
                fn(xgT[s].rearrange("p (h c) n -> p c h n", h=2), cut(bank[0], 0, KC // 2, 2, BLK), ACT.Copy).then_inc(done_.sem, 1)

            def moe_silu(s, done_):
                fn(gs[s][64:128, :], bank[1][0:64, :], ACT.Silu).then_inc(done_.sem, 1)

            def moe_turned(s, done_):
                fn(aT[s], cut(bank[2], 0, FE // P, BLK), ACT.Copy).then_inc(done_.sem, 1)

            act.wait_ge(s_head, 16)
            done(fn(csil[:, :, 0:2], par("c", KC, 2), ACT.Silu), s_c)
            act.wait_ge(s_x, 16)
            squares(nbuf1, KC, 0, T, n1_ac[0], n1_sq[0])
            for m in range(MOD_FIRST):
                act.wait_ge(mod_mm, m + 1)
                done(fn(mraw[m % 2], pmods[m % 4][:, 0:COLS], ACT.Copy), mod_ev)
                mod_store_pending()
                unstored.append(m)
            mod_store_pending()
            for l in range(L):
                act.wait_ge(*since(n1_f[l], 1))
                modulate(0, T, n1_nt[l], h_ready[l], modT[:, l, 0:KC, :], normA)
                for g in range(NDENSE):
                    for c in range(2):
                        chunk(l, g, c)
                    if g == first_group("q") + 1:
                        act.wait_ge(*since(conv_done[l], 1))
                        done(fn(xc.rearrange("p c t -> p (c t)"), xc.rearrange("p c t -> p (c t)"), ACT.Silu), xc_done[l].sem)
                    if g == first_group("bv") + 1:
                        act.wait_ge(dense_out, copied[0])
                        for i, t in enumerate(TILES[l]):
                            done(fn(attw, vG[:, t, :], ACT.Square, scale=W ** -0.5, accum=ssq[:, t:t + 1]), bv_sq[l].sem)
                        root(rst[:, TILES[l][0]:NTILE])
                act.wait_ge(*since(lam_in[l], 1))
                done(fn(lamv[:, 2:4], lamv[:, 0:2], ACT.Exp), lam_ex[l].sem)
                nu = len(UNITS[l])
                for u in range(nu):
                    attention_exp(l, u)
                    for i in fillers(l, u):
                        chunk(l, NDENSE + i // 2, i % 2)
                    attention_T(l, u)
                    if u >= H and u % H == 0:
                        attention_y(l, u // H - 1)
                    attention_square(l, u)
                attention_y(l, nu // H - 1)
                gate = 16
                for seg in range(2):
                    ml_features(l, seg)
                    act.wait_ge(*since(ml_gc[l], seg + 1))
                    done(fn(grow, bank[7][0:16, 0:256], ACT.Copy), ml_gr[l].sem)
                    ml_logf(l, seg)
                    for i in range(2):
                        chunk(l, NDENSE + gate // 2, gate % 2)
                        gate += 1
                    for w in range(5):
                        if w < 4:
                            ml_unit(l, seg, w)
                        if w > 0 and with_h(l, seg):
                            ml_inter(l, seg, w - 1)
                        if w in ML_FILL:
                            chunk(l, NDENSE + gate // 2, gate % 2)
                            gate += 1
                    if with_h(l, seg):
                        root(hss)
                mod_store_pending()
                act.wait_ge(*since(br_done[l], BRG + 2))
                squares(nbuf2, 2, T0[l], T, n2_ac[l], n2_sq[l], res1[l])
                modulate(T0[l], T, n2_nt[l], h2_ready[l], modT[:, l, 3 * KC:4 * KC, :], normA)
                act.wait_ge(*since(ro_cm[l], 1))
                done(fn(lgT[:, 0:NT[l]], bank[0][0:GROUPS + E, 0:NT[l]], ACT.Copy), ro_cc[l].sem)
                for i, t in enumerate(TILES[l]):
                    act.wait_ge(*since(h2_T[l], i + 1))
                    b = 4 + 2 * (i % 2)
                    done(fn(hT[:, :, P * t:P * t + P], cut(psum, 512 * b, KC, P), ACT.Copy), h2_row[l].sem)
                act.wait_ge(*since(ro_ei[l], 1))
                done(fn(ro["ge"][l], ro["ge"][l], ACT.Exp), ro_ex[l].sem)
                act.wait_ge(*since(ro_ei[l], 2))
                done(fn(ro["e2"][l], ro["e2"][l], ACT.Exp), ro_ex[l].sem)
                act.wait_ge(*since(mo_xs[l], 1))
                moe_rows(mo_xk[l])
                act.wait_ge(*since(mo_xT[l], 1))
                moe_x(0, mo_xc[l])
                act.wait_ge(*since(ro_done[l], 1))

                def pair(j, last):
                    for s in range(2):
                        e = 2 * j + s
                        act.wait_ge(*since(mo_gu[l], e + 1))
                        moe_silu(s, mo_s[l])
                        if not (last and s == 1):
                            act.wait_ge(*since(mo_xs[l], e + 2))
                            moe_rows(mo_xk[l])
                        act.wait_ge(*since(mo_aT[l], e + 1))
                        moe_turned(s, mo_ac[l])
                        if not (last and s == 1):
                            act.wait_ge(*since(mo_xT[l], e + 2))
                            moe_x(1 - s, mo_xc[l])
                with act.Fori(0, E // 2 - 1) as j:
                    pair(j, False)
                pair(E // 2 - 1, True)
                act.wait_ge(*since(ro_done[l], 1))
                n = act.value_load(ownI[0:1, XBLK[l]:XBLK[l] + 1], min_val=0, max_val=XBLK[l])
                with act.If(n > 0):
                    with act.Fori(0, n) as b:
                        act.wait_ge(*since(xt_mm[l], 5 * b + 1))
                        moe_rows(xt_act[l])
                        act.wait_ge(*since(xt_mm[l], 5 * b + 2))
                        moe_x(0, xt_act[l])
                        act.wait_ge(*since(xt_mm[l], 5 * b + 3))
                        moe_silu(0, xt_act[l])
                        act.wait_ge(*since(xt_mm[l], 5 * b + 4))
                        moe_turned(0, xt_act[l])
                with act.Else():
                    act.nop()
                weights_and_squares(l, (n1_sq[1].sem, f_sq[0].sem)[l], (since(n1_mm[1], 0), (f_mm, 0))[l])

        @block.vector
        def _(dve):
            step = [0]
            count = {}
            roots = [0]
            V = nc.vector

            def done(ins, s):
                ins.then_inc(s, 1)
                count[s.name] = count.get(s.name, 0) + 1
                dve.wait_ge(s, count[s.name])

            def link(ins):
                step[0] += 1
                ins.then_inc(dve_step, 1)
                dve.wait_ge(dve_step, step[0])

            def chain():
                dve.wait_ge(dve_step, step[0])

            def free(ins):
                step[0] += 1
                ins.then_inc(dve_step, 1)

            def bc(ap, *shape):
                return ap.to_broadcast(list(shape))

            def rstd(o, i, scale=1.0, meanwhile=None):
                done(V.tensor_scalar(o, i, scale, EPS, ALU.mult, ALU.add), rms_in)
                if meanwhile:
                    meanwhile()
                roots[0] += 1
                dve.wait_ge(rms_out, roots[0])
                link(V.reciprocal(o, o))

            def norm(buf, t0, t1, summed, scaled, b):
                n = t1 - t0
                dve.wait_ge(*since(summed, 1))
                rs = trs if buf is slotB else cut(buf, 1024, n)
                rstd(rs, b[:, 0:n])
                scale(rs, t0, t1, scaled)

            def accumulate(acc, buf, n_buf, n, c, sq, out):
                dve.wait_ge(*since(sq, c + 1))
                a = cut(buf, 0, n) if c == 1 else acc
                done(V.tensor_tensor(acc, a, cut(buf, 512 * (c % n_buf), n), ALU.add), out.sem)

            def scale(rs, t0, t1, scaled):
                n = t1 - t0
                for c in range(KC):
                    done(V.tensor_tensor(hT[:, c, t0:t1], xT[:, c, t0:t1], rs, ALU.mult), scaled.sem)

            def factor(scale_mod, gain):
                return V.scalar_tensor_tensor(normA, scale_mod, 1.0, bc(gain.unsqueeze(2), P, KC, 2), ALU.add, ALU.mult)

            def rope(l, i):
                src = (kT if i < WC else qT)[:, i % WC, CTX:T]
                dve.wait_ge(*since(rope_mm[l], i + 1))
                free(V.tensor_tensor(rope_c, src, const("cos"), ALU.mult))
                link(V.tensor_tensor(rope_s, bank[4 + i % 2][:, 0:LAT], const("sin"), ALU.mult))
                done(V.tensor_tensor(src, rope_c, rope_s, ALU.add), kq_done[l].sem)

            def conv(l):
                dve.wait_ge(*since(s_small[l], 16))
                wc, b = par("w_conv", CONV_K, WC), par("b_conv", WC)
                for c in range(WC):
                    dve.wait_ge(dense_out, chunk_no(l, first_group("x") + c // 2, c % 2))
                    x = xm[:, c, :].rearrange("p (s t) -> p s t", s=2)
                    o = xc[:, c, :].rearrange("p (s t) -> p s t", s=2)
                    link(V.tensor_scalar(o, x, wc[:, 1, c:c + 1], b[:, c:c + 1], ALU.mult, ALU.add))
                    link(V.scalar_tensor_tensor(o[:, :, 1:256], x[:, :, 0:255], wc[:, 0, c:c + 1], o[:, :, 1:256], ALU.mult, ALU.add))
                    last = V.scalar_tensor_tensor(o[:, :, 0:255], x[:, :, 1:256], wc[:, 2, c:c + 1], o[:, :, 0:255], ALU.mult, ALU.add)
                    if c < WC - 1:
                        free(last)
                done(last, conv_done[l].sem)

            def gmlp(l):
                dve.wait_ge(*since(bv_sq[l], len(TILES[l])))
                a, b = TILES[l][0], NTILE
                dve.wait_ge(*since(s_early[l], 16))
                rstd(rst[:, a:b], ssq[:, a:b])
                for t in TILES[l]:
                    done(V.tensor_scalar(vG[:, t, :], vG[:, t, :], rst[:, t:t + 1], None, ALU.mult), bv_done[l].sem)
                gv, bs = par("g_v", WC), par("b_s", WC, P)
                n = len(TILES[l])
                for g in range(WC):
                    dve.wait_ge(*since(mixg_mm[l], g + 1))
                    dve.wait_ge(dense_out, chunk_no(l, first_group("u") + 1))
                    link(V.scalar_tensor_tensor(cut(slotA, 7680, n, P), cut(bank[4 + g % 2], 0, n, P), gv[:, g:g + 1],
                                                bc(bs[:, g, :].unsqueeze(1), P, n, P), ALU.mult, ALU.add))
                    o = uT[:, g, T0[l]:T]
                    done(V.tensor_tensor(o, o, attw[:, 0:NT[l]], ALU.mult), yb_done[l].sem)

            def factors(l):
                init = 0.8 - 0.6 * math.exp(-0.3 * l)
                lam = par("lam", 4, DK)
                prod = cut(slotA, 7680, 2, DK)
                link(V.tensor_tensor(prod, lam[:, 0:4:2, :], lam[:, 1:4:2, :], ALU.mult))
                done(V.tensor_reduce(lamv[:, 0:2], prod, AX, ALU.add), lam_in[l].sem)
                free(V.tensor_scalar(gvec[:, 0:1], par("g_diff"), 1.0 - init, None, ALU.mult))
                free(V.tensor_scalar(gvec[:, 1:1 + WC], par("g_ml", WC), 0.5, None, ALU.mult))
                free(V.tensor_scalar(gvec[:, 5:5 + WC], par("skip", WC), 0.5, None, ALU.mult))
                dve.wait_ge(*since(lam_ex[l], 1))
                link(V.scalar_tensor_tensor(lamv[:, 0:1], lamv[:, 2:3], init, lamv[:, 3:4], ALU.add, ALU.subtract))

            def att_weights(l, u):
                h, t = UNITS[l][u]
                keys = CTX if t < 2 else T
                dve.wait_ge(*since(at_s[l], u + 1))
                link(V.tensor_reduce(nmax, cut(psum, 4 * 512, 2, 512)[:, :, 0:keys], AX, ALU.max))
                done(V.tensor_scalar(nbias, nmax, -SCALE, None, ALU.mult), at_nb[l].sem)
                dve.wait_ge(*since(at_exp[l], 2 * u + 2))
                link(V.reciprocal(prec, psum_))
                link(V.tensor_tensor(prec[:, 1:2], prec[:, 1:2], lamv[:, 0:1], ALU.mult))
                link(V.tensor_scalar(probs[:, 1, 0:keys], probs[:, 1, 0:keys], prec[:, 1:2], None, ALU.mult))
                if u >= 1:
                    dve.wait_ge(*since(at_T[l], u))
                done(V.scalar_tensor_tensor(attw[:, 0:keys], probs[:, 0, 0:keys], prec[:, 0:1], probs[:, 1, 0:keys],
                                       ALU.mult, ALU.subtract), at_a[l].sem)

            def att_norm(l, u):
                h, t = UNITS[l][u]
                dve.wait_ge(*since(at_sq[l], u + 1))
                done(V.tensor_copy(oraw[:, h, :], bank[7][:, 0:P]), at_on[l].sem)
                if h == H - 1:
                    dve.wait_ge(*since(at_on[l], u + 1))
                    rstd(orms, oss)
                    if u >= H:
                        dve.wait_ge(*since(at_oT[l], u // H))
                    done(V.tensor_tensor(oN, oraw, bc(orms.unsqueeze(2), P, H, P), ALU.mult), at_nd[l].sem)

            def ml_features(l, seg):
                for i in range(NFA, NF):
                    dve.wait_ge(*since(ml_ff[l], seg * NF + i + 1))
                    b = cut(bank[4 + i % 4], 0, WC, P)
                    t = (i - NFA) // 2
                    if i % 2 == 0:
                        done(V.tensor_scalar(mkt[:, t, :, :], b, MSCALE, None, ALU.mult), ml_fe[l].sem)
                    else:
                        done(V.tensor_copy(mvt[:, t, :, 0:DV], b), ml_fe[l].sem)

            def ml_gates(l, seg):
                dve.wait_ge(*since(ml_gm[l], seg + 1))
                link(V.tensor_tensor(mgate, cut(bank[2], 0, 2, 16), bc(par("b_if", 16).unsqueeze(1), P, 2, 16), ALU.add))
                g4 = mgate.rearrange("p t (d i h) -> p (t d) i h", d=2, i=2)
                f = g4[:, :, 1, :]
                tm = mtmp.rearrange("p t d h -> p (t d) h")
                done(V.scalar_tensor_tensor(tm, f, -1.0, f, ALU.mult, ALU.max), ml_ga[l].sem)
                dve.wait_ge(*since(ml_gl[l], seg + 1))
                done(V.scalar_tensor_tensor(mlf.rearrange("p t d h -> p (t d) h"), f, 0.0, tm, ALU.min, ALU.subtract), ml_lf[l].sem)
                dve.wait_ge(*since(ml_cs[l], seg + 1))
                free(V.tensor_copy(mg, cut(bank[2], 48, 2, 2, H)))
                link(V.tensor_copy(mb, cut(bank[2], 32, 2, 2, H)))
                g5 = mgate.rearrange("p t (d i h) -> p t d i h", d=2, i=2)
                for d in range(2):
                    last = V.tensor_tensor(mr[:, d, :, :], g5[:, :, d, 0, :], mb[:, d, :, :], ALU.subtract)
                    if d == 0:
                        free(last)
                done(last, ml_r[l].sem)
                for i in range(2):
                    free(V.memset(cmax[i][:, 0, 0:PAD], -BIG))
                    free(V.memset(cmax[i][:, 1, P:P + PAD], -BIG))
                dve.wait_ge(*since(ml_rT[l], seg + 1))
                for d in range(2):
                    free(V.tensor_copy(cm_at(0, d), bank[2][0:8, P * (d + 1):P * (d + 2)]))
                chain()
                for i in range(7):
                    for d in range(2):
                        last = V.tensor_tensor(cm_at((i + 1) % 2, d), cm_at(i % 2, d), cm_at(i % 2, d, 2 ** i), ALU.max)
                        if i < 6 or d == 0:
                            free(last)
                    if i < 6:
                        chain()
                done(last, ml_cm[l].sem)
                dve.wait_ge(*since(ml_mt[l], seg + 1))
                link(V.tensor_copy(mMt, cut(bank[2], 64, 2, 2, H)))

            def ml_exponents(l, seg, w):
                d, t = MUN[w]
                n = 4 * seg + w
                m0 = mst[:, d, :]
                dve.wait_ge(*since(ml_bc[l], n + 1))
                link(V.tensor_tensor(mend, m0, cut(bank[4], 0, H, P)[:, :, P - 1 if d == 0 else 0], ALU.max))
                if n >= 1:
                    dve.wait_ge(*since(ml_ex[l], n))
                free(V.tensor_tensor(mex[:, 0, :], m0, mend, ALU.subtract))
                last = V.tensor_tensor(mex[:, 1, :], mr[:, d, t, :], mend, ALU.subtract)
                if with_h(l, seg):
                    free(last)
                    link(V.tensor_tensor(mmax, mMt[:, d, t, :], m0, ALU.max))
                    free(V.tensor_tensor(mex[:, 2, :], m0, mmax, ALU.subtract))
                    last = V.scalar_tensor_tensor(mex[:, 3, :], mb[:, d, t, :], -1.0, mmax, ALU.mult, ALU.subtract)
                done(last, ml_ei[l].sem)
                if with_h(l, seg):
                    for h in range(H):
                        last = V.scalar_tensor_tensor(sg[w % 2][:, h, :], bank[4][:, P * h:P * h + P], m0[:, h:h + 1],
                                                      const(("mask_f", "mask_b")[d]), ALU.max, ALU.add)
                        if h < H - 1:
                            free(last)
                    done(last, ml_nd[l].sem)
                    dve.wait_ge(*since(ml_nd[l], 4 * (seg - l) + w + 1))
                free(V.tensor_tensor(m0, mg[:, t, d, :], mend, ALU.add))

            def ml_weights(l, seg, w):
                d, t = MUN[w]
                n, nh = 4 * seg + w, 4 * (seg - l) + w
                s = sg[w % 2]
                if with_h(l, seg):
                    dve.wait_ge(*since(ml_d[l], nh + 1))
                    dve.wait_ge(*since(ml_qk[l], nh + 1))
                    done(V.scalar_tensor_tensor(s, cut(bank[5], 0, H, P), MSCALE, s, ALU.mult, ALU.mult), ml_sg[l].sem)
                dve.wait_ge(*since(ml_ex[l], n + 1))
                done(V.tensor_tensor(vw[w % 2], mvt[:, t, :, :], bc(mee[w % 2][:, 1, :].unsqueeze(2), P, H, DV1), ALU.mult), ml_vw[l].sem)

            def ml_unit(l, seg, w):
                d, t = MUN[w]
                n, nh = 4 * seg + w, 4 * (seg - l) + w
                e = mee[w % 2]
                if with_h(l, seg):
                    dve.wait_ge(*since(ml_int[l], nh + 1))
                    free(V.tensor_tensor(num[:, 0:3, :], inter[:, 0:3, :], cut(bank[6], 0, 3, DV1), ALU.add))
                    link(V.tensor_tensor(num[:, 3, :], inter[:, 3, :], num_ps[3], ALU.add))
                    den = num[:, :, DV]
                    link(V.scalar_tensor_tensor(mden, den, -1.0, den, ALU.mult, ALU.max))
                    link(V.tensor_tensor(mden, mden, e[:, 3, :], ALU.max))
                    link(V.reciprocal(mden2, mden))
                    r = bc(mden2.unsqueeze(2), P, H, P)
                    if w < 2:
                        done(V.tensor_tensor(hsum[:, t, :, :], num[:, :, 0:DV], r, ALU.mult), ml_hr[l].sem)
                    else:
                        link(V.tensor_tensor(num[:, :, 0:DV], num[:, :, 0:DV], r, ALU.mult))
                        done(V.tensor_tensor(hsum[:, t, :, :], hsum[:, t, :, :], num[:, :, 0:DV], ALU.add), ml_hr[l].sem)
                else:
                    dve.wait_ge(*since(ml_upd[l], n + 1))
                for h in range(H):
                    c = state[:, d, h, :]
                    last = V.scalar_tensor_tensor(c, c, e[:, 0, h:h + 1], upd_ps[h], ALU.mult, ALU.add)
                    if h < H - 1:
                        free(last)
                done(last, ml_st[l].sem)

            def ml_output(l, seg):
                i = seg - l
                dve.wait_ge(*since(ml_hr[l], 4 * (i + 1)))
                for t in range(2):
                    link(V.tensor_tensor(hsq, hsum[:, t, :, :], hsum[:, t, :, :], ALU.mult))
                    link(V.tensor_reduce(hss[:, t, :], hsq, AX, ALU.add))

                def skip():
                    for h in range(H):
                        free(V.tensor_scalar(xs[:, h, :], xc[:, h, 256 * seg:256 * seg + 256], gvec[:, 5 + h:6 + h], None, ALU.mult))
                rstd(hss, hss, 1.0 / DV, skip)
                for t in range(2):
                    last = V.tensor_tensor(hn[:, t, :, :], hsum[:, t, :, :], bc(hss[:, t, :].unsqueeze(2), P, H, P), ALU.mult)
                    if t == 0:
                        free(last)
                done(last, ml_hn[l].sem)

            def ml_finish(l, seg):
                i = seg - l
                sl = slice(256 * seg, 256 * seg + 256)
                dve.wait_ge(*since(ml_hT[l], i + 1))
                for h in range(H):
                    src = cut(psum, 2 * 512, 2, 512)[:, :, P * h:P * h + P]
                    free(V.scalar_tensor_tensor(yt[:, h, :].rearrange("p (t e) -> p t e", t=2), src, gvec[:, 1 + h:2 + h],
                                                xs[:, h, :].rearrange("p (t e) -> p t e", t=2), ALU.mult, ALU.add))
                chain()
                dve.wait_ge(dense_out, chunk_no(l, first_group("z") + 1))
                done(V.scalar_tensor_tensor(zT[:, :, sl], zT[:, :, sl], 1.0, yt, ALU.add, ALU.mult), ml_y[l].sem)

            def first_of(o, idx, x, big, iota, n, m):
                tmp = ro["cand"][0][:, 0:n * m].rearrange("p (n m) -> p n m", n=n)
                link(V.tensor_tensor(o, x, bc(big.unsqueeze(2), P, n, m), ALU.is_equal))
                link(V.scalar_tensor_tensor(tmp, o, -1024.0, bc(iota.unsqueeze(1), P, n, m), ALU.mult, ALU.add))
                link(V.tensor_reduce(idx, tmp, AX, ALU.min))
                link(V.tensor_scalar(idx, idx, 1024.0, None, ALU.add))
                link(V.tensor_tensor(o, bc(iota.unsqueeze(1), P, n, m), bc(idx.unsqueeze(2), P, n, m), ALU.is_equal))

            def route(l):
                n = len(TILES[l])
                br = par("b_route", GROUPS + E)
                lg, le, oh12, m = (ro[k][l] for k in ("lg", "le", "oh", "m"))
                oh1, oh2 = oh12[:, 0, :, :], oh12[:, 1, :, :]
                iota = const("iota")
                logits = cut(bank[1], 0, n, GROUPS + E)
                dve.wait_ge(*since(ro_mm[l], 1))
                free(V.tensor_tensor(lg, logits[:, :, 0:GROUPS], bc(br[:, 0:GROUPS].unsqueeze(1), P, n, GROUPS), ALU.add))
                done(V.tensor_tensor(le, logits[:, :, GROUPS:], bc(br[:, GROUPS:].unsqueeze(1), P, n, E), ALU.add), ro_in[l].sem)
                dve.wait_ge(*since(ro_in[l], 1))
                gm, gi, ge = ro["gm"][l], ro["gi"][l], ro["ge"][l]
                link(V.tensor_reduce(gm, lg, AX, ALU.max))
                done(V.tensor_tensor(ge, lg, bc(gm.unsqueeze(2), P, n, GROUPS), ALU.subtract), ro_ei[l].sem)
                oh = ro["goh"][l]
                first_of(oh, gi, lg, gm, iota[:, 0:GROUPS], n, GROUPS)
                link(V.tensor_scalar(oh, oh, 1.0, BIG, ALU.subtract, ALU.mult))
                v = le.rearrange("p n (g e) -> p (n g) e", g=GROUPS)
                link(V.tensor_tensor(v, v, bc(oh.rearrange("p n g -> p (n g)").unsqueeze(2), P, n * GROUPS, PER), ALU.add))
                m1, m2, idx, e2 = ro["m1"][l], ro["m2"][l], ro["idx"][l], ro["e2"][l]
                link(V.tensor_reduce(m1, le, AX, ALU.max))
                first_of(oh1, idx[:, 0, :], le, m1, iota[:, 0:E], n, E)
                link(V.scalar_tensor_tensor(le, oh1, -4.0 * BIG, le, ALU.mult, ALU.add))
                link(V.tensor_reduce(m2, le, AX, ALU.max))
                first_of(oh2, idx[:, 1, :], le, m2, iota[:, 0:E], n, E)
                done(V.tensor_tensor(m, oh1, oh2, ALU.add), ro_m[l].sem)
                done(V.tensor_tensor(e2, m2, m1, ALU.subtract), ro_ei[l].sem)
                dve.wait_ge(*since(ro_cnt[l], 1))
                cmp_, cnt = ro["cmp"][l], ro["cnt"][l]
                link(V.tensor_copy(cnt, bank[1][0:E, 256:257]))
                link(V.tensor_scalar(cmp_, const("thr", E), cnt, None, ALU.is_lt))
                done(V.tensor_reduce(ro["obl"][l], cmp_, AX, ALU.add), ro_obl[l].sem)
                rank, ob, fl, jj, bb = (ro[k][l] for k in ("rank", "ob", "fl", "jj", "bb"))
                tmp = ro["cand2"][l]
                for k in range(2):
                    last = V.tensor_tensor(tmp[:, k, :, :], oh12[:, k, :, :], cut(bank[1], 0, n, E), ALU.mult)
                    if k == 0:
                        free(last)
                link(last)
                link(V.tensor_reduce(rank, tmp, AX, ALU.add))
                dve.wait_ge(*since(ro_ob[l], 1))
                oe = ro["oe"][l]
                link(V.tensor_copy(oe, cut(bank[2], 0, 2, E)))
                for k in range(2):
                    last = V.tensor_tensor(tmp[:, k, :, :], oh12[:, k, :, :], bc(oe[:, 0, :].unsqueeze(1), P, n, E), ALU.mult)
                    if k == 0:
                        free(last)
                link(last)
                link(V.tensor_reduce(ob, tmp, AX, ALU.add))
                fc = ro["fc"][l]
                f1 = [a.rearrange("p k n -> p (k n)") for a in (rank, ob, fl, jj, bb, idx)]
                rank, ob, fl, jj, bb, ix = f1
                link(V.tensor_tensor(fc, bc(rank.unsqueeze(2), P, 2 * n, STEPS), bc(const("thr").unsqueeze(1), P, 2 * n, STEPS), ALU.is_ge))
                link(V.tensor_reduce(fl, fc, AX, ALU.add))
                link(V.scalar_tensor_tensor(jj, fl, -float(BLK), rank, ALU.mult, ALU.add))
                link(V.tensor_tensor(ob, ob, fl, ALU.add))
                link(V.scalar_tensor_tensor(ob, ob, E - 1.0, ix, ALU.add, ALU.subtract))
                link(V.scalar_tensor_tensor(bb, fl, 1.0, ob, ALU.is_ge, ALU.mult))
                link(V.tensor_tensor(bb, bb, ix, ALU.add))
                BT, places = ro["BT"][l], ro["places"][l]
                nb = NBLK[l]
                link(V.tensor_scalar(jj, jj, 1.0, None, ALU.add))
                link(V.tensor_tensor(BT, bc(iota[:, 0:nb].unsqueeze(1), P, 2 * n, nb), bc(bb.unsqueeze(2), P, 2 * n, nb), ALU.is_equal))
                link(V.tensor_tensor(BT, BT, bc(jj.unsqueeze(2), P, 2 * n, nb), ALU.mult))
                link(V.scalar_tensor_tensor(places, BT[:, 0:n, :], -1.0, BT[:, n:2 * n, :], ALU.add, ALU.add))

            def route_rest(l):
                n = len(TILES[l])
                ge, e2, bb, jj, oe = (ro[k][l] for k in ("ge", "e2", "bb", "jj", "oe"))
                bb, jj = (a.rearrange("p k n -> p (k n)") for a in (bb, jj))
                iota = const("iota")
                dve.wait_ge(*since(ro_ex[l], 1))
                pg = ro["pg"][l]
                link(V.tensor_reduce(pg, ge, AX, ALU.add))
                link(V.reciprocal(pg, pg))
                dve.wait_ge(*since(ro_ex[l], 2))
                t1 = ro["t1"][l]
                wt = ro["wt"][l]
                link(V.tensor_scalar(t1, e2, 1.0, None, ALU.add))
                link(V.reciprocal(t1, t1))
                link(V.tensor_tensor(wt[:, 0, :], pg, t1, ALU.mult))
                link(V.tensor_tensor(wt[:, 1, :], wt[:, 0, :], e2, ALU.mult))
                link(V.tensor_scalar(jj, jj, 1.0, None, ALU.subtract))
                free(V.scalar_tensor_tensor(slotI[:, 0:2 * n], bb, float(BLK), jj, ALU.mult, ALU.add))
                xb = XBLK[l]
                own, owc = ro["own"][l], ro["owc"][l]
                link(V.tensor_tensor(owc, bc(oe[0:1, 1, :].unsqueeze(1), 1, xb, E), bc(iota[0:1, 0:xb].unsqueeze(2), 1, xb, E), ALU.is_le))
                link(V.tensor_reduce(own[:, 0:xb], owc, AX, ALU.add))
                free(V.tensor_scalar(ownI[:, 0:xb], own[:, 0:xb], E - 1.0, None, ALU.min))
                done(V.tensor_copy(ownI[:, xb:xb + 1], oe[0:1, 1, E - 1:E]), ro_done[l].sem)

            def moe_onehot(l, s, b, done_):
                n = len(TILES[l])
                V.tensor_tensor(onehot[s][:, 0:n, :], bc(const("iota").unsqueeze(1), P, n, BLK),
                                bc(ro["places"][l][:, :, bass.ds(b, 1)], P, n, BLK), ALU.is_equal).then_inc(done_.sem, 1)

            def moe_act(s, o):
                return V.tensor_tensor(act_[s][64:128, :], gs[s][64:128, :], bank[1][64:128, :], ALU.mult).then_inc(o.sem, 1)

            def factors1(l):
                head = modT[:, l, 0:2 * KC, :]
                link(V.tensor_tensor(head, head, bc(par("b_mod", NMOD * KC)[:, 0:2 * KC].unsqueeze(2), P, 2 * KC, 2), ALU.add))
                done(factor(modT[:, l, KC:2 * KC, :], par("g1", KC)), n1_f[l].sem)

            dve.wait_ge(s_const, 16)
            for l in range(L):
                if l == 0:
                    dve.wait_ge(s_x, 16)
                    for c in range(1, KC):
                        accumulate(nbuf1[:, 0:T], nbuf1, KC, T, c, n1_sq[l], n1_ac[l])
                    norm(nbuf1, 0, T, n1_mm[l], n1_nt[l], bank[7])
                    dve.wait_ge(s_head, 16)
                    dve.wait_ge(mod_out, MOD_FIRST)
                    factors1(l)
                else:
                    scale(trs, 0, T, n1_nt[l])
                bm = par("b_mod", NMOD * KC)
                for i in range(WC):
                    rope(l, i)
                conv(l)
                for i in range(WC, 2 * WC):
                    rope(l, i)
                gmlp(l)
                factors(l)
                for u in range(len(UNITS[l])):
                    att_weights(l, u)
                    att_norm(l, u)
                for seg in range(2):
                    ml_features(l, seg)
                    if seg == 1 and with_h(l, 0):
                        ml_finish(l, 0)
                    if seg == 0:
                        free(V.memset(state, 0.0))
                        free(V.memset(mvt[:, :, :, DV:DV1], 1.0))
                        free(V.memset(mst, 0.0))
                    ml_gates(l, seg)
                    for w in range(5):
                        if w < 4:
                            ml_exponents(l, seg, w)
                            ml_weights(l, seg, w)
                        if w > 0:
                            ml_unit(l, seg, w - 1)
                    if with_h(l, seg):
                        ml_output(l, seg)
                ml_finish(l, 1)
                dve.wait_ge(mod_out, MODG * (l + 1))
                tail = modT[:, l, 2 * KC:, :]
                link(V.tensor_tensor(tail, tail, bc(bm[:, 2 * KC:].unsqueeze(2), P, 4 * KC, 2), ALU.add))
                link(V.tensor_scalar(gate2, modT[:, l, 2 * KC:3 * KC, :], 0.5, None, ALU.mult))
                dve.wait_ge(dense_out, chunk_no(l, len(WIN) - 1))
                dve.sem_inc(br_done[l].sem, 2)
                t0, n = T0[l], NT[l]
                with dve.Fori(0, BRG // 2) as j:
                    for s in range(2):
                        i = 2 * j + s
                        dve.wait_ge(*since(br_mm[l], i + 1))
                        for b in range(3):
                            g = gates[:, bass.ds(i + KC * b, 1), t0:T].rearrange("p a t -> p (a t)")
                            last = V.scalar_tensor_tensor(mrg[b][:, 0:n], g, 1.0, bank[BRB[s][b]][:, 0:n], ALU.add, ALU.mult)
                        last.then_inc(br_step[l].sem, 1)
                        dve.wait_ge(*since(br_step[l], 4 * j + (2 * s + 1)))
                        V.tensor_tensor(mrg[0][:, 0:n], mrg[0][:, 0:n], mrg[1][:, 0:n], ALU.add).then_inc(br_step[l].sem, 1)
                        dve.wait_ge(*since(br_step[l], 4 * j + (2 * s + 2)))
                        o = hT[:, bass.ds(i, 1), t0:T].rearrange("p a t -> p (a t)")
                        V.tensor_tensor(o, mrg[0][:, 0:n], mrg[2][:, 0:n], ALU.add).then_inc(br_done[l].sem, 1)
                        dve.wait_ge(*since(br_done[l], 2 * j + (s + 3)))
                for c in range(KC):
                    dve.wait_ge(*since(wo_mm[l], c + 1))
                    for w in range(1 if l else 0, 2):
                        x = xT[:, c, 256 * w:256 * w + 256]
                        y = bank[4 + c % 4][:, 256 * w - t0:256 * w - t0 + 256]
                        last = V.scalar_tensor_tensor(x, y, gate2[:, c, w:w + 1], x, ALU.mult, ALU.add)
                    done(last, res1[l].sem)
                    if c >= 2:
                        accumulate(nbuf2[:, 1536:1536 + n], nbuf2, 2, n, c - 1, n2_sq[l], n2_ac[l])
                accumulate(nbuf2[:, 1536:1536 + n], nbuf2, 2, n, KC - 1, n2_sq[l], n2_ac[l])
                dve.wait_ge(*since(res1[l], KC))
                link(factor(modT[:, l, 4 * KC:5 * KC, :], par("g2", KC)))
                norm(nbuf2, t0, T, n2_mm[l], n2_nt[l], bank[3])
                route(l)
                for s in range(2):
                    moe_onehot(l, s, s, mo_oh[l])
                route_rest(l)

                def pair(j, last):
                    for s in range(2):
                        e = 2 * j + s
                        dve.wait_ge(*since(mo_s[l], e + 1))
                        moe_act(s, mo_a[l])
                        if not last:
                            moe_onehot(l, s, e + 2, mo_oh[l])
                        dve.wait_ge(*since(mo_d[l], e + 1))
                        dve.wait_ge(*since(mo_st[l][s], 32 * j + 16))
                        V.tensor_copy(yS[s], bank[3 + s]).then_inc(mo_y[l].sem, 1)
                with dve.Fori(0, E // 2 - 1) as j:
                    pair(j, False)
                pair(E // 2 - 1, True)
                dve.wait_ge(*since(mo_st[l][0], 16 + 16 * E))
                nx = dve.value_load(ownI[0:1, XBLK[l]:XBLK[l] + 1], min_val=0, max_val=XBLK[l])
                with dve.If(nx > 0):
                    with dve.Fori(0, nx) as b:
                        moe_onehot(l, 0, b + E, xt_oh[l])
                        dve.wait_ge(*since(xt_act[l], 4 * b + 3))
                        moe_act(0, xt_a[l])
                        dve.wait_ge(*since(xt_mm[l], 5 * b + 5))
                        dve.wait_ge(*since(xt_st[l], 32 * b))
                        V.tensor_copy(yS[0], bank[3]).then_inc(xt_y[l].sem, 1)
                with dve.Else():
                    dve.nop()
                nt = len(TILES[l])
                wt = ro["wt"][l]

                def residual2(i):
                    dve.wait_ge(*since(cb_T[l], i + 1))
                    t = TILES[l][i]
                    w = 0 if t < 2 else 1
                    for c in range(KC):
                        x = xT[:, c, P * t:P * t + P]
                        o = 512 * (4 + 2 * (i % 2)) + P * c
                        last = V.scalar_tensor_tensor(x, psum[:, o:o + P], modT[:, l, 5 * KC + c, w:w + 1], x, ALU.mult, ALU.add)
                        if c < KC - 1:
                            free(last)
                    done(last, cb_r[l].sem)

                def tile_rstd(a, b):
                    summed = (since(n1_mm[1], b), (f_mm, b))[l]
                    dve.wait_ge(*summed)
                    rstd(cut(trs, P * a, b - a, P), cut(psum, 0, NTILE, 512)[:, a:b, 0:P])
                if l == 0:
                    dve.wait_ge(*since(s_small[1], 16))
                    dve.wait_ge(mod_out, MODG + MOD_FIRST)
                    factors1(1)
                for i in range(nt):
                    dve.wait_ge(*since(cb_s[l], i + 1))
                    done(V.scalar_tensor_tensor(fw[i % 2], yg[i][:, 1, :], wt[:, 1, i:i + 1], fw[i % 2], ALU.mult, ALU.add), cb_w[l].sem)
                    if i >= 1:
                        residual2(i - 1)
                residual2(nt - 1)
                tile_rstd(0, nt - 1)
                tile_rstd(nt - 1, nt)
            gf = par("g_fin", KC)
            for c in range(KC):
                done(V.scalar_tensor_tensor(fin[:, c * LAT:(c + 1) * LAT], xT[:, c, CTX:T], gf[:, c:c + 1], trs[:, 0:LAT], ALU.mult, ALU.mult), f_out)

        @block.gpsimd
        def _(pool):
            nc.gpsimd.memset(csil[:, :, 2:32], 0.0).then_inc(s_zero, 1)
            n = XBLK[0] * BLK * D // P
            spare = y_flat[E * BLK:, :].rearrange("r n -> (r n)").rearrange("(p n) -> p n", p=P)
            pool.wait_ge(s_const, 16)
            pool.wait_ge(mod_mm, MOD_FIRST)
            for i in range(SPARE):
                w = n // SPARE
                pool.dma_start(spare[:, w * i:w * i + w], consts[:, 0:w]).then_inc(s_spare, 16)

            def gather(o, src, idx, s_):
                nc.gpsimd.indirect_dma_start(o, None, src[:, :], bass.IndirectOffsetOnAxis(ap=idx, axis=0)).then_inc(s_, 16)

            for l in range(L):
                n = len(TILES[l])
                pool.wait_ge(s_spare, 16 * SPARE)
                pool.wait_ge(*since(ro_done[l], 1))
                nx = pool.value_load(ownI[0:1, XBLK[l]:XBLK[l] + 1], min_val=0, max_val=XBLK[l])
                with pool.If(nx > 0):
                    with pool.Fori(0, nx) as b:
                        pool.wait_ge(*since(xt_y[l], b + 1))
                        store(pool, b + E, yS[0], xt_st[l])
                        pool.wait_ge(*since(xt_st[l], 32 * b + 32))
                with pool.Else():
                    pool.nop()
                for s in range(2):
                    pool.wait_ge(*since(mo_st[l][s], 16 + 16 * E))
                for i, t in enumerate(TILES[l]):
                    for k in range(2):
                        q = k * n + i
                        gather(yg[i][:, k, :], y_flat, slotI[:, q:q + 1], cb_g[t])



def kernel(**inputs):
    import concourse.bacc as bacc
    from concourse.bass_utils import run_bass_kernel_spmd

    def a(name):
        return np.ascontiguousarray(inputs[name])

    def chan(v, n):
        return v.reshape(-1, n, P).transpose(2, 0, 1).reshape(P, -1)

    def rows(v):
        return np.broadcast_to(v.reshape(1, -1), (P, v.size))

    def groups(w, cols, k=KC):
        l, _, n = w.shape
        return np.ascontiguousarray(w.reshape(l, k, P, n // cols, cols).transpose(0, 3, 2, 1, 4)).reshape(-1, P, k * cols)

    x = np.concatenate([a("ctx")[0], a("x")[0]], 0)
    xt = np.ascontiguousarray(x.reshape(T, KC, P).transpose(2, 1, 0)).reshape(P, KC * T)
    small = np.zeros((L, P, SMALL_W), np.float32)
    for l in range(L):
        parts = {
            "b_mod": chan(a("b_mod")[l], NMOD * KC), "g1": chan(a("g_norm1")[l], KC), "g2": chan(a("g_norm2")[l], KC),
            "g_diff": a("g_diff_subln")[l][:, None], "g_v": chan(a("g_gmlp_v")[l], WC),
            "w_conv": chan(a("w_conv_m")[l], WC), "b_conv": chan(a("b_conv_m")[l], WC),
            "g_ml": chan(a("g_mlstm_norm")[l], WC), "skip": chan(a("skip_m")[l], WC), "g_fin": chan(a("g_final"), KC),
            "c": np.stack([a("c_ctx"), a("c")[0]]).reshape(2, KC, P).transpose(2, 1, 0).reshape(P, -1),
            "w_if": a("w_if_m")[l].reshape(3 * WC, P, 16).transpose(1, 0, 2).reshape(P, -1),
            "w_route": np.concatenate([a("w_route_g")[l], a("w_route_e")[l]], 1)
                .reshape(KC, P, GROUPS + E).transpose(1, 0, 2).reshape(P, -1),
            "b_if": rows(a("b_if_m")[l]), "b_route": rows(np.concatenate([a("b_route_g")[l], a("b_route_e")[l]])),
            "w_sT": a("w_gmlp_s")[l].transpose(2, 0, 1).reshape(P, -1),
            "w_qkv": a("w_qkv_m")[l].transpose(2, 0, 1, 3).reshape(P, -1),
        }
        for k, v in parts.items():
            small[l, :, SMALL[k][0]:SMALL[k][1]] = v
    early = np.stack([np.concatenate([rows(a("b_gmlp_s")[l]), rows(a("diff_lambda")[l])], 1) for l in range(L)])
    w = a("w_in").reshape(L, KC, P, -1)
    win = np.stack([w[..., c:c + COLS] for _, c, _ in WIN], 1).transpose(0, 1, 3, 2, 4)
    arrays = {
        "xt": xt, "consts": constants(), "small": small, "early": early,
        "wmod": groups(a("w_mod"), COLS), "win": np.ascontiguousarray(win).reshape(L * len(WIN), P, RW),
        "wbr": groups(a("w_branch").reshape(L, 3 * W, D), P, 3 * WC), "wout": groups(a("w_out"), COLS),
        "w_gate": a("w_e_gate").reshape(L * E, D, FE), "w_up": a("w_e_up").reshape(L * E, D, FE),
        "w_down": a("w_e_down").reshape(L * E, FE, D),
    }
    nc = bacc.Bacc("TRN2", target_bir_lowering=False, num_devices=1)
    t = {k: nc.dram_tensor(f"{k}_dram", v.shape, F32, kind="ExternalInput").ap() for k, v in arrays.items()}
    out = nc.dram_tensor("out", (P, KC * LAT), F32, kind="ExternalOutput").ap()
    y = nc.dram_tensor("y_rows", (NBLK[0] * BLK, D), F32, kind="Internal").ap()
    build(nc, *(t[k] for k in ("xt", "consts", "small", "early", "wmod", "win", "wbr", "wout", "w_gate", "w_up", "w_down")), out, y)
    r = run_bass_kernel_spmd(nc, [{f"{k}_dram": v for k, v in arrays.items()}], core_ids=[0])
    got = r.results[0]["out"]
    return got.reshape(P, KC, LAT).transpose(2, 1, 0).reshape(1, LAT, D)
```
